# Optimizing a Trainium2 kernel written in Bass

```python
import jax, jax.numpy as jnp
from jax import lax
import numpy as np
import math

D_MODEL = 1024
BATCH = 1
SEQ = 512
DEPTH = 2

GRID_W = 64
CTX_LEN = 256
FOUR_GROUPS = 4
FOUR_GC = D_MODEL // 8
FOUR_WIDTH = FOUR_GROUPS * FOUR_GC
NA_HEADS = 8
NA_HEAD_DIM = D_MODEL // 16
NA_WIDTH = NA_HEADS * NA_HEAD_DIM
NA_WIN_ROWS = 8
NA_WIN_COLS = 16
POOL_SIZES = (2, 4, 8, 16)
POOL_GC = D_MODEL // len(POOL_SIZES)
MLP_HIDDEN = 4 * D_MODEL
N_MOD = 6
RMS_EPS = 1e-6
N_EVEN = (DEPTH + 1) // 2
N_ODD = DEPTH // 2


def rms_norm(x, g):
    xf = x.astype(jnp.float32)
    y = xf * lax.rsqrt(jnp.mean(xf * xf, axis=-1, keepdims=True) + RMS_EPS)
    return (y * g.astype(jnp.float32)).astype(x.dtype)

def modulate(xn, shift, scale):
    return xn * (1.0 + scale) + shift

def sq_relu_mlp(u, w1, w2):
    a = jnp.maximum(u @ w1, 0.0)
    return (a * a) @ w2

def fourier_mix(f, w_four):
    B, N, _ = f.shape
    fg = f.reshape(B, N, FOUR_GROUPS, FOUR_GC).transpose(0, 2, 1, 3)
    mixed = jnp.fft.fft2(fg.astype(jnp.float32), norm="ortho").real.astype(f.dtype)
    out = jnp.einsum('bgnc,gcd->bngd', mixed, w_four)
    return out.reshape(B, N, FOUR_WIDTH)

def neighbourhood_attention(q, k, v, k_ctx, v_ctx, rpb):
    B, N, H, dh = q.shape
    rows = N // GRID_W
    wr = min(NA_WIN_ROWS, rows)

    def to_grid(a):
        return a.reshape(B, rows, GRID_W, H, dh).transpose(0, 3, 1, 2, 4)

    qg, kg, vg = to_grid(q), to_grid(k), to_grid(v)
    r = jnp.arange(rows)
    row_start = jnp.clip(r - wr // 2, 0, rows - wr)
    row_idx = row_start[:, None] + jnp.arange(wr)[None, :]
    kb = kg[:, :, row_idx]
    vb = vg[:, :, row_idx]
    cidx = jnp.arange(GRID_W)
    col_start = jnp.clip(cidx - NA_WIN_COLS // 2, 0, GRID_W - NA_WIN_COLS)
    col_mask = (cidx[None, :] >= col_start[:, None]) & (cidx[None, :] < col_start[:, None] + NA_WIN_COLS)
    dr = row_idx - r[:, None] + (NA_WIN_ROWS - 1)
    dc = jnp.clip(cidx[None, :] - cidx[:, None] + (NA_WIN_COLS - 1), 0, 2 * NA_WIN_COLS - 2)
    bias = rpb[:, dr[:, None, :, None], dc[None, :, None, :]]
    scale = dh ** -0.5
    s_win = jnp.einsum('bhrqd,bhrjkd->bhrqjk', qg, kb).astype(jnp.float32) * scale + bias.astype(jnp.float32)
    s_win = jnp.where(col_mask[:, None, :], s_win, -jnp.inf)
    s_win = s_win.reshape(B, H, rows, GRID_W, wr * GRID_W)
    s_ctx = jnp.einsum('bhrqd,blhd->bhrql', qg, k_ctx).astype(jnp.float32) * scale
    p = jax.nn.softmax(jnp.concatenate([s_win, s_ctx], axis=-1), axis=-1)
    p_win = p[..., :wr * GRID_W].reshape(B, H, rows, GRID_W, wr, GRID_W).astype(v.dtype)
    p_ctx = p[..., wr * GRID_W:].astype(v.dtype)
    o = jnp.einsum('bhrqjk,bhrjkd->bhrqd', p_win, vb) + jnp.einsum('bhrql,blhd->bhrqd', p_ctx, v_ctx)
    return o.transpose(0, 2, 3, 1, 4).reshape(B, N, H * dh)

def context_attention(qc, kc, vc):
    B, L, H, dh = qc.shape
    s = jnp.einsum('blhd,bmhd->bhlm', qc, kc).astype(jnp.float32) * (dh ** -0.5)
    p = jax.nn.softmax(s, axis=-1).astype(vc.dtype)
    return jnp.einsum('bhlm,bmhd->blhd', p, vc).reshape(B, L, H * dh)

def split_heads(a):
    return a.reshape(a.shape[0], a.shape[1], NA_HEADS, NA_HEAD_DIM)

def even_mixer(u, uc, w_in, w_four, q_g, k_g, rpb, w_out, update_ctx):
    p = u @ w_in
    f, q, k, v = jnp.split(p, [FOUR_WIDTH, FOUR_WIDTH + NA_WIDTH, FOUR_WIDTH + 2 * NA_WIDTH], axis=-1)
    q = rms_norm(split_heads(q), q_g)
    k = rms_norm(split_heads(k), k_g)
    v = split_heads(v)
    kvc = uc @ w_in[:, FOUR_WIDTH + NA_WIDTH:]
    kc, vc = jnp.split(kvc, [NA_WIDTH], axis=-1)
    kc = rms_norm(split_heads(kc), k_g)
    vc = split_heads(vc)
    o_four = fourier_mix(f, w_four)
    o_na = neighbourhood_attention(q, k, v, kc, vc, rpb)
    y = jnp.concatenate([o_four, o_na], axis=-1) @ w_out
    if not update_ctx:
        return y, None
    fc, qc = jnp.split(uc @ w_in[:, :FOUR_WIDTH + NA_WIDTH], [FOUR_WIDTH], axis=-1)
    qc = rms_norm(split_heads(qc), q_g)
    yc = jnp.concatenate([fourier_mix(fc, w_four), context_attention(qc, kc, vc)], axis=-1) @ w_out
    return y, yc

def multiscale_pool(u):
    N = u.shape[1]
    uf = u.astype(jnp.float32)
    zeros = jnp.zeros((uf.shape[0], 1, uf.shape[2]), jnp.float32)
    cs = jnp.concatenate([zeros, jnp.cumsum(uf, axis=1)], axis=1)
    t = jnp.arange(N)
    outs = []
    for gi, w in enumerate(POOL_SIZES):
        sl = slice(gi * POOL_GC, (gi + 1) * POOL_GC)
        lo = jnp.clip(t - w // 2, 0, N)
        hi = jnp.clip(t + w - w // 2, 0, N)
        csg = cs[..., sl]
        s = jnp.take(csg, hi, axis=1) - jnp.take(csg, lo, axis=1)
        cnt = (hi - lo).astype(jnp.float32)[None, :, None]
        outs.append(s / cnt - uf[..., sl])
    return jnp.concatenate(outs, axis=-1).astype(u.dtype)

def pool_mixer(u, w_pool, pool_scale):
    B, N, _ = u.shape
    pooled = multiscale_pool(u).reshape(B, N, len(POOL_SIZES), POOL_GC)
    y = jnp.einsum('bngc,gcd->bngd', pooled, w_pool).reshape(B, N, D_MODEL)
    return y * pool_scale

def first_inputs(seed: int = 0) -> dict:
    key = jax.random.key(seed)
    ks = jax.random.split(key, 20)
    f32 = jnp.float32
    n = lambda k, s: jax.random.normal(k, s, f32)
    return {
        "x": n(ks[0], (BATCH, SEQ, D_MODEL)),
        "c": n(ks[1], (BATCH, D_MODEL)),
        "ctx": n(ks[2], (BATCH, CTX_LEN, D_MODEL)),
        "c_ctx": n(ks[3], (D_MODEL,)),
        "w_mod": n(ks[4], (DEPTH, D_MODEL, N_MOD * D_MODEL)) * D_MODEL ** -0.5,
        "b_mod": n(ks[5], (DEPTH, N_MOD * D_MODEL)) * 0.02,
        "norm1_g": 1.0 + 0.02 * n(ks[6], (DEPTH, D_MODEL)),
        "norm2_g": 1.0 + 0.02 * n(ks[7], (DEPTH, D_MODEL)),
        "w_in_even": n(ks[8], (N_EVEN, D_MODEL, FOUR_WIDTH + 3 * NA_WIDTH)) * D_MODEL ** -0.5,
        "w_four": n(ks[9], (N_EVEN, FOUR_GROUPS, FOUR_GC, FOUR_GC)) * FOUR_GC ** -0.5,
        "q_norm_g": 1.0 + 0.02 * n(ks[10], (N_EVEN, NA_HEAD_DIM)),
        "k_norm_g": 1.0 + 0.02 * n(ks[11], (N_EVEN, NA_HEAD_DIM)),
        "rpb": 0.1 * n(ks[12], (N_EVEN, NA_HEADS, 2 * NA_WIN_ROWS - 1, 2 * NA_WIN_COLS - 1)),
        "w_out_even": n(ks[13], (N_EVEN, FOUR_WIDTH + NA_WIDTH, D_MODEL)) * (FOUR_WIDTH + NA_WIDTH) ** -0.5,
        "w_pool": n(ks[14], (N_ODD, len(POOL_SIZES), POOL_GC, POOL_GC)) * POOL_GC ** -0.5,
        "pool_scale": 1.0 + 0.1 * n(ks[15], (N_ODD, D_MODEL)),
        "w_mlp1": n(ks[16], (DEPTH, D_MODEL, MLP_HIDDEN)) * D_MODEL ** -0.5,
        "w_mlp2": n(ks[17], (DEPTH, MLP_HIDDEN, D_MODEL)) * MLP_HIDDEN ** -0.5,
    }

def first_block(x, c, ctx, c_ctx, w_mod, b_mod, norm1_g, norm2_g, w_in_even, w_four, q_norm_g, k_norm_g,
              rpb, w_out_even, w_pool, pool_scale, w_mlp1, w_mlp2):
    h, hc = x, ctx
    sc = jax.nn.silu(c)
    scc = jax.nn.silu(c_ctx)
    for l in range(DEPTH):
        update_ctx = any(j % 2 == 0 for j in range(l + 1, DEPTH))
        need_ctx_in = (l % 2 == 0) or update_ctx
        mod = (sc @ w_mod[l] + b_mod[l])[:, None, :]
        sh1, sc1, g1, sh2, sc2, g2 = jnp.split(mod, N_MOD, axis=-1)
        u = modulate(rms_norm(h, norm1_g[l]), sh1, sc1)
        if need_ctx_in:
            mod_c = scc @ w_mod[l] + b_mod[l]
            csh1, csc1, cg1, csh2, csc2, cg2 = jnp.split(mod_c, N_MOD, axis=-1)
            uc = modulate(rms_norm(hc, norm1_g[l]), csh1, csc1)
        if l % 2 == 0:
            e = l // 2
            y, yc = even_mixer(u, uc, w_in_even[e], w_four[e], q_norm_g[e], k_norm_g[e], rpb[e],
                               w_out_even[e], update_ctx)
        else:
            o = l // 2
            y = pool_mixer(u, w_pool[o], pool_scale[o])
            yc = pool_mixer(uc, w_pool[o], pool_scale[o]) if update_ctx else None
        h = h + g1 * y
        h = h + g2 * sq_relu_mlp(modulate(rms_norm(h, norm2_g[l]), sh2, sc2), w_mlp1[l], w_mlp2[l])
        if update_ctx:
            hc = hc + cg1 * yc
            hc = hc + cg2 * sq_relu_mlp(modulate(rms_norm(hc, norm2_g[l]), csh2, csc2), w_mlp1[l], w_mlp2[l])
    return h


DEPTH_2 = 1

ATTN_HEAD_DIM = 64
ATTN_Q_HEADS = 16
ATTN_KV_HEADS = 2
ATTN_GROUP = ATTN_Q_HEADS // ATTN_KV_HEADS
ATTN_WIDTH = ATTN_Q_HEADS * ATTN_HEAD_DIM
ATTN_KV_WIDTH = ATTN_KV_HEADS * ATTN_HEAD_DIM
WINDOW = 128
ATTN_BLOCK = 128
HGRN_EXPAND = 128
HGRN_HEADS = D_MODEL // HGRN_EXPAND
HGRN_K = HGRN_EXPAND
HGRN_V = D_MODEL // HGRN_HEADS
HGRN_KEY_WIDTH = HGRN_HEADS * HGRN_K
HGRN_WIDTH = HGRN_HEADS * HGRN_V
CHUNK = 64
FFN_HIDDEN = -(-(8 * D_MODEL) // (3 * 256)) * 256
EPS = 1e-6
NEG_INF = -1e30
IN_SPLITS = (ATTN_WIDTH, ATTN_KV_WIDTH, ATTN_KV_WIDTH,
             HGRN_KEY_WIDTH, HGRN_KEY_WIDTH, HGRN_WIDTH, HGRN_WIDTH,
             D_MODEL, D_MODEL)
IN_WIDTH = sum(IN_SPLITS)


def rmsnorm(x, g):
    xf = x.astype(jnp.float32)
    y = xf * lax.rsqrt(jnp.mean(xf * xf, axis=-1, keepdims=True) + EPS)
    return (y * g.astype(jnp.float32)).astype(x.dtype)

def split_columns(p):
    idx = np.cumsum(np.array(IN_SPLITS))[:-1].tolist()
    return jnp.split(p, idx, axis=-1)

def sliding_window_sink_attention(q, k, v, sinks):
    B, S = q.shape[0], q.shape[1]
    nb = S // ATTN_BLOCK
    qb = q.reshape(B, nb, ATTN_BLOCK, ATTN_KV_HEADS, ATTN_GROUP, ATTN_HEAD_DIM)
    kb = k.reshape(B, nb, ATTN_BLOCK, ATTN_KV_HEADS, ATTN_HEAD_DIM)
    vb = v.reshape(B, nb, ATTN_BLOCK, ATTN_KV_HEADS, ATTN_HEAD_DIM)

    def with_prev(t):
        prev = jnp.concatenate([jnp.zeros_like(t[:, :1]), t[:, :-1]], axis=1)
        return jnp.concatenate([prev, t], axis=2)

    kw, vw = with_prev(kb), with_prev(vb)
    scale = 1.0 / math.sqrt(ATTN_HEAD_DIM)
    scores = jnp.einsum('bnqhgd,bnkhd->bnhgqk', qb, kw).astype(jnp.float32) * scale
    qi = jnp.arange(ATTN_BLOCK)[:, None]
    kj = jnp.arange(2 * ATTN_BLOCK)[None, :]
    rel = qi + ATTN_BLOCK - kj
    key_pos = jnp.arange(nb)[:, None, None] * ATTN_BLOCK - ATTN_BLOCK + kj[None]
    valid = (rel >= 0)[None] & (rel < WINDOW)[None] & (key_pos >= 0)
    scores = jnp.where(valid[None, :, None, None], scores, NEG_INF)
    sink = jnp.broadcast_to(
        sinks.astype(jnp.float32).reshape(1, 1, ATTN_KV_HEADS, ATTN_GROUP, 1, 1),
        scores.shape[:-1] + (1,))
    probs = jax.nn.softmax(jnp.concatenate([scores, sink], axis=-1), axis=-1)[..., :-1]
    out = jnp.einsum('bnhgqk,bnkhd->bnqhgd', probs.astype(v.dtype), vw)
    return out.reshape(B, S, ATTN_WIDTH)

def hgrn2_chunkwise(q, k, v, log_f):
    B, S, H, K = q.shape
    V = v.shape[-1]
    n = S // CHUNK

    def to_chunks(t):
        return t.reshape(B, n, CHUNK, H, t.shape[-1]).transpose(1, 0, 3, 2, 4)

    causal = jnp.tril(jnp.ones((CHUNK, CHUNK), dtype=bool))

    def step(state, inp):
        qc, kc, vc, gc = inp
        b = jnp.cumsum(gc, axis=2)
        b_mid = b[:, :, CHUNK // 2 - 1:CHUNK // 2]
        b_last = b[:, :, -1:]
        a = jnp.einsum('bhck,bhsk->bhcs', qc * jnp.exp(b - b_mid), kc * jnp.exp(b_mid - b))
        a = jnp.where(causal, a, 0.0)
        o = (jnp.einsum('bhcs,bhsv->bhcv', a, vc)
             + jnp.einsum('bhck,bhkv->bhcv', qc * jnp.exp(b), state))
        state = (jnp.exp(b_last)[:, :, 0, :, None] * state
                 + jnp.einsum('bhsk,bhsv->bhkv', kc * jnp.exp(b_last - b), vc))
        return state, o

    s0 = jnp.zeros((B, H, K, V), jnp.float32)
    _, o = lax.scan(step, s0, (to_chunks(q), to_chunks(k), to_chunks(v), to_chunks(log_f)))
    return o.transpose(1, 0, 3, 2, 4).reshape(B, S, H, V)

def hgrn2_branch(hq, hf, hi, hg, lb, norm_g):
    B, S = hq.shape[0], hq.shape[1]
    fp = hf.astype(jnp.float32)
    log_f = jnp.log(lb + (1.0 - lb) * jax.nn.sigmoid(fp))
    k = (1.0 - lb) * jax.nn.sigmoid(-fp)
    q = jax.nn.silu(hq.astype(jnp.float32))
    shp_k = (B, S, HGRN_HEADS, HGRN_K)
    o = hgrn2_chunkwise(q.reshape(shp_k), k.reshape(shp_k),
                        hi.astype(jnp.float32).reshape(B, S, HGRN_HEADS, HGRN_V),
                        log_f.reshape(shp_k))
    o = o * lax.rsqrt(jnp.mean(o * o, axis=-1, keepdims=True) + EPS)
    o = o.reshape(B, S, HGRN_WIDTH) * norm_g.astype(jnp.float32)
    o = o * jax.nn.sigmoid(hg.astype(jnp.float32))
    return o.astype(hq.dtype)

def second_inputs(seed: int = 0) -> dict:
    key = jax.random.key(seed)
    ks = jax.random.split(key, 20)
    D, F = D_MODEL, FFN_HIDDEN
    nrm = lambda k, shape, fan_in: jax.random.normal(k, shape, jnp.float32) * fan_in ** -0.5
    gain = lambda k, shape: 1.0 + 0.05 * jax.random.normal(k, shape, jnp.float32)
    return {
        "x": jax.random.normal(ks[0], (BATCH, SEQ, D), jnp.float32),
        "norm_mix_g": gain(ks[1], (DEPTH_2, D)),
        "w_in": nrm(ks[2], (DEPTH_2, D, IN_WIDTH), D),
        "b_in": 0.01 * jax.random.normal(ks[3], (DEPTH_2, IN_WIDTH), jnp.float32),
        "attn_sinks": 0.5 * jax.random.normal(ks[4], (DEPTH_2, ATTN_Q_HEADS), jnp.float32),
        "hgrn_lb_logits": gain(ks[5], (DEPTH_2 + 1, HGRN_KEY_WIDTH)),
        "hgrn_norm_g": gain(ks[6], (DEPTH_2, HGRN_WIDTH)),
        "w_branch_attn": nrm(ks[7], (DEPTH_2, ATTN_WIDTH, D), ATTN_WIDTH),
        "w_branch_hgrn": nrm(ks[8], (DEPTH_2, HGRN_WIDTH, D), HGRN_WIDTH),
        "w_out": nrm(ks[9], (DEPTH_2, D, D), D),
        "norm_ffn_g": gain(ks[10], (DEPTH_2, D)),
        "w_ffn_gate": nrm(ks[11], (DEPTH_2, D, F), D),
        "w_ffn_up": nrm(ks[12], (DEPTH_2, D, F), D),
        "w_ffn_down": nrm(ks[13], (DEPTH_2, F, D), F),
        "norm_final_g": gain(ks[14], (D,)),
    }

def second_block(x, norm_mix_g, w_in, b_in, attn_sinks, hgrn_lb_logits, hgrn_norm_g,
              w_branch_attn, w_branch_hgrn, w_out, norm_ffn_g, w_ffn_gate, w_ffn_up,
              w_ffn_down, norm_final_g):
    lb_all = jnp.cumsum(jax.nn.softmax(hgrn_lb_logits.astype(jnp.float32), axis=0), axis=0)
    h = x
    for layer in range(DEPTH_2):
        u = rmsnorm(h, norm_mix_g[layer])
        p = jnp.einsum('bsd,de->bse', u, w_in[layer]) + b_in[layer]
        aq, ak, av, hq, hf, hi, hg, gate_a, gate_b = split_columns(p)
        y_attn = sliding_window_sink_attention(aq, ak, av, attn_sinks[layer])
        y_hgrn = hgrn2_branch(hq, hf, hi, hg, lb_all[layer], hgrn_norm_g[layer])
        ya = jnp.einsum('bse,ed->bsd', y_attn, w_branch_attn[layer])
        yb = jnp.einsum('bse,ed->bsd', y_hgrn, w_branch_hgrn[layer])
        merged = jax.nn.sigmoid(gate_a) * ya + jax.nn.sigmoid(gate_b) * yb
        h = h + jnp.einsum('bsd,de->bse', merged, w_out[layer])
        u = rmsnorm(h, norm_ffn_g[layer])
        z = (jax.nn.silu(jnp.einsum('bsd,df->bsf', u, w_ffn_gate[layer]))
             * jnp.einsum('bsd,df->bsf', u, w_ffn_up[layer]))
        h = h + jnp.einsum('bsf,fd->bsd', z, w_ffn_down[layer])
    return rmsnorm(h, norm_final_g)


def setup_inputs(seed=0):
    out = dict(first_inputs(seed))
    for name, value in second_inputs(seed + 1).items():
        if name != "x":
            out[name + "_2"] = value
    return out


def reference(
    x, c, ctx, c_ctx, w_mod, b_mod, norm1_g, norm2_g, w_in_even, w_four, q_norm_g, k_norm_g,
    rpb, w_out_even, w_pool, pool_scale, w_mlp1, w_mlp2, norm_mix_g_2, w_in_2, b_in_2,
    attn_sinks_2, hgrn_lb_logits_2, hgrn_norm_g_2, w_branch_attn_2, w_branch_hgrn_2, w_out_2,
    norm_ffn_g_2, w_ffn_gate_2, w_ffn_up_2, w_ffn_down_2, norm_final_g_2,
):
    x = first_block(
        x, c, ctx, c_ctx, w_mod, b_mod, norm1_g, norm2_g, w_in_even, w_four, q_norm_g, k_norm_g,
        rpb, w_out_even, w_pool, pool_scale, w_mlp1, w_mlp2,
    )
    return second_block(
        x, norm_mix_g_2, w_in_2, b_in_2, attn_sinks_2, hgrn_lb_logits_2, hgrn_norm_g_2,
        w_branch_attn_2, w_branch_hgrn_2, w_out_2, norm_ffn_g_2, w_ffn_gate_2, w_ffn_up_2,
        w_ffn_down_2, norm_final_g_2,
    )


_drawn_inputs = setup_inputs


def setup_inputs(seed=0):
    import zlib

    import numpy as np

    out = dict(_drawn_inputs(seed))
    spreads = {}
    factors = {'norm1_g': 5.946,
     'q_norm_g': 8.0,
     'k_norm_g': 8.0,
     'rpb': 8.0,
     'norm_mix_g_2': 4.952,
     'b_in_2': 8.0,
     'attn_sinks_2': 58.927,
     'hgrn_lb_logits_2': 8.0,
     'hgrn_norm_g_2': 8.0,
     'norm_ffn_g_2': 3.247}
    for name, (base, spread) in spreads.items():
        noise = np.random.default_rng([zlib.crc32(name.encode()), seed]).standard_normal(out[name].shape)
        drawn = base * np.exp(spread * noise) if base else spread * noise
        out[name] = __import__('jax').numpy.asarray(drawn.astype(out[name].dtype))
    for name, factor in factors.items():
        out[name] = (out[name] * factor).astype(out[name].dtype)
    return out
```

```python
from contextlib import ExitStack

import numpy as np

import concourse.bass as bass
from concourse import mybir

F32 = mybir.dt.float32
F32R = mybir.dt.float32r
ALU = mybir.AluOpType
ACT = mybir.ActivationFunctionType
AX_X = mybir.AxisListType.X

P = 128
D = 1024
KC = D // P
S = 512
L = 256
BC = 256
EPS = 1e-6
NEG = -1e30
SQ0 = 2
KB = 1024

NH, DH = 8, 64
ROWS, COLS, WIN = 8, 64, 32
QT, QC = 4, 16
W0 = [0, 8, 24, 32]
TOFF = [16, 8, 8, 0]
TMASK = [0, 1, 1, 2]
FG = 4
RAW = 4

PLAN = [("v", 2), ("k", 2), ("q", 2), ("f", 2), ("wout", 4), ("mlp0", 32), ("pool", 4), ("mlp1", 32),
        ("aq", 4), ("akv", 1), ("ga", 8), ("hgrn", 16), ("gb", 8), ("wout2", 4), ("ffn", 34)]
FIRST, _at = {}, 0
for _name, _n in PLAN:
    FIRST[_name] = _at
    _at += _n
BLOCKS = _at
NORM = {"x": 0, "ctx": 1, "mlp0": 2, "pool": 3, "mlp1": 4, "mix2": 5, "ffn": 6, "final": 7}
H_FROM = {"mlp0": FIRST["wout"], "pool": FIRST["mlp0"] + 28, "mix2": FIRST["mlp1"] + 28,
          "ffn": FIRST["wout2"], "final": FIRST["ffn"] + 30}
MOD0, MOD1 = 16, 24

C_ID, C_OND, C_ONH, C_ONE, C_EPS, C_EPSQ, C_ONV, C_END = 0, 128, 256, 384, 385, 386, 387, 515
V_G1, V_G2, V_QG, V_KG, V_MIX, V_FFN, V_FIN, V_PS, V_HG, V_BQ, V_BK, V_BGA, V_BGB, V_BHQ, V_BHF, V_BHG, V_LB, V_SINK, V_END = (
    0, 16, 32, 33, 34, 42, 50, 58, 66, 74, 82, 83, 91, 99, 107, 115, 123, 139, 155)
HG_HEADS = 8


def build_program(nc, t):
    es = ExitStack()
    with es:
        def sem(name):
            return es.enter_context(nc.semaphore(name))

        base = 16512

        def at(name, shape, dt, offset):
            return nc.alloc_sbuf_tensor_at(name, shape, dt, offset=base + offset)

        o = 0
        h = at("h", [P, KC, S], F32, o); o += 16 * KB
        uh = at("uh", [P, KC, S], F32R, o); o += 16 * KB
        ul = at("ul", [P, KC, S], F32R, o); o += 16 * KB
        raw = at("raw", [P, RAW, KC, BC], F32, o); o += 32 * KB
        wh = at("wh", [P, 2, KC, BC], F32R, o); o += 16 * KB
        wl = at("wl", [P, 2, KC, BC], F32R, o); o += 16 * KB
        con = at("con", [P, C_END + 5], F32, o); o += 2080
        vec = at("vec", [P, V_END + 5], F32, o); o += 640
        bmod = at("bmod", [P, 96], F32, o); o += 384
        modc = at("modc", [P, 96], F32, o); o += 384
        modx = at("modx", [P, 16], F32, o); o += 64
        gm = at("gm", [P, 6, KC], F32, o); o += 192
        lbs = at("lbs", [P, 3, KC], F32, o); o += 96
        csil = at("csil", [P, KC, 2], F32, o); o += 64
        craw = at("craw", [P, KC, 2], F32, o); o += 64
        stat = at("stat", [P, 10, 2], F32, o); o += 96
        A = (o + 31) // 32 * 32
        modf = at("modf", [P, 8, KC, BC], F32, A)
        ctxT = at("ctxT", [P, KC, L], F32, A + 64 * KB)
        modrow = at("modrow", [2, 2048], F32, A + 72 * KB)
        qT = at("qT", [P, 4, S], F32, A)
        kT = at("kT", [P, 4, S], F32, A + 8 * KB)
        kcT = at("kcT", [P, 4, L], F32, A + 16 * KB)
        vc = at("vc", [P, 2, S], F32, A + 20 * KB)
        fT = at("fT", [P, 4, S], F32, A + 24 * KB)
        vnat = at("vnat", [P, 4, S], F32, A + 24 * KB)
        vwin = at("vwin", [P, 2 * QT, S], F32, A + 32 * KB)
        mraw = at("mraw", [P, 2, KC, BC], F32, A + 48 * KB)
        tab = at("tab", [P, NH * ROWS, 48], F32, A + 48 * KB)
        tm = at("tm", [P, 2, S], F32, A + 60 * KB)
        cs = at("cs", [P, 2 * P], F32, A + 60 * KB)
        w4 = at("w4", [P, FG, P], F32, A + 61 * KB)
        uch = at("uch", [P, KC, L], F32R, A + 72 * KB)
        ucl = at("ucl", [P, KC, L], F32R, A + 64 * KB)
        dftc = at("dftc", [P, 4, S], F32, A + 64 * KB)
        dfts = at("dfts", [P, 4, S], F32, A + 72 * KB)
        sc = at("sc", [P, 2, S], F32, A + 64 * KB)
        pn = at("pn", [P, 2, S], F32, A + 68 * KB)
        pT = at("pT", [P, 2, S], F32, A + 72 * KB)
        sq = at("sq", [P, 2, S], F32, A + 80 * KB)
        tt = at("tt", [P, 2, S], F32, A + 84 * KB)
        ysb = at("ysb", [P, 4, 2 * P], F32, A + 80 * KB)
        cw = at("cw", [P, FG, 2 * P], F32, A + 84 * KB)
        rstd = at("rstd", [P, S], F32, A + 88 * KB)
        mask = at("mask", [P, 3, 256], F32, A + 88 * KB)
        acc = at("acc", [P, 2, BC], F32, A + 88 * KB)
        ah = at("ah", [P, KC, S], F32R, A)
        al = at("al", [P, KC, S], F32R, A + 16 * KB)
        r1 = at("r1", [P, 2, S], F32, A + 64 * KB)
        v1 = at("v1", [P, 2, S], F32, A + 68 * KB)

        band = at("band", [P, 3, FG, 144], F32, A)
        zt = at("zt", [P, FG, 4, BC], F32, A + 16 * KB)
        aqT = at("aqT", [P, KC, S], F32, A + 32 * KB)
        akT = at("akT", [P, S], F32, A + 48 * KB)
        av = at("av", [P, 4, P], F32, A + 50 * KB)
        wmask = at("wmask", [P, 2, 256], F32, A + 52 * KB)
        bvrow = at("bvrow", [P, P], F32, A + 54 * KB)
        sc2 = at("sc2", [P, 2, S], F32, A + 55 * KB)
        pn2 = at("pn2", [P, 2, S], F32, A + 59 * KB)
        pT2 = at("pT2", [P, 2, S], F32, A + 64 * KB)
        merged = at("merged", [P, KC, S], F32, A + 64 * KB)
        sg = at("sg", [P, 2, S], F32, A + 80 * KB)
        mt = at("mt", [P, 2, S], F32, A + 84 * KB)
        yh = at("yh", [P, KC, S], F32, A + 32 * KB)
        hq = at("hq", [P, 2, S], F32, A)
        hk = at("hk", [P, 2, S], F32, A + 4 * KB)
        hv = at("hv", [P, 2, 4, P], F32, A + 8 * KB)
        hg = at("hg", [P, 2, S], F32, A + 12 * KB)
        ex = at("ex", [P, 4, S], F32, A + 16 * KB)
        lf = at("lf", [P, S], F32, A + 24 * KB)
        lft = at("lft", [P, 4, P], F32, A + 26 * KB)
        krt = at("krt", [P, 4, P], F32, A + 28 * KB)
        qb = at("qb", [P, S], F32, A + 30 * KB)
        att = at("att", [P, S], F32, A + 48 * KB)
        st = at("st", [P, 8, P], F32, A + 50 * KB)
        cm = at("cm", [P, 3, P], F32, A + 54 * KB)
        cmask = at("cmask", [P, S], mybir.dt.uint32, A + 56 * KB)
        bhrow = at("bhrow", [P, HG_HEADS, P], F32, A + 58 * KB)
        osq = at("osq", [P, S], F32, A + 62 * KB)
        ort = at("ort", [P, S], F32, A + 80 * KB)
        sgm = at("sgm", [P, S], F32, A + 82 * KB)
        onum = at("onum", [P, S], F32, A + 84 * KB)
        gs = at("gs", [P, 2, S], F32, A + 32 * KB)
        gz = at("gz", [P, 2, S], F32, A + 36 * KB)
        fin = at("fin", [P, KC, S], F32, A + 40 * KB)

        bank = [nc.alloc_psum_tensor(f"bank{i}", [P, S], F32) for i in range(8)]

        raw_full = [sem(f"raw_full{i}") for i in range(RAW)]
        split_hi, split_lo = sem("split_hi"), sem("split_lo")
        bank_full = [sem(f"bank_full{i}") for i in range(4)]
        bank_free = [sem(f"bank_free{i}") for i in range(4)]
        c_in, const_in, x_in, ctx_in = sem("c_in"), sem("const_in"), sem("x_in"), sem("ctx_in")
        modf_in = [sem(f"modf_in{i}") for i in range(8)]
        mraw_full = [sem(f"mraw_full{i}") for i in range(2)]
        macc, mcol_full, mcol_used = sem("macc"), sem("mcol_full"), sem("mcol_used")
        csil_ready, modrow_full, modrow_copied, mod0_full, mod0_ready = (
            sem("csil_ready"), sem("modrow_full"), sem("modrow_copied"), sem("mod0_full"), sem("mod0_ready"))
        sq_ready, sq_used, root_ready, rstd_ready = sem("sq_ready"), sem("sq_used"), sem("root_ready"), sem("rstd_ready")
        t_ready, uhi_ready, ulo_ready = sem("t_ready"), sem("uhi_ready"), sem("ulo_ready")
        gain_ready = sem("gain_ready")
        ctx_full, ctx_free = sem("ctx_full"), sem("ctx_free")
        v_copied, vwin_in, tab_in, dft_in, w4_in = (
            sem("v_copied"), sem("vwin_in"), sem("tab_in"), sem("dft_in"), sem("w4_in"))
        hsq_ready, hsum_full, hroot_ready, hrstd_ready, hn_done = (
            sem("hsq_ready"), sem("hsum_full"), sem("hroot_ready"), sem("hrstd_ready"), sem("hn_done"))
        f_copied, cw_full, cw_ready, y_full, y_ready, four_full, four_hi, four_lo = (
            sem("f_copied"), sem("cw_full"), sem("cw_ready"), sem("y_full"), sem("y_ready"),
            sem("four_full"), sem("four_hi"), sem("four_lo"))
        tm_zero, tm_half, tm_ready, s_full, smax, nmax, p_exp, p_recip, p_norm = (
            sem("tm_zero"), sem("tm_half"), sem("tm_ready"), sem("s_full"), sem("smax"), sem("nmax"),
            sem("p_exp"), sem("p_recip"), sem("p_norm"))
        pt_full, pt_copied, o_full, o_hi, o_lo = sem("pt_full"), sem("pt_copied"), sem("o_full"), sem("o_hi"), sem("o_lo")
        square_ready, a_hi, a_lo = sem("square_ready"), sem("a_hi"), sem("a_lo")
        band_in, yp_full, yp_free = sem("band_in"), sem("yp_full"), sem("yp_free")
        b2_in, lb_ready, akv_ready = sem("b2_in"), sem("lb_ready"), sem("akv_ready")
        s2_full, smax2, nmax2, sink_ready, p2_exp, tot2, p2_recip, p2_norm = (
            sem("s2_full"), sem("smax2"), sem("nmax2"), sem("sink_ready"), sem("p2_exp"), sem("tot2"), sem("p2_recip"), sem("p2_norm"))
        pt2_full, pt2_copied, o2_full, o2_hi, o2_lo = sem("pt2_full"), sem("pt2_copied"), sem("o2_full"), sem("o2_hi"), sem("o2_lo")
        merged_ready = sem("merged_ready")
        hg_in, att_zero = sem("hg_in"), sem("att_zero")
        q_sig, q_done, f_sig, k_done, f_lin, f_log, v_done, g_done = (
            sem("q_sig"), sem("q_done"), sem("f_sig"), sem("k_done"), sem("f_lin"), sem("f_log"), sem("v_done"), sem("g_done"))
        lft_full, lft_copied, cum_full, ex_done, qd_done, kd_done, qb_done, kr_done = (
            sem("lft_full"), sem("lft_copied"), sem("cum_full"), sem("ex_done"), sem("qd_done"), sem("kd_done"), sem("qb_done"), sem("kr_done"))
        krt_full, krt_copied, att_full, att_done, upd_full, st_done, oh_full = (
            sem("krt_full"), sem("krt_copied"), sem("att_full"), sem("att_done"), sem("upd_full"), sem("st_done"), sem("oh_full"))
        osq_ready, osum_full, oroot_ready, orstd_ready, on_ready, yh_ready = (
            sem("osq_ready"), sem("osum_full"), sem("oroot_ready"), sem("orstd_ready"), sem("on_ready"), sem("yh_ready"))
        y_hi, y_lo, m_hi, m_lo = sem("y_hi"), sem("y_lo"), sem("m_hi"), sem("m_lo")
        gs_ready, gz_ready, zv_ready, z_hi, z_lo, out_ready = (
            sem("gs_ready"), sem("gz_ready"), sem("zv_ready"), sem("z_hi"), sem("z_lo"), sem("out_ready"))
        out_done = sem("out_done")
        S2_BANKS = [(4, 5), (0, 1)]
        ITEMS2 = [(c, n) for c in range(KC) for n in range(4)]

        ident = con[:, C_ID:C_ID + P]
        ones_d = con[:, C_OND:C_OND + P]
        ones_h = con[:, C_ONH:C_ONH + P]
        ones_v = con[:, C_ONV:C_ONV + P]
        one_col = con[:, C_ONE:C_ONE + 1]
        eps_col = con[:, C_EPS:C_EPS + 1]
        epsq_col = con[:, C_EPSQ:C_EPSQ + 1]
        MODS_AT = [3, 3, 1, 1, 1, 1, 3, 3]
        mods_before = [sum(MODS_AT[:b]) for b in range(9)]

        def f32(x):
            return x.bitcast(F32)

        def mod(layer, j, k):
            return modc[:, 48 * layer + 8 * j + k:48 * layer + 8 * j + k + 1]

        def bank_of(b, half):
            return 2 * (b % 2) + half

        def used(b, q=0, per=0):
            return b // 2 + (per // 2) * q if per else b // 2

        def count(b, q=0, per=0):
            return b + per * q if per else b

        def wait_block(eng, b, q=0, per=0):
            eng.wait_ge(bank_full[bank_of(b, 1)], used(b, q, per) + 1)

        HN = [("k", 0), ("k", 1), ("kc", 0), ("k", 2), ("k", 3), ("kc", 1), ("q", 0), ("q", 1), ("q", 2), ("q", 3)]
        HN_OF = {2: [0, 1, 2], 3: [3, 4, 5], 4: [6, 7], 5: [8, 9]}

        def hn_place(i):
            kind, m = HN[i]
            if kind == "kc":
                return bank[4 + m][:, :], ctx_free, kcT[:, 2 * m:2 * m + 2, :].rearrange("p a n -> p (a n)")
            b = {"k": 2, "q": 4}[kind] + m // 2
            return bank[bank_of(b, m % 2)][:, :], bank_free[bank_of(b, m % 2)], (kT if kind == "k" else qT)[:, m, :]

        def hn_wait(eng, i):
            kind, m = HN[i]
            if kind == "kc":
                eng.wait_ge(ctx_full, 3 + m)
            else:
                b = {"k": 2, "q": 4}[kind] + m // 2
                eng.wait_ge(bank_full[bank_of(b, m % 2)], used(b) + 1)

        def hn_wait_done(eng, i):
            kind, m = HN[i]
            if kind == "kc":
                eng.wait_ge(ctx_free, 3 + m)
            else:
                b = {"k": 2, "q": 4}[kind] + m // 2
                eng.wait_ge(bank_free[bank_of(b, m % 2)], used(b) + 1)

        def h_wait(eng, name, k):
            if name == "mlp1":
                eng.wait_ge(yp_free, k + 1)
                return
            b = H_FROM[name] + k // 2
            eng.wait_ge(bank_free[bank_of(b, k % 2)], used(b) + 1)

        ITEMS = [(hp, q, e) for hp in range(4) for q in range(QT) for e in range(2)]

        def by_column(x, lo, n):
            return x.rearrange("p (r c) -> p r c", c=COLS)[:, :, lo:lo + n]

        block = es.enter_context(nc.Block())

        @block.sync
        def _(sp):
            def load(b, src, q=0, per=0, nk=KC):
                if per or b >= RAW:
                    sp.wait_ge(split_hi, count(b - RAW + 1, q, per))
                    sp.wait_ge(split_lo, count(b - RAW + 1, q, per))
                sp.dma_start(raw[:, b % RAW, 0:nk, :], src).then_inc(raw_full[b % RAW], 16)

            def load_mod(m, q=0, per=0):
                if m < 2 and not per:
                    sp.wait_ge(modrow_full, 8)
                else:
                    sp.wait_ge(macc, 8 * (m - 1) + 8 * per * q if per else 8 * (m - 1))
                sp.dma_start(mraw[:, m % 2], t["w_modr"][count(m, q, per)]).then_inc(mraw_full[m % 2], 16)

            sp.dma_start(craw[:], t["c_cols"]).then_inc(c_in, 16)
            sp.dma_start(con[:, 0:C_END], t["consts"]).then_inc(const_in, 16)
            sp.dma_start(vec[:, 0:V_END], t["vecs"]).then_inc(const_in, 16)
            sp.dma_start(bmod[:], t["b_mod"]).then_inc(const_in, 16)
            for i in range(8):
                sp.dma_start(modf[:, i], t["w_modf"][i]).then_inc(modf_in[i], 16)
            sp.dma_start(h[:], t["xT"]).then_inc(x_in, 16)
            sp.dma_start(ctxT[:], t["ctxT"]).then_inc(ctx_in, 16)
            for b in range(8):
                load(b, t["w_in"][b])
                for m in range(mods_before[b], mods_before[b + 1]):
                    load_mod(m)
                if b == 5:
                    for bi in range(4):
                        sp.wait_ge(bank_free[bi], 1)
                    for w in range(QT):
                        for j in range(ROWS):
                            sp.dma_start(vwin[32 * (j % 4):32 * (j % 4) + 32, 2 * w + j // 4, :],
                                         vnat[64 * (j % 2) + W0[w]:64 * (j % 2) + W0[w] + WIN, j // 2, :])\
                              .then_inc(vwin_in, 16)
                if b == 6:
                    sp.wait_ge(ctx_full, 4)
                    sp.dma_start(dftc[:], t["dftc"]).then_inc(dft_in, 16)
                    sp.dma_start(dfts[:], t["dfts"]).then_inc(dft_in, 16)
            for b in range(8, 12):
                if b == 10:
                    sp.wait_ge(macc, 8 * MOD0)
                    sp.dma_start(cs[:], t["cs"]).then_inc(w4_in, 16)
                    sp.dma_start(w4[:], t["w4"]).then_inc(w4_in, 16)
                    for c in range(QC):
                        sp.dma_start(tab[c::QC], t["rpb"][:, :, QC - 1 - c:QC - 1 - c + 48]).then_inc(tab_in, 16)
                    sp.wait_ge(mcol_full, MOD0)
                    sp.dma_start(mask[:], t["mask"]).then_inc(tab_in, 16)
                load(b, t["w_out"][b - 8])
            m0 = FIRST["mlp0"]
            with sp.Fori(0, 4) as q:
                for j in range(8):
                    load(m0 + j, (t["w1_0"] if j < 4 else t["w2_0"])[4 * q + j % 4], q, 8)
                    if j == 0:
                        sp.wait_ge(tm_ready, len(ITEMS))
                    if j < 6:
                        load_mod(MOD0 + j, q, 6)
            b0 = FIRST["pool"]
            for g in range(FG):
                load(b0 + g, t["w_pool"][g], nk=2)
                if g == 0:
                    wait_block(sp, FIRST["pool"] - 1)
                    sp.dma_start(band[:], t["band"]).then_inc(band_in, 16)
            b0 = FIRST["mlp1"]
            with sp.Fori(0, 4) as q:
                for j in range(8):
                    load(b0 + j, (t["w1_1"] if j < 4 else t["w2_1"])[4 * q + j % 4], q, 8)
            b0 = FIRST["aq"]
            for j in range(5):
                load(b0 + j, t["w_att2"][j])
                if j == 2:
                    wait_block(sp, b0 - 1)
                    sp.dma_start(wmask[:], t["wmask"]).then_inc(b2_in, 16)
                    sp.dma_start(bvrow[:], t["bvrow"]).then_inc(b2_in, 16)
            for j in range(8):
                load(FIRST["ga"] + j, (t["w_ga"] if j % 2 == 0 else t["w_ba"])[j // 2])
            sp.wait_ge(o2_lo, KC)
            for dst, src in ((cm, "cm"), (cmask, "cmask"), (bhrow, "bhrow")):
                sp.dma_start(dst[:], t[src]).then_inc(hg_in, 16)
            b0 = FIRST["hgrn"]
            with sp.Fori(0, 4) as q:
                for j in range(4):
                    load(b0 + j, t["w_hg"][4 * q + j], q, 4)
            for j in range(8):
                load(FIRST["gb"] + j, (t["w_gb"] if j % 2 == 0 else t["w_bb"])[j // 2])
            for j in range(4):
                load(FIRST["wout2"] + j, t["w_out2"][j])
            b0 = FIRST["ffn"]
            with sp.Fori(0, 2) as q:
                for j in range(12):
                    src = t["w_gu"][8 * q + j] if j < 8 else t["w_dn"][4 * q + j - 8]
                    load(b0 + j, src, q, 12)
            for j in range(10):
                load(b0 + 24 + j, t["w_gu"][16 + j] if j < 6 else t["w_dn"][8 + j - 6, :, 0:6, :], nk=KC if j < 6 else 6)
            for k in range(KC):
                sp.wait_ge(out_ready, k + 1)
                sp.dma_start(t["out"][:, k, :], fin[:, k, :]).then_inc(out_done, 16)
            sp.wait_ge(out_done, 16 * KC)

        @block.scalar
        def _(act):
            def split(b, q=0, per=0):
                s = b % RAW
                act.wait_ge(raw_full[s], 16 * (b // RAW + 1) + 16 * (per // RAW) * q if per else 16 * (b // RAW + 1))
                if per or b >= 2:
                    act.wait_ge(bank_full[bank_of(b, 1)], used(b, q, per))
                act.activation(wh[:, b % 2], raw[:, s], ACT.Copy).then_inc(split_hi, 1)

            def norm(name, src, shift, hi, n=S, wait=None):
                i = NORM[name]
                for k in range(KC):
                    wait(k)
                    if i or k >= 2:
                        act.wait_ge(sq_used, 8 * i + k - 1)
                    act.activation(sq[:, k % 2, 0:n], src[:, k, :], ACT.Square).then_inc(sq_ready, 1)
                act.wait_ge(sq_used, 8 * i + 8)
                act.activation(rstd[:, 0:n], bank[6][:, 0:n], ACT.Sqrt, bias=eps_col).then_inc(root_ready, 1)
                if hi is None:
                    return
                for k in range(KC):
                    act.wait_ge(t_ready, 8 * i + k + 1)
                    if shift is None:
                        ins = act.activation(hi[:, k, :], tt[:, k % 2, 0:n], ACT.Copy)
                    else:
                        ins = act.activation(hi[:, k, :], tt[:, k % 2, 0:n], ACT.Identity, bias=shift(k))
                    ins.then_inc(uhi_ready, 1)

            act.wait_ge(c_in, 16)
            act.activation(csil[:], craw[:], ACT.Silu).then_inc(csil_ready, 1)
            act.wait_ge(const_in, 48)
            norm("x", h, lambda k: mod(0, 0, k), uh, wait=lambda k: act.wait_ge(x_in, 16) if k == 0 else None)
            norm("ctx", ctxT, lambda k: modx[:, k:k + 1], uch, L, wait=lambda k: act.wait_ge(ctx_in, 16) if k == 0 else None)
            split(0)

            def hn_square(i):
                hn_wait(act, i)
                if i >= 2:
                    act.wait_ge(hsum_full, i - 1)
                act.activation(sq[:, i % 2], hn_place(i)[0], ACT.Square).then_inc(hsq_ready, 1)

            def hn_root(i):
                act.wait_ge(hsum_full, i + 1)
                if i >= 2:
                    hn_wait_done(act, i - 2)
                if HN[i][0] == "q":
                    act.activation(tt[:, i % 2], bank[6][:], ACT.Sqrt, bias=epsq_col, scale=float(DH)).then_inc(hroot_ready, 1)
                else:
                    act.activation(tt[:, i % 2], bank[6][:], ACT.Sqrt, bias=eps_col).then_inc(hroot_ready, 1)

            for b in range(8):
                split(b + 1)
                for i in HN_OF.get(b - 1, []):
                    hn_root(i)
                if b < 2:
                    act.wait_ge(ctx_full, b + 1)
                    act.activation(vc[:, :, BC * b:BC * b + BC], bank[4 + b][:].rearrange("p (a n) -> p a n", a=2), ACT.Copy).then_inc(ctx_free, 1)
                    for half in range(2):
                        bi = bank_of(b, half)
                        act.wait_ge(bank_full[bi], used(b) + 1)
                        act.activation(vnat[:, 2 * half:2 * half + 2, BC * b:BC * b + BC],
                                       bank[bi][:].rearrange("p (a n) -> p a n", a=2), ACT.Copy).then_inc(bank_free[bi], 1)
                for i in HN_OF.get(b, []):
                    hn_square(i)
                if b >= 6:
                    for half in range(2):
                        bi = bank_of(b, half)
                        act.wait_ge(bank_full[bi], used(b) + 1)
                        if b == 6 and half == 0:
                            act.wait_ge(vwin_in, 16 * 32)
                        act.activation(fT[:, 2 * (b - 6) + half, :], bank[bi][:], ACT.Copy).then_inc(bank_free[bi], 1)
            for g in range(FG):
                act.wait_ge(y_full, 2 * g + 1)
                if g:
                    act.wait_ge(four_full, g)
                act.activation(ysb[:, 0:2, :], bank[6][:].rearrange("p (a n) -> p a n", a=2), ACT.Copy).then_inc(y_ready, 1)
                act.wait_ge(y_full, 2 * g + 2)
                act.activation(ysb[:, 2:4, :], bank[7][:].rearrange("p (a n) -> p a n", a=2), ACT.Copy).then_inc(y_ready, 1)
                act.wait_ge(four_full, g + 1)
                act.activation(uh[:, g, :], bank[4 + g % 2][:], ACT.Copy).then_inc(four_hi, 1)

            def exp(i):
                act.wait_ge(nmax, i + 1)
                act.activation(sc[:, i % 2], sc[:, i % 2], ACT.Exp, bias=stat[:, 1, i % 2:i % 2 + 1],
                               accum_out=stat[:, 2, i % 2:i % 2 + 1]).then_inc(p_exp, 1)

            def copy_pt(i):
                act.wait_ge(pt_full, i + 1)
                if i >= 2:
                    act.wait_ge(o_full, i - 1)
                act.activation(pT[:, i % 2], bank[6 + i % 2][:], ACT.Copy).then_inc(pt_copied, 1)

            def o_high(hp):
                act.wait_ge(o_full, 8 * hp + 8)
                act.activation(uh[:, 4 + hp, :].rearrange("p (r w c) -> p w r c", r=ROWS, c=QC),
                               bank[2 + hp % 2][:].rearrange("p (w r c) -> p w r c", r=ROWS, c=QC), ACT.Copy).then_inc(o_hi, 1)

            for i in range(len(ITEMS) + 1):
                if i < len(ITEMS):
                    exp(i)
                if i >= 1:
                    copy_pt(i - 1)
                if i >= 8 and i % 8 == 2:
                    o_high(i // 8 - 1)
            o_high(3)
            for b in range(8, 12):
                split(b + 1)

            def mlp(layer):
                b0 = FIRST[f"mlp{layer}"]
                with act.Fori(0, 4) as q:
                    for j in range(8):
                        split(b0 + j + 1, q, 8)
                        if j >= 4:
                            continue
                        for half in range(2):
                            bi, m = bank_of(b0 + j, half), 2 * j + half
                            act.wait_ge(bank_full[bi], used(b0 + j, q, 8) + 1)
                            act.wait_ge(square_ready, SQ0 + 32 * layer + m - 1 + 8 * q)
                            act.activation(r1[:, m % 2], bank[bi][:], ACT.Relu).then_inc(bank_free[bi], 1)

            norm("mlp0", h, lambda k: mod(0, 3, k), uh, wait=lambda k: h_wait(act, "mlp0", k))
            mlp(0)

            norm("pool", h, lambda k: mod(1, 0, k), uh, wait=lambda k: h_wait(act, "pool", k))
            b0 = FIRST["pool"]
            for g in range(FG):
                split(b0 + g + 1)
                for half in range(2):
                    bi = bank_of(b0 + g, half)
                    act.wait_ge(bank_full[bi], used(b0 + g) + 1)
                    act.activation(zt[:, g, 2 * half:2 * half + 2, :], bank[bi][:].rearrange("p (a n) -> p a n", a=2), ACT.Copy).then_inc(bank_free[bi], 1)
            norm("mlp1", h, lambda k: mod(1, 3, k), uh, wait=lambda k: h_wait(act, "mlp1", k))
            mlp(1)

            norm("mix2", h, None, uh, wait=lambda k: h_wait(act, "mix2", k))
            act.wait_ge(lb_ready, 1)
            act.activation(lbs[:, 0, :], lbs[:, 0, :], ACT.Sigmoid).then_inc(lb_ready, 1)
            b0 = FIRST["aq"]
            for j in range(5):
                split(b0 + j + 1)
                for half in range(2 if j < 4 else 1):
                    bi = bank_of(b0 + j, half)
                    act.wait_ge(bank_full[bi], used(b0 + j) + 1)
                    out, col = (aqT[:, 2 * j + half, :], V_BQ + 2 * j + half) if j < 4 else (akT[:], V_BK)
                    act.activation(out, bank[bi][:], ACT.Identity, bias=vec[:, col:col + 1]).then_inc(bank_free[bi], 1)

            def exp2(i):
                act.wait_ge(sink_ready, i + 1)
                act.activation(stat[:, 6, :], stat[:, 5, :], ACT.Exp).then_inc(p2_exp, 1)
                for e in range(2):
                    x = sc2[:, i % 2, 256 * e:256 * e + 256]
                    act.activation(x, x, ACT.Exp, bias=stat[:, 4, e:e + 1], accum_out=stat[:, 7, e:e + 1]).then_inc(p2_exp, 1)

            def copy_pt2(i):
                act.wait_ge(pt2_full, i + 1)
                if i >= 2:
                    act.wait_ge(o2_full, i - 1)
                act.activation(pT2[:, i % 2], bank[6 + i % 2][:], ACT.Copy).then_inc(pt2_copied, 1)

            def o2_high(c):
                act.wait_ge(o2_full, 4 * c + 4)
                act.activation(ah[:, c, :], bank[2 + c % 2][:], ACT.Copy).then_inc(o2_hi, 1)

            for i in range(len(ITEMS2) + 1):
                if i < len(ITEMS2):
                    exp2(i)
                if i >= 1:
                    copy_pt2(i - 1)
                if i >= 4 and i % 4 == 2:
                    o2_high(i // 4 - 1)
            o2_high(KC - 1)

            def gates(first, col):
                for j in range(8):
                    split(first + j + 1)
                    if j % 2:
                        continue
                    for half in range(2):
                        bi, m = bank_of(first + j, half), j + half
                        act.wait_ge(bank_full[bi], used(first + j) + 1)
                        if j:
                            act.wait_ge(bank_free[bank_of(first + j - 1, half)], used(first + j - 1) + 1)
                        act.activation(sg[:, half], bank[bi][:], ACT.Sigmoid, bias=vec[:, col + m:col + m + 1]).then_inc(bank_free[bi], 1)

            gates(FIRST["ga"], V_BGA)

            b0 = FIRST["hgrn"]

            def col(first, hd, q):
                return vec[:, first + hd:first + hd + 1] if isinstance(q, int) else vec[:, bass.ds(first + hd + 2 * q, 1)]

            def head_units(hd, q=0):
                per = 0 if isinstance(q, int) else 4
                n = count(hd, q, 2 if per else 0)
                b = b0 + 2 * hd
                split(b + 1, q, per)
                act.wait_ge(bank_full[bank_of(b, 0)], used(b, q, per) + 1)
                if per or hd:
                    act.wait_ge(q_done, n)
                act.activation(sgm[:], bank[bank_of(b, 0)][:], ACT.Sigmoid, bias=col(V_BHQ, hd, q)).then_inc(q_sig, 1)
                act.wait_ge(bank_full[bank_of(b, 1)], used(b, q, per) + 1)
                if per or hd:
                    act.wait_ge(lft_full, n)
                act.activation(lf[:], bank[bank_of(b, 1)][:], ACT.Sigmoid, bias=col(V_BHF, hd, q)).then_inc(f_sig, 1)
                if per or hd >= 2:
                    act.wait_ge(kr_done, n - 1)
                bias = lbs[:, 2, hd:hd + 1] if not per else lbs[:, 2, bass.ds(hd + 2 * q, 1)]
                act.activation(hk[:, hd % 2], bank[bank_of(b, 1)][:], ACT.Sigmoid, bias=bias, scale=-1.0).then_inc(bank_free[bank_of(b, 1)], 1)
                split(b + 2, q, per)

            def head_gate(hd, q=0):
                per = 0 if isinstance(q, int) else 4
                n = count(hd, q, 2 if per else 0)
                b = b0 + 2 * hd + 1
                act.wait_ge(bank_full[bank_of(b, 1)], used(b, q, per) + 1)
                if per or hd >= 2:
                    act.wait_ge(yh_ready, n - 1)
                act.activation(hg[:, hd % 2], bank[bank_of(b, 1)][:], ACT.Sigmoid, bias=col(V_BHG, hd, q)).then_inc(bank_free[bank_of(b, 1)], 1)

            def head_log(hd, q=0):
                n = count(hd, q, 0 if isinstance(q, int) else 2)
                act.wait_ge(f_lin, n + 1)
                act.activation(lf[:], lf[:], ACT.Ln).then_inc(f_log, 1)

            def head_exps(hd, q=0):
                n = count(hd, q, 0 if isinstance(q, int) else 2)
                act.wait_ge(lft_full, n + 1)
                act.activation(lft[:].rearrange("p a n -> p (a n)"), bank[4][:], ACT.Copy).then_inc(lft_copied, 1)
                act.wait_ge(cum_full, n + 1)
                for e, (src, sgn) in enumerate(((5, 1.0), (5, -1.0), (6, 1.0), (7, 1.0))):
                    act.activation(ex[:, e], bank[src][:], ACT.Exp, scale=sgn).then_inc(ex_done, 1)

            def head_turned(hd, q=0):
                n = count(hd, q, 0 if isinstance(q, int) else 2)
                act.wait_ge(krt_full, n + 1)
                act.activation(krt[:].rearrange("p a n -> p (a n)"), bank[4][:], ACT.Copy).then_inc(krt_copied, 1)

            def head_norm(hd, q=0):
                n = count(hd, q, 0 if isinstance(q, int) else 2)
                act.wait_ge(oh_full, n + 1)
                act.activation(osq[:], bank[5][:], ACT.Square).then_inc(osq_ready, 1)
                act.wait_ge(osum_full, n + 1)
                act.activation(ort[:], bank[6][:], ACT.Sqrt, bias=eps_col).then_inc(oroot_ready, 1)

            def period(p, q=0):
                if p >= 2:
                    head_norm(p - 2, q)
                if p < HG_HEADS:
                    head_units(p, q)
                if 1 <= p <= HG_HEADS:
                    head_exps(p - 1, q)
                if p < HG_HEADS:
                    head_log(p, q)
                if 1 <= p <= HG_HEADS:
                    head_turned(p - 1, q)
                if p < HG_HEADS:
                    head_gate(p, q)

            act.wait_ge(o2_lo, KC)
            for half in range(2):
                act.wait_ge(bank_free[bank_of(FIRST["ga"] + 7, half)], used(FIRST["ga"] + 7) + 1)
            period(0)
            period(1)
            with act.Fori(0, 3) as q:
                period(2, q)
                period(3, q)
            period(8)
            period(9)

            for k in range(KC):
                act.wait_ge(yh_ready, max(k + 1, HG_HEADS))
                act.activation(ah[:, k, :], yh[:, k, :], ACT.Copy).then_inc(y_hi, 1)
            gates(FIRST["gb"], V_BGB)
            wait_block(act, FIRST["wout2"] - 1)
            for k in range(KC):
                act.wait_ge(merged_ready, k + 1)
                act.activation(uh[:, k, :], merged[:, k, :], ACT.Copy).then_inc(m_hi, 1)
            for j in range(4):
                split(FIRST["wout2"] + j + 1)
            norm("ffn", h, None, uh, wait=lambda k: h_wait(act, "ffn", k))

            b0 = FIRST["ffn"]

            def gate_units(j, n, q=0, per=0, n_per=0):
                for half in range(2):
                    b = b0 + j
                    bi = bank_of(b, half)
                    act.wait_ge(bank_full[bi], used(b, q, per) + 1)
                    act.wait_ge(gz_ready, SQ0 + (n + half - 1 + n_per * q if per else n + half - 1))
                    act.activation(gs[:, half], bank[bi][:], ACT.Sigmoid).then_inc(gs_ready, 1)

            with act.Fori(0, 2) as q:
                for j in range(12):
                    split(b0 + j + 1, q, 12)
                    if j < 8 and j % 2 == 0:
                        gate_units(j, j, q, 12, 8)
            for j in range(10):
                if j < 9:
                    split(b0 + 24 + j + 1)
                if j < 6 and j % 2 == 0:
                    gate_units(24 + j, 16 + j)
            norm("final", h, None, None, wait=lambda k: h_wait(act, "final", k))

        @block.gpsimd
        def _(pool):
            def split(b, q=0, per=0):
                pool.wait_ge(split_hi, count(b, q, per) + 1)
                pool.tensor_tensor(wl[:, b % 2], raw[:, b % RAW], f32(wh[:, b % 2]), ALU.subtract).then_inc(split_lo, 1)

            for b in range(9):
                split(b)
            pool.wait_ge(cw_ready, 2)
            pool.memset(tm[:], 0.0).then_inc(tm_zero, 1)
            pool.wait_ge(tm_zero, 1)
            pool.wait_ge(tab_in, 16 * 17)
            for i, (hp, q, e) in enumerate(ITEMS):
                if i >= 2:
                    pool.wait_ge(smax, i - 1)
                pool.tensor_tensor(tm[:, i % 2, 0:256].rearrange("p (j c) -> p j c", c=WIN),
                                   tab[:, ROWS * (2 * hp + e):ROWS * (2 * hp + e) + ROWS, TOFF[q]:TOFF[q] + WIN],
                                   mask[:, TMASK[q], :].rearrange("p (j c) -> p j c", c=WIN), ALU.add).then_inc(tm_ready, 1)
            for b in range(9, 13):
                split(b)
            with pool.Fori(0, 4) as q:
                for j in range(8):
                    split(FIRST["mlp0"] + j + 1, q, 8)
            for b in range(FIRST["pool"], FIRST["pool"] + 4):
                split(b + 1)
            with pool.Fori(0, 4) as q:
                for j in range(8):
                    split(FIRST["mlp1"] + j + 1, q, 8)
            for b in range(FIRST["aq"], FIRST["hgrn"]):
                split(b + 1)
            with pool.Fori(0, 4) as q:
                for j in range(4):
                    split(FIRST["hgrn"] + j + 1, q, 4)
            for b in range(FIRST["gb"], FIRST["ffn"]):
                split(b + 1)
            with pool.Fori(0, 2) as q:
                for j in range(12):
                    split(FIRST["ffn"] + j + 1, q, 12)
            for b in range(FIRST["ffn"] + 24, BLOCKS - 1):
                split(b + 1)

        @block.tensor
        def _(pe):
            def passes(out, ah_, al_, bh, bl, first, last):
                pe.matmul(out, ah_, bh, start=first, stop=False)
                pe.matmul(out, ah_, bl, start=False, stop=False)
                return pe.matmul(out, al_, bh, start=False, stop=last)

            def product(b, xh, xl, q=0, per=0, nk=KC, ready=None):
                pe.wait_ge(split_lo, count(b, q, per) + 1)
                for half in range(2):
                    bi = bank_of(b, half)
                    if per or b >= 2:
                        pe.wait_ge(bank_free[bi], used(b, q, per))
                    for k in range(nk):
                        if ready and not half:
                            ready(k)
                        w = slice(P * half, P * half + P)
                        last = passes(bank[bi][:], wh[:, b % 2, k, w], wl[:, b % 2, k, w], xh[:, k, :], xl[:, k, :], k == 0, k == nk - 1)
                    last.then_inc(bank_full[bi], 1)

            def product_by_token(b, first=0, nk=KC):
                pe.wait_ge(split_lo, b + 1)
                for half in range(2):
                    bi = bank_of(b, half)
                    if b >= 2:
                        pe.wait_ge(bank_free[bi], used(b))
                    for a in range(2):
                        tok = slice(P * (2 * half + a), P * (2 * half + a) + P)
                        for k in range(nk):
                            last = passes(bank[bi][:, BC * a:BC * a + BC], uh[:, first + k, tok], ul[:, first + k, tok], wh[:, b % 2, k, :], wl[:, b % 2, k, :], k == 0, k == nk - 1)
                    last.then_inc(bank_full[bi], 1)

            def norm_sum(name, n=S):
                i = NORM[name]
                for k in range(KC):
                    pe.wait_ge(sq_ready, 8 * i + k + 1)
                    pe.matmul(bank[6][:, 0:n], ones_d, sq[:, k % 2, 0:n], start=(k == 0), stop=(k == KC - 1)).then_inc(sq_used, 1)

            def mod_columns(m, q=0, per=0):
                pe.wait_ge(macc, 8 * (m + 1) + 8 * per * q if per else 8 * (m + 1))
                if per or m:
                    pe.wait_ge(mcol_used, count(m, q, per))
                for a in range(2):
                    last = pe.matmul(bank[7][:, a:a + 1], acc[:, m % 2, P * a:P * a + P], one_col, start=True, stop=True)
                last.then_inc(mcol_full, 1)

            pe.wait_ge(csil_ready, 1)
            for i in range(8):
                pe.wait_ge(modf_in[i], 16)
                for k in range(KC):
                    last = pe.matmul(bank[4 + i // 2][0:2, BC * (i % 2):BC * (i % 2) + BC], csil[:, k, :], modf[:, i, k, :], start=(k == 0), stop=(k == KC - 1))
                last.then_inc(modrow_full, 1)
            pe.wait_ge(const_in, 48)
            for j in range(16):
                if j % 4 == 0:
                    pe.wait_ge(modrow_copied, j // 4 + 1)
                last = pe.matmul(bank[0][:, 2 * j:2 * j + 2], modrow[0:2, P * j:P * j + P], ident[0:2, 0:2], start=True, stop=True)
            last.then_inc(mod0_full, 1)
            norm_sum("x")
            pe.wait_ge(root_ready, 1)
            norm_sum("ctx", L)

            def head_sum(i):
                pe.wait_ge(hsq_ready, i + 1)
                if i:
                    pe.wait_ge(hroot_ready, i)
                pe.matmul(bank[6][:], ones_h, sq[:, i % 2], start=True, stop=True).then_inc(hsum_full, 1)

            pe.wait_ge(ulo_ready, 16)
            for b in range(8):
                pe.wait_ge(split_lo, b + 1)
                if b < 2:
                    for a in range(2):
                        tok = slice(P * a, P * a + P)
                        for k in range(KC):
                            last = passes(bank[4 + b][:, BC * a:BC * a + BC], uch[:, k, tok], ucl[:, k, tok], wh[:, b % 2, k, :], wl[:, b % 2, k, :], k == 0, k == KC - 1)
                    last.then_inc(ctx_full, 1)
                    product_by_token(b)
                elif b < 4:
                    pe.wait_ge(ctx_free, b - 1)
                    for half in range(2):
                        w = slice(P * half, P * half + P)
                        for k in range(KC):
                            last = passes(bank[2 + b][:, L * half:L * half + L], wh[:, b % 2, k, w], wl[:, b % 2, k, w], uch[:, k, :], ucl[:, k, :], k == 0, k == KC - 1)
                    last.then_inc(ctx_full, 1)
                    product(b, uh, ul)
                else:
                    product(b, uh, ul)
                for m in range(mods_before[b], mods_before[b + 1]):
                    mod_columns(m)
                for i in HN_OF.get(b - 1, []):
                    head_sum(i)

            pe.wait_ge(w4_in, 32)
            pe.wait_ge(ctx_free, 4)
            for g in range(FG):
                for a in range(2):
                    last = pe.matmul(bank[4 + g // 2][:, 2 * P * (g % 2) + P * a:2 * P * (g % 2) + P * a + P], cs[:, P * a:P * a + P], w4[:, g, :], start=True, stop=True)
                if g % 2:
                    last.then_inc(cw_full, 1)

            def fourier_y(g):
                if g == 0:
                    pe.wait_ge(bank_free[bank_of(7, 0)], used(7) + 1)
                    pe.wait_ge(bank_free[bank_of(7, 1)], used(7) + 1)
                    pe.wait_ge(cw_ready, 2)
                    pe.wait_ge(hroot_ready, 10)
                    pe.wait_ge(mcol_used, MOD0)
                for i in range(4):
                    if i % 2 == 0 and g:
                        pe.wait_ge(y_ready, 2 * g - 1 + i // 2)
                    last = pe.matmul(bank[6 + i // 2][:, 2 * P * (i % 2):2 * P * (i % 2) + 2 * P], fT[:, g, P * i:P * i + P], cw[:, g, :], start=True, stop=True)
                    if i % 2:
                        last.then_inc(y_full, 1)

            def fourier_out(g):
                if g == 0:
                    pe.wait_ge(dft_in, 32)
                if g >= 2:
                    pe.wait_ge(four_lo, g - 1)
                pe.wait_ge(y_ready, 2 * g + 2)
                for i in range(4):
                    pe.matmul(bank[4 + g % 2][:], ysb[:, i, 0:P], dftc[:, i, :], start=(i == 0), stop=False)
                    last = pe.matmul(bank[4 + g % 2][:], ysb[:, i, P:2 * P], dfts[:, i, :], start=False, stop=(i == 3))
                last.then_inc(four_full, 1)

            for g in range(FG):
                fourier_y(g)
                fourier_out(g)

            def scores(i):
                hp, w, e = ITEMS[i]
                r = slice(64 * e, 64 * e + 64)
                if i < 2:
                    pe.wait_ge(four_lo, 3 + i)
                    for n in range(len(HN)):
                        hn_wait_done(pe, n)
                else:
                    pe.wait_ge(smax, i - 1)
                qv = qT[r, hp, P * w:P * w + P]
                pe.matmul(bank[4 + i % 2][:, 0:256], qv, by_column(kT[r, hp, :], W0[w], WIN), start=True, stop=True)
                pe.matmul(bank[4 + i % 2][:, 256:512], qv, kcT[r, hp, :], start=True, stop=True).then_inc(s_full, 1)

            def turn(i):
                pe.wait_ge(p_norm, i + 1)
                if i < 2:
                    pe.wait_ge(y_ready, 8)
                else:
                    pe.wait_ge(pt_copied, i - 1)
                for c in range(4):
                    last = pe.transpose(bank[6 + i % 2][:, P * c:P * c + P], pn[:, i % 2, P * c:P * c + P], ident)
                last.then_inc(pt_full, 1)

            def values(i):
                hp, w, e = ITEMS[i]
                hd = slice(64 * (2 * hp + e), 64 * (2 * hp + e) + 64)
                if i == 0:
                    pe.wait_ge(vwin_in, 16 * 32)
                if i % 8 == 0 and hp >= 2:
                    pe.wait_ge(o_lo, hp - 1)
                pe.wait_ge(pt_copied, i + 1)
                for c in range(4):
                    v = vwin[:, 2 * w + c, hd] if c < 2 else vc[:, c - 2, hd]
                    last = pe.matmul(bank[2 + hp % 2][64 * e:64 * e + 64, P * w:P * w + P], v, pT[:, i % 2, P * c:P * c + P], start=(c == 0), stop=(c == 3))
                last.then_inc(o_full, 1)

            for i in range(len(ITEMS) + 2):
                if i < len(ITEMS):
                    scores(i)
                if 1 <= i <= len(ITEMS):
                    turn(i - 1)
                if i >= 2:
                    values(i - 2)
            pe.wait_ge(o_lo, 4)
            for b in range(8, 12):
                product(b, uh, ul)

            def mlp(layer):
                b0, i = FIRST[f"mlp{layer}"], NORM[f"mlp{layer}"]
                pe.wait_ge(ulo_ready, 8 * i + 8)
                with pe.Fori(0, 4) as q:
                    for j in range(8):
                        if j < 4:
                            product(b0 + j, uh, ul, q, 8)
                        else:
                            product(b0 + j, ah, al, q, 8,
                                    ready=(lambda k: pe.wait_ge(a_lo, SQ0 + 32 * layer + k + 1 + 8 * q)) if j == 4 else None)
                        if layer == 0 and j < 6:
                            mod_columns(MOD0 + j, q, 6)

            norm_sum("mlp0")
            mlp(0)

            norm_sum("pool")
            b0 = FIRST["pool"]
            pe.wait_ge(ulo_ready, 8 * NORM["pool"] + 8)
            for g in range(FG):
                product_by_token(b0 + g, first=2 * g, nk=2)
            pe.wait_ge(band_in, 16)
            for m in range(KC):
                g = m // 2
                if m % 2 == 0:
                    for half in range(2):
                        bi = bank_of(b0 + g, half)
                        pe.wait_ge(bank_free[bi], used(b0 + g) + 1)
                if m >= 2:
                    pe.wait_ge(yp_free, m - 1)
                w = slice(P * (m % 2), P * (m % 2) + P)
                for i in range(4):
                    lo, hi = max(0, P * i - 8), min(S, P * i + P + 8)
                    kind = 0 if i == 0 else 2 if i == 3 else 1
                    r = lo - (P * i - 8)
                    last = pe.matmul(bank[4 + m % 2][:, lo:hi], zt[:, g, i, w], band[:, kind, g, r:r + hi - lo],
                                     start=(i == 0), stop=(i == 3), skip_group_check=True)
                last.then_inc(yp_full, 1)
            norm_sum("mlp1")
            mlp(1)

            norm_sum("mix2")
            pe.wait_ge(ulo_ready, 8 * NORM["mix2"] + 8)
            b0 = FIRST["aq"]
            for j in range(4):
                product(b0 + j, uh, ul)

            def half_and_half(b, first_by_token, q=0, per=0):
                pe.wait_ge(split_lo, count(b, q, per) + 1)
                for half in range(2):
                    bi = bank_of(b, half)
                    w = slice(P * half, P * half + P)
                    pe.wait_ge(bank_free[bi], used(b, q, per))
                    if half == (0 if first_by_token else 1):
                        for a in range(4):
                            tok = slice(P * a, P * a + P)
                            for k in range(KC):
                                last = passes(bank[bi][:, P * a:P * a + P], uh[:, k, tok], ul[:, k, tok], wh[:, b % 2, k, w], wl[:, b % 2, k, w], k == 0, k == KC - 1)
                    else:
                        for k in range(KC):
                            last = passes(bank[bi][:], wh[:, b % 2, k, w], wl[:, b % 2, k, w], uh[:, k, :], ul[:, k, :], k == 0, k == KC - 1)
                    last.then_inc(bank_full[bi], 1)

            half_and_half(b0 + 4, False)

            def scores2(i):
                c, n = ITEMS2[i]
                if i == 0:
                    for b in range(b0, b0 + 5):
                        for half in range(2):
                            pe.wait_ge(bank_free[bank_of(b, half)], used(b) + 1)
                if i >= 2:
                    pe.wait_ge(smax2, 2 * (i - 1))
                ks = P * max(0, n - 1)
                for e in range(2):
                    r = slice(64 * e, 64 * e + 64)
                    last = pe.matmul(bank[S2_BANKS[i % 2][e]][:, 0:256], aqT[r, c, P * n:P * n + P], akT[r, ks:ks + 256], start=True, stop=True)
                last.then_inc(s2_full, 1)

            def turn2(i):
                pe.wait_ge(p2_norm, 2 * (i + 1))
                if i >= 2:
                    pe.wait_ge(pt2_copied, i - 1)
                for c in range(4):
                    last = pe.transpose(bank[6 + i % 2][:, P * c:P * c + P], pn2[:, i % 2, P * c:P * c + P], ident)
                last.then_inc(pt2_full, 1)

            def values2(i):
                c, n = ITEMS2[i]
                if n == 0 and c >= 2:
                    pe.wait_ge(o2_lo, c - 1)
                pe.wait_ge(pt2_copied, i + 1)
                for e in range(2):
                    for a in range(2):
                        last = pe.matmul(bank[2 + c % 2][64 * e:64 * e + 64, P * n:P * n + P], av[:, max(0, n - 1) + a, 64 * e:64 * e + 64],
                                         pT2[:, i % 2, P * (2 * e + a):P * (2 * e + a) + P], start=(a == 0), stop=(a == 1))
                last.then_inc(o2_full, 1)

            for i in range(len(ITEMS2) + 2):
                if i < len(ITEMS2):
                    scores2(i)
                if 1 <= i <= len(ITEMS2):
                    turn2(i - 1)
                if i >= 2:
                    values2(i - 2)
            pe.wait_ge(o2_lo, KC)
            for j in range(8):
                if j % 2 == 0:
                    product(FIRST["ga"] + j, uh, ul)
                else:
                    product(FIRST["ga"] + j, ah, al)

            b0 = FIRST["hgrn"]

            def n_of(hd, q):
                return count(hd, q, 0 if isinstance(q, int) else 2)

            def turn_log(hd, q=0):
                n = n_of(hd, q)
                pe.wait_ge(f_log, n + 1)
                if not isinstance(q, int) or hd:
                    pe.wait_ge(krt_copied, n)
                for a in range(4):
                    last = pe.transpose(bank[4][:, P * a:P * a + P], lf[:, P * a:P * a + P], ident)
                last.then_inc(lft_full, 1)

            def sums(hd, q=0):
                n = n_of(hd, q)
                pe.wait_ge(lft_copied, n + 1)
                if not isinstance(q, int) or hd:
                    pe.wait_ge(on_ready, 2 * n)
                    pe.wait_ge(st_done, 8 * n)
                for e in range(3):
                    for a in range(4):
                        last = pe.matmul(bank[5 + e][:, P * a:P * a + P], lft[:, a, :], cm[:, e, :], start=True, stop=True)
                last.then_inc(cum_full, 1)

            def attend(hd, q=0):
                n = n_of(hd, q)
                pe.wait_ge(qd_done, n + 1)
                pe.wait_ge(kd_done, n + 1)
                pe.wait_ge(ex_done, 4 * n + 4)
                for a in range(4):
                    w = slice(P * a, P * a + P)
                    last = pe.matmul(bank[5][:, w], ex[:, 1, w], ex[:, 0, w], start=True, stop=True)
                last.then_inc(att_full, 1)
                pe.wait_ge(kr_done, n + 1)
                for a in range(4):
                    last = pe.transpose(bank[4][:, P * a:P * a + P], ex[:, 3, P * a:P * a + P], ident)
                last.then_inc(krt_full, 1)

            def updates(hd, q=0):
                n = n_of(hd, q)
                pe.wait_ge(krt_copied, n + 1)
                pe.wait_ge(v_done, n + 1)
                for j in range(8):
                    r = slice(64 * (j % 2), 64 * (j % 2) + 64)
                    last = pe.matmul(bank[6 + j % 2][:, P * (j // 2):P * (j // 2) + P], krt[r, j // 2, :], hv[r, hd % 2, j // 2, :], start=True, stop=True)
                last.then_inc(upd_full, 1)

            def outputs(hd, q=0):
                n = n_of(hd, q)
                pe.wait_ge(att_done, n + 1)
                pe.wait_ge(qb_done, n + 1)
                pe.wait_ge(st_done, 8 * n + 8)
                for a in range(4):
                    w = slice(P * a, P * a + P)
                    pe.matmul(bank[5][:, w], hv[:, hd % 2, a, :], att[:, w], start=True, stop=False)
                    for j in (2 * a, 2 * a + 1):
                        c = slice(64 * j, 64 * j + 64)
                        last = pe.matmul(bank[5][:, c], st[:, j, :], qb[:, c], start=False, stop=(j % 2 == 1))
                last.then_inc(oh_full, 1)

            def out_sum(hd, q=0):
                n = n_of(hd, q)
                pe.wait_ge(osq_ready, n + 1)
                pe.matmul(bank[6][:], ones_v, osq[:], start=True, stop=True).then_inc(osum_full, 1)

            def period(p, q=0):
                per = 0 if isinstance(q, int) else 4
                b = b0 + 2 * p
                if p >= 2:
                    outputs(p - 2, q)
                if p < HG_HEADS:
                    unit(b, 0, q, per)
                if p >= 2:
                    out_sum(p - 2, q)
                if 1 <= p <= HG_HEADS:
                    turn_log(p - 1, q)
                if p < HG_HEADS:
                    unit(b, 1, q, per)
                if 1 <= p <= HG_HEADS:
                    sums(p - 1, q)
                if p < HG_HEADS:
                    unit(b + 1, 0, q, per, by_token=True)
                if 1 <= p <= HG_HEADS:
                    attend(p - 1, q)
                if p < HG_HEADS:
                    unit(b + 1, 1, q, per)
                if 1 <= p <= HG_HEADS:
                    updates(p - 1, q)

            def unit(b, half, q=0, per=0, by_token=False):
                if half == 0:
                    pe.wait_ge(split_lo, count(b, q, per) + 1)
                bi = bank_of(b, half)
                w = slice(P * half, P * half + P)
                pe.wait_ge(bank_free[bi], used(b, q, per))
                if by_token:
                    for a in range(4):
                        tok = slice(P * a, P * a + P)
                        for k in range(KC):
                            last = passes(bank[bi][:, P * a:P * a + P], uh[:, k, tok], ul[:, k, tok], wh[:, b % 2, k, w], wl[:, b % 2, k, w], k == 0, k == KC - 1)
                else:
                    for k in range(KC):
                        last = passes(bank[bi][:], wh[:, b % 2, k, w], wl[:, b % 2, k, w], uh[:, k, :], ul[:, k, :], k == 0, k == KC - 1)
                last.then_inc(bank_full[bi], 1)

            pe.wait_ge(hg_in, 48)
            period(0)
            period(1)
            with pe.Fori(0, 3) as q:
                period(2, q)
                period(3, q)
            period(8)
            period(9)
            for j in range(8):
                if j % 2 == 0:
                    product(FIRST["gb"] + j, uh, ul)
                else:
                    product(FIRST["gb"] + j, ah, al, ready=(lambda k: pe.wait_ge(y_lo, k + 1)) if j == 1 else None)
            for j in range(4):
                product(FIRST["wout2"] + j, uh, ul, ready=(lambda k: pe.wait_ge(m_lo, k + 1)) if j == 0 else None)
            norm_sum("ffn")
            pe.wait_ge(ulo_ready, 8 * NORM["ffn"] + 8)
            b0 = FIRST["ffn"]
            with pe.Fori(0, 2) as q:
                for j in range(12):
                    if j < 8:
                        product(b0 + j, uh, ul, q, 12)
                    else:
                        product(b0 + j, ah, al, q, 12, ready=(lambda k: pe.wait_ge(z_lo, k + 1 + 8 * q)) if j == 8 else None)
            for j in range(10):
                if j < 6:
                    product(b0 + 24 + j, uh, ul)
                else:
                    product(b0 + 24 + j, ah, al, nk=6, ready=(lambda k: pe.wait_ge(z_lo, 16 + k + 1)) if j == 6 else None)
            norm_sum("final")

        @block.vector
        def _(dve):
            def norm(name, src, gain, shift, hi, lo, n=S):
                i = NORM[name]
                dve.wait_ge(root_ready, i + 1)
                dve.reciprocal(rstd[:, 0:n], rstd[:, 0:n]).then_inc(rstd_ready, 1)
                dve.wait_ge(rstd_ready, i + 1)

                def scaled(k):
                    if k >= 2:
                        dve.wait_ge(ulo_ready, 8 * i + k - 1)
                    dve.scalar_tensor_tensor(tt[:, k % 2, 0:n], src[:, k, :], gain(k), rstd[:, 0:n], ALU.mult, ALU.mult).then_inc(t_ready, 1)

                def low(k):
                    dve.wait_ge(uhi_ready, 8 * i + k + 1)
                    if shift is None:
                        ins = dve.tensor_tensor(lo[:, k, :], tt[:, k % 2, 0:n], f32(hi[:, k, :]), ALU.subtract)
                    else:
                        ins = dve.scalar_tensor_tensor(lo[:, k, :], tt[:, k % 2, 0:n], shift(k), f32(hi[:, k, :]), ALU.add, ALU.subtract)
                    ins.then_inc(ulo_ready, 1)

                for k in range(KC + 1):
                    if k < KC:
                        scaled(k)
                    if k:
                        low(k - 1)

            def gain_of(n, scale, g):
                dve.scalar_tensor_tensor(gm[:, n, :], scale, 1.0, g, ALU.add, ALU.mult).then_inc(gain_ready, 1)
                dve.wait_ge(gain_ready, n + 1)

            def mod_sum(m, q=0, per=0):
                n = 8 * (m + 0) + 8 * per * q if per else 8 * m
                dve.wait_ge(mraw_full[m % 2], 16 * (m // 2 + 1) + 8 * per * q if per else 16 * (m // 2 + 1))
                if per or m >= 2:
                    dve.wait_ge(mcol_full, count(m - 1, q, per))
                dve.tensor_scalar(acc[:, m % 2], mraw[:, m % 2, 0], csil[:, 0, 0:1], None, ALU.mult).then_inc(macc, 1)
                for k in range(1, KC):
                    dve.wait_ge(macc, n + k)
                    dve.scalar_tensor_tensor(acc[:, m % 2], mraw[:, m % 2, k], csil[:, k, 0:1], acc[:, m % 2], ALU.mult, ALU.add).then_inc(macc, 1)

            def mod_store(m, q=0, per=0):
                dve.wait_ge(mcol_full, count(m + 1, q, per))
                c = 16 + 2 * m
                if per:
                    c = c + 2 * per * q
                    out, b = modc[:, bass.ds(c, 2)], bmod[:, bass.ds(c, 2)]
                else:
                    out, b = modc[:, c:c + 2], bmod[:, c:c + 2]
                dve.tensor_tensor(out, bank[7][:, 0:2], b, ALU.add).then_inc(mcol_used, 1)

            for i in range(4):
                dve.wait_ge(modrow_full, 2 * i + 2)
                dve.tensor_copy(modrow[0:2, S * i:S * i + S], bank[4 + i][0:2, :]).then_inc(modrow_copied, 1)
            dve.wait_ge(const_in, 48)
            dve.wait_ge(mod0_full, 1)
            both = bank[0][:, 0:32].rearrange("p (j a) -> p j a", a=2)
            dve.tensor_tensor(modc[:, 0:16], both[:, :, 0], bmod[:, 0:16], ALU.add).then_inc(mod0_ready, 1)
            dve.tensor_tensor(modx[:, :], both[:, :, 1], bmod[:, 0:16], ALU.add).then_inc(mod0_ready, 1)
            dve.wait_ge(mod0_ready, 2)
            gain_of(0, modc[:, 8:16], vec[:, V_G1:V_G1 + 8])
            gain_of(1, modx[:, 8:16], vec[:, V_G1:V_G1 + 8])
            norm("x", h, lambda k: gm[:, 0, k:k + 1], lambda k: mod(0, 0, k), uh, ul)
            norm("ctx", ctxT, lambda k: gm[:, 1, k:k + 1], lambda k: modx[:, k:k + 1], uch, ucl, L)

            def hn_scale(i):
                src, free, out = hn_place(i)
                dve.wait_ge(hroot_ready, i + 1)
                dve.reciprocal(tt[:, i % 2], tt[:, i % 2]).then_inc(hrstd_ready, 1)
                dve.wait_ge(hrstd_ready, i + 1)
                if HN[i][0] != "q":
                    dve.scalar_tensor_tensor(out, src, vec[:, V_KG:V_KG + 1], tt[:, i % 2], ALU.mult, ALU.mult).then_inc(free, 1)
                    return
                for w in range(QT):
                    last = dve.scalar_tensor_tensor(out[:, P * w:P * w + P].rearrange("p (r c) -> p r c", c=QC), by_column(src, QC * w, QC),
                                                    vec[:, V_QG:V_QG + 1], by_column(tt[:, i % 2], QC * w, QC), ALU.mult, ALU.mult)
                last.then_inc(free, 1)

            for b in range(8):
                for m in range(mods_before[b], mods_before[b + 1]):
                    mod_sum(m)
                    if m > mods_before[b]:
                        mod_store(m - 1)
                mod_store(mods_before[b + 1] - 1)
                for i in HN_OF.get(b - 1, []):
                    hn_scale(i)
            gain_of(2, modc[:, 32:40], vec[:, V_G2:V_G2 + 8])
            for a in range(2):
                dve.wait_ge(cw_full, a + 1)
                dve.tensor_copy(cw[:, 2 * a:2 * a + 2, :].rearrange("p a n -> p (a n)"), bank[4 + a][:]).then_inc(cw_ready, 1)
            for g in range(FG):
                dve.wait_ge(four_hi, g + 1)
                dve.tensor_tensor(ul[:, g, :], bank[4 + g % 2][:], f32(uh[:, g, :]), ALU.subtract).then_inc(four_lo, 1)

            def row_max(i):
                dve.wait_ge(s_full, i + 1)
                dve.wait_ge(tm_ready, i + 1)
                if i < 2:
                    dve.wait_ge(four_full, 4)
                else:
                    dve.wait_ge(p_norm, i - 1)
                dve.tensor_tensor_reduce(sc[:, i % 2], bank[4 + i % 2][:], tm[:, i % 2], 1.0, -3e38, ALU.add, ALU.max, stat[:, 0, i % 2:i % 2 + 1]).then_inc(smax, 1)
                dve.wait_ge(smax, i + 1)
                dve.tensor_scalar(stat[:, 1, i % 2:i % 2 + 1], stat[:, 0, i % 2:i % 2 + 1], -1.0, None, ALU.mult).then_inc(nmax, 1)

            def normalise(i):
                dve.wait_ge(p_exp, i + 1)
                dve.reciprocal(stat[:, 3, i % 2:i % 2 + 1], stat[:, 2, i % 2:i % 2 + 1]).then_inc(p_recip, 1)
                dve.wait_ge(p_recip, i + 1)
                if i >= 2:
                    dve.wait_ge(pt_full, i - 1)
                dve.tensor_scalar(pn[:, i % 2], sc[:, i % 2], stat[:, 3, i % 2:i % 2 + 1], None, ALU.mult).then_inc(p_norm, 1)

            def o_low(hp):
                dve.wait_ge(o_hi, hp + 1)
                for w in range(QT):
                    out = by_column(ul[:, 4 + hp, :], QC * w, QC)
                    src = bank[2 + hp % 2][:, P * w:P * w + P].rearrange("p (r c) -> p r c", c=QC)
                    last = dve.tensor_tensor(out, src, by_column(f32(uh[:, 4 + hp, :]), QC * w, QC), ALU.subtract)
                last.then_inc(o_lo, 1)

            for i in range(len(ITEMS) + 1):
                if i < len(ITEMS):
                    row_max(i)
                if i >= 1:
                    normalise(i - 1)
                if i >= 8 and i % 8 == 3:
                    o_low(i // 8 - 1)
            o_low(3)

            def add_to_h(b, m, gate, q=0, per=0):
                bi = bank_of(b, m % 2)
                dve.wait_ge(bank_full[bi], used(b, q, per) + 1)
                if gate is None:
                    ins = dve.tensor_tensor(h[:, m, :], bank[bi][:], h[:, m, :], ALU.add)
                else:
                    ins = dve.scalar_tensor_tensor(h[:, m, :], bank[bi][:], gate, h[:, m, :], ALU.mult, ALU.add)
                ins.then_inc(bank_free[bi], 1)

            for b in range(8, 12):
                for half in range(2):
                    add_to_h(b, 2 * (b - 8) + half, mod(0, 2, 2 * (b - 8) + half), 0)

            def mlp(layer):
                b0, n0 = FIRST[f"mlp{layer}"], 32 * layer
                with dve.Fori(0, 4) as q:
                    for j in range(8):
                        if layer == 0 and j < 6:
                            mod_sum(MOD0 + j, q, 6)
                        for half in range(2):
                            m = 2 * (j % 4) + half
                            if j >= 4:
                                add_to_h(b0 + j, m, mod(layer, 5, m), q, 8)
                                continue
                            bi = bank_of(b0 + j, half)
                            dve.wait_ge(bank_free[bi], used(b0 + j, q, 8) + 1)
                            dve.wait_ge(a_lo, SQ0 + n0 + m - 1 + 8 * q)
                            dve.tensor_tensor(v1[:, m % 2], r1[:, m % 2], r1[:, m % 2], ALU.mult).then_inc(square_ready, 1)
                            dve.wait_ge(square_ready, SQ0 + n0 + m + 1 + 8 * q)
                            dve.tensor_copy(ah[:, m], v1[:, m % 2]).then_inc(a_hi, 1)
                            dve.wait_ge(a_hi, n0 + m + 1 + 8 * q)
                            dve.tensor_tensor(al[:, m], v1[:, m % 2], f32(ah[:, m]), ALU.subtract).then_inc(a_lo, 1)
                        if layer == 0 and j < 6:
                            mod_store(MOD0 + j, q, 6)

            norm("mlp0", h, lambda k: gm[:, 2, k:k + 1], lambda k: mod(0, 3, k), uh, ul)
            dve.memset(stat[:, 4, 0:1], 0.0).then_inc(square_ready, SQ0)
            dve.memset(stat[:, 4, 1:2], 0.0).then_inc(a_lo, SQ0)
            mlp(0)

            gain_of(3, modc[:, 56:64], vec[:, V_G1 + 8:V_G1 + 16])
            gain_of(4, modc[:, 80:88], vec[:, V_G2 + 8:V_G2 + 16])
            dve.tensor_tensor(gm[:, 5, :], modc[:, 64:72], vec[:, V_PS:V_PS + 8], ALU.mult).then_inc(gain_ready, 1)
            norm("pool", h, lambda k: gm[:, 3, k:k + 1], lambda k: mod(1, 0, k), uh, ul)
            dve.wait_ge(gain_ready, 6)
            for m in range(KC):
                dve.wait_ge(yp_full, m + 1)
                dve.scalar_tensor_tensor(h[:, m, :], bank[4 + m % 2][:], gm[:, 5, m:m + 1], h[:, m, :], ALU.mult, ALU.add).then_inc(yp_free, 1)
            norm("mlp1", h, lambda k: gm[:, 4, k:k + 1], lambda k: mod(1, 3, k), uh, ul)
            mlp(1)

            dve.tensor_tensor(lbs[:, 0, :], vec[:, V_LB:V_LB + 8], vec[:, V_LB + 8:V_LB + 16], ALU.subtract).then_inc(lb_ready, 1)
            dve.tensor_scalar(lbs[:, 2, :], vec[:, V_BHF:V_BHF + 8], -1.0, None, ALU.mult).then_inc(lb_ready, 0 + 1)
            norm("mix2", h, lambda k: vec[:, V_MIX + k:V_MIX + k + 1], None, uh, ul)
            dve.wait_ge(lb_ready, 3)
            dve.tensor_scalar(lbs[:, 1, :], lbs[:, 0, :], -1.0, 1.0, ALU.mult, ALU.add).then_inc(lb_ready, 1)
            b = FIRST["aq"] + 4
            dve.wait_ge(b2_in, 32)
            dve.wait_ge(bank_full[bank_of(b, 1)], used(b) + 1)
            dve.tensor_tensor(av[:], bank[bank_of(b, 1)][:].rearrange("p (a n) -> p a n", a=4),
                              bvrow[:].rearrange("p (a n) -> p a n", a=1).to_broadcast([P, 4, P]), ALU.add).then_inc(bank_free[bank_of(b, 1)], 1)
            sinks = vec[:, V_SINK:V_SINK + 16].rearrange("p (e c) -> p c e", e=2)

            def row_max2(i):
                c, n = ITEMS2[i]
                dve.wait_ge(s2_full, i + 1)
                if i >= 2:
                    dve.wait_ge(p2_norm, 2 * (i - 1))
                if i >= 1:
                    dve.wait_ge(p2_exp, 3 * i)
                    dve.wait_ge(p2_recip, i)
                for e in range(2):
                    w = slice(256 * e, 256 * e + 256)
                    dve.tensor_tensor_reduce(sc2[:, i % 2, w], bank[S2_BANKS[i % 2][e]][:, 0:256], wmask[:, min(n, 1), :], DH ** -0.5, sinks[:, c, e:e + 1],
                                             ALU.add, ALU.max, stat[:, 3, e:e + 1]).then_inc(smax2, 1)
                dve.wait_ge(smax2, 2 * i + 2)
                dve.tensor_scalar(stat[:, 4, :], stat[:, 3, :], -1.0, None, ALU.mult).then_inc(nmax2, 1)
                dve.wait_ge(nmax2, i + 1)
                dve.tensor_tensor(stat[:, 5, :], stat[:, 4, :], sinks[:, c, :], ALU.add).then_inc(sink_ready, 1)

            def total2(i):
                dve.wait_ge(p2_exp, 3 * i + 3)
                dve.tensor_tensor(stat[:, 8, :], stat[:, 7, :], stat[:, 6, :], ALU.add).then_inc(tot2, 1)
                dve.wait_ge(tot2, i + 1)
                dve.reciprocal(stat[:, 9, :], stat[:, 8, :]).then_inc(p2_recip, 1)
                dve.wait_ge(p2_recip, i + 1)
                if i >= 2:
                    dve.wait_ge(pt2_full, i - 1)
                for e in range(2):
                    w = slice(256 * e, 256 * e + 256)
                    dve.tensor_scalar(pn2[:, i % 2, w], sc2[:, i % 2, w], stat[:, 9, e:e + 1], None, ALU.mult).then_inc(p2_norm, 1)

            def o2_low(c):
                dve.wait_ge(o2_hi, c + 1)
                dve.tensor_tensor(al[:, c, :], bank[2 + c % 2][:], f32(ah[:, c, :]), ALU.subtract).then_inc(o2_lo, 1)

            for i in range(len(ITEMS2)):
                row_max2(i)
                total2(i)
                if i >= 4 and i % 4 == 3:
                    o2_low(i // 4 - 1)
            o2_low(KC - 1)

            def branches(first, second):
                for j in range(1, 8, 2):
                    for half in range(2):
                        b, m = first + j, j - 1 + half
                        bi = bank_of(b, half)
                        dve.wait_ge(bank_full[bi], used(b) + 1)
                        dve.wait_ge(bank_free[bank_of(b - 1, half)], used(b - 1) + 1)
                        out = mt[:, half] if second else merged[:, m, :]
                        if second and m >= 2:
                            dve.wait_ge(merged_ready, m - 1)
                        dve.tensor_tensor(out, bank[bi][:], sg[:, half], ALU.mult).then_inc(bank_free[bi], 1)
                        if second:
                            dve.wait_ge(bank_free[bi], used(b) + 1)
                            dve.tensor_tensor(merged[:, m, :], merged[:, m, :], mt[:, half], ALU.add).then_inc(merged_ready, 1)

            branches(FIRST["ga"], False)

            b0 = FIRST["hgrn"]

            def n_of(hd, q):
                return count(hd, q, 0 if isinstance(q, int) else 2)

            def column(x, first, hd, q):
                return x[:, first + hd:first + hd + 1] if isinstance(q, int) else x[:, bass.ds(first + hd + 2 * q, 1)]

            def head_inputs(hd, q=0):
                n, per, b = n_of(hd, q), (0 if isinstance(q, int) else 4), b0 + 2 * hd
                dve.wait_ge(q_sig, n + 1)
                if per or hd >= 2:
                    dve.wait_ge(qb_done, n - 1)
                dve.scalar_tensor_tensor(hq[:, hd % 2], bank[bank_of(b, 0)][:], column(vec, V_BHQ, hd, q), sgm[:], ALU.add, ALU.mult).then_inc(q_done, 1)
                dve.wait_ge(q_done, n + 1)
                dve.tensor_copy(stat[:, 0, 0:1], hq[:, hd % 2, 0:1]).then_inc(bank_free[bank_of(b, 0)], 1)
                dve.wait_ge(f_sig, n + 1)
                dve.tensor_scalar(lf[:], lf[:], column(lbs[:, 1, :], 0, hd, q), column(lbs[:, 0, :], 0, hd, q), ALU.mult, ALU.add).then_inc(f_lin, 1)
                dve.wait_ge(bank_free[bank_of(b, 1)], used(b, q, per) + 1)
                dve.tensor_scalar(hk[:, hd % 2], hk[:, hd % 2], column(lbs[:, 1, :], 0, hd, q), None, ALU.mult).then_inc(k_done, 1)

            def head_values(hd, q=0):
                n, per, b = n_of(hd, q), (0 if isinstance(q, int) else 4), b0 + 2 * hd + 1
                bi = bank_of(b, 0)
                dve.wait_ge(bank_full[bi], used(b, q, per) + 1)
                if per or hd >= 2:
                    dve.wait_ge(oh_full, n - 1)
                row = bhrow[:, hd:hd + 1, :] if not per else bhrow[:, bass.ds(hd + 2 * q, 1), :]
                dve.tensor_tensor(hv[:, hd % 2], bank[bi][:].rearrange("p (a n) -> p a n", a=4), row.to_broadcast([P, 4, P]), ALU.add).then_inc(v_done, 1)
                dve.wait_ge(v_done, n + 1)
                dve.tensor_copy(stat[:, 0, 1:2], hv[:, hd % 2, 0, 0:1]).then_inc(bank_free[bi], 1)

            def head_decay(hd, q=0):
                n, s = n_of(hd, q), hd % 2
                dve.wait_ge(k_done, n + 1)
                dve.wait_ge(ex_done, 4 * n + 2)
                dve.tensor_tensor(ex[:, 0], hq[:, s], ex[:, 0], ALU.mult).then_inc(qd_done, 1)
                dve.tensor_tensor(ex[:, 1], hk[:, s], ex[:, 1], ALU.mult).then_inc(kd_done, 1)
                dve.wait_ge(ex_done, 4 * n + 4)
                dve.tensor_tensor(ex[:, 3], hk[:, s], ex[:, 3], ALU.mult).then_inc(kr_done, 1)
                if not isinstance(q, int) or hd:
                    dve.wait_ge(oh_full, n)
                dve.tensor_tensor(qb[:], hq[:, s], ex[:, 2], ALU.mult).then_inc(qb_done, 1)

            def head_mask(hd, q=0):
                n = n_of(hd, q)
                dve.wait_ge(att_full, n + 1)
                dve.tensor_copy(stat[:, 0, 0:1], bank[5][:, 0:1])
                dve.copy_predicated(att[:], cmask[:], bank[5][:]).then_inc(att_done, 1)

            def head_states(hd, q=0):
                n = n_of(hd, q)
                dve.wait_ge(upd_full, n + 1)
                dve.tensor_copy(st[:, 1, :], bank[6][:, 0:P]).then_inc(st_done, 1)
                for j in range(1, 7):
                    dve.wait_ge(st_done, 8 * n + j)
                    dve.scalar_tensor_tensor(st[:, j + 1, :], st[:, j, :], ex[:, 2, 64 * j + 63:64 * j + 64], bank[6 + j % 2][:, P * (j // 2):P * (j // 2) + P],
                                             ALU.mult, ALU.add).then_inc(st_done, 1)
                dve.memset(stat[:, 1, 0:1], 0.0).then_inc(st_done, 1)

            def head_out(hd, q=0):
                n = n_of(hd, q)
                dve.wait_ge(oroot_ready, n + 1)
                dve.reciprocal(ort[:], ort[:]).then_inc(orstd_ready, 1)
                dve.wait_ge(orstd_ready, n + 1)
                dve.scalar_tensor_tensor(onum[:], bank[5][:], column(vec, V_HG, hd, q), ort[:], ALU.mult, ALU.mult).then_inc(on_ready, 1)
                dve.wait_ge(on_ready, 2 * n + 1)
                dve.wait_ge(bank_free[bank_of(b0 + 2 * hd + 1, 1)], used(b0 + 2 * hd + 1, q, 0 if isinstance(q, int) else 4) + 1)
                out = yh[:, hd, :] if isinstance(q, int) else yh[:, bass.ds(hd + 2 * q, 1), :].rearrange("p a n -> p (a n)")
                dve.tensor_tensor(out, onum[:], hg[:, hd % 2], ALU.mult).then_inc(yh_ready, 1)
                dve.memset(stat[:, 1, 1:2], 0.0).then_inc(on_ready, 1)

            def period(p, q=0):
                if p >= 2:
                    head_out(p - 2, q)
                if p < HG_HEADS:
                    head_inputs(p, q)
                if 1 <= p <= HG_HEADS:
                    head_decay(p - 1, q)
                if p < HG_HEADS:
                    head_values(p, q)
                if 1 <= p <= HG_HEADS:
                    head_mask(p - 1, q)
                    head_states(p - 1, q)

            dve.wait_ge(lb_ready, 4)
            dve.wait_ge(hg_in, 48)
            dve.memset(att[:], 0.0).then_inc(att_zero, 1)
            dve.memset(st[:, 0, :], 0.0).then_inc(att_zero, 1)
            dve.wait_ge(att_zero, 2)
            period(0)
            period(1)
            with dve.Fori(0, 3) as q:
                period(2, q)
                period(3, q)
            period(8)
            period(9)

            for k in range(KC):
                dve.wait_ge(y_hi, k + 1)
                dve.tensor_tensor(al[:, k, :], yh[:, k, :], f32(ah[:, k, :]), ALU.subtract).then_inc(y_lo, 1)
            branches(FIRST["gb"], True)
            for k in range(KC):
                dve.wait_ge(m_hi, k + 1)
                dve.tensor_tensor(ul[:, k, :], merged[:, k, :], f32(uh[:, k, :]), ALU.subtract).then_inc(m_lo, 1)
            for j in range(4):
                for half in range(2):
                    add_to_h(FIRST["wout2"] + j, 2 * j + half, None)
            norm("ffn", h, lambda k: vec[:, V_FFN + k:V_FFN + k + 1], None, uh, ul)

            b0 = FIRST["ffn"]
            dve.memset(stat[:, 4, 0:1], 0.0).then_inc(gz_ready, SQ0)

            def hidden(j, n, m0, q=0, per=0):
                for half in range(2):
                    bi, c = bank_of(b0 + j, half), (n + half + 8 * q if per else n + half)
                    dve.wait_ge(gs_ready, c + 1)
                    dve.wait_ge(zv_ready, SQ0 + c - 1)
                    dve.tensor_tensor(gz[:, half], bank[bi][:], gs[:, half], ALU.mult).then_inc(gz_ready, 1)
                    dve.wait_ge(gz_ready, SQ0 + c + 1)
                    dve.tensor_copy(stat[:, 0, 0:1], gz[:, half, 0:1]).then_inc(bank_free[bi], 1)
                for half in range(2):
                    bi, c, m = bank_of(b0 + j + 1, half), (n + half + 8 * q if per else n + half), m0 + half
                    dve.wait_ge(bank_full[bi], used(b0 + j + 1, q, per) + 1)
                    dve.tensor_tensor(gz[:, half], bank[bi][:], gz[:, half], ALU.mult).then_inc(bank_free[bi], 1)
                    dve.wait_ge(bank_free[bi], used(b0 + j + 1, q, per) + 1)
                    dve.tensor_copy(ah[:, m], gz[:, half]).then_inc(z_hi, 1)
                    dve.wait_ge(z_hi, c + 1)
                    dve.tensor_tensor(al[:, m], gz[:, half], f32(ah[:, m]), ALU.subtract).then_inc(z_lo, 1)
                    dve.memset(stat[:, 0, 1:2], 0.0).then_inc(zv_ready, 1)

            dve.memset(stat[:, 4, 1:2], 0.0).then_inc(zv_ready, SQ0)
            with dve.Fori(0, 2) as q:
                for j in range(0, 8, 2):
                    hidden(j, j, j, q, 12)
                for j in range(8, 12):
                    for half in range(2):
                        add_to_h(b0 + j, 2 * (j - 8) + half, None, q, 12)
            for j in range(0, 6, 2):
                hidden(24 + j, 16 + j, j)
            for j in range(6, 10):
                for half in range(2):
                    add_to_h(b0 + 24 + j, 2 * (j - 6) + half, None)
            i = NORM["final"]
            dve.wait_ge(root_ready, i + 1)
            dve.reciprocal(rstd[:], rstd[:]).then_inc(rstd_ready, 1)
            dve.wait_ge(rstd_ready, i + 1)
            for k in range(KC):
                dve.scalar_tensor_tensor(fin[:, k, :], h[:, k, :], vec[:, V_FIN + k:V_FIN + k + 1], rstd[:], ALU.mult, ALU.mult).then_inc(out_ready, 1)


def blocks(w, kc=KC):
    rows, cols = w.shape
    return np.ascontiguousarray(w.reshape(rows // P, P, cols // BC, BC).transpose(2, 1, 0, 3))


def by_feature(v):
    v = np.asarray(v).reshape(-1, P)
    return np.ascontiguousarray(v.T)


def layout(i):
    f = np.float32
    t = {}
    t["xT"] = i["x"][0].T.reshape(KC, P, S).transpose(1, 0, 2)
    t["ctxT"] = i["ctx"][0].T.reshape(KC, P, L).transpose(1, 0, 2)
    t["c_cols"] = np.stack([i["c"][0].reshape(KC, P).T, i["c_ctx"].reshape(KC, P).T], axis=2)
    t["w_modf"] = blocks(i["w_mod"][0][:, :2048])
    t["w_modr"] = np.concatenate([blocks(i["w_mod"][0][:, 2048:]), blocks(i["w_mod"][1])])
    t["b_mod"] = by_feature(i["b_mod"])
    w = i["w_in_even"][0]
    t["w_in"] = np.concatenate([blocks(w[:, n:n + 512]) for n in (1536, 1024, 512, 0)])
    t["w_out"] = blocks(i["w_out_even"][0])
    t["w4"] = i["w_four"][0].transpose(1, 0, 2)
    for l in range(2):
        t[f"w1_{l}"] = blocks(i["w_mlp1"][l])
        t[f"w2_{l}"] = np.concatenate([blocks(i["w_mlp2"][l][D * q:D * q + D]) for q in range(4)])
    pairs = (np.arange(8)[:, None, None] + 8 * np.arange(2)[None, :, None]) * DH + np.arange(DH)
    pairs = pairs.reshape(-1)
    w, b = i["w_in_2"][0], i["b_in_2"][0]
    aq, akv, hq, hf, hi, hg, ga, gb = (slice(x, y) for x, y in zip((0, 1024, 1280, 2304, 3328, 4352, 5376, 6400), (1024, 1280, 2304, 3328, 4352, 5376, 6400, 7424)))
    t["vecs"] = np.concatenate([by_feature(x) for x in (
        i["norm1_g"], i["norm2_g"], np.tile(i["q_norm_g"][0], 2), np.tile(i["k_norm_g"][0], 2), i["norm_mix_g_2"], i["norm_ffn_g_2"],
        i["norm_final_g_2"], i["pool_scale"], i["hgrn_norm_g_2"], b[aq][pairs], b[1024:1152], b[ga], b[gb], b[hq], b[hf], b[hg],
        i["hgrn_lb_logits_2"])] + [np.broadcast_to(i["attn_sinks_2"][0], (P, 16))], axis=1)
    t["bvrow"] = np.broadcast_to(b[1152:1280], (P, P))
    t["bhrow"] = np.broadcast_to(b[hi].reshape(8, P), (P, 8, P))
    t["w_att2"] = np.concatenate([blocks(w[:, aq][:, pairs]), blocks(w[:, akv])])
    t["w_ga"], t["w_gb"] = blocks(w[:, ga]), blocks(w[:, gb])
    t["w_ba"], t["w_bb"] = blocks(i["w_branch_attn_2"][0][pairs]), blocks(i["w_branch_hgrn_2"][0])
    t["w_hg"] = blocks(np.concatenate([w[:, x].reshape(D, 8, 1, P) for x in (hq, hf, hi, hg)], axis=2).reshape(D, 4 * D))
    t["w_out2"] = blocks(i["w_out_2"][0])
    gate, up = (i[n][0].reshape(D, 11, 1, BC) for n in ("w_ffn_gate_2", "w_ffn_up_2"))
    t["w_gu"] = blocks(np.concatenate([gate, up], axis=2).reshape(D, 22 * BC))
    down = np.zeros((3 * D, D), f)
    down[:2816] = i["w_ffn_down_2"][0]
    t["w_dn"] = np.concatenate([blocks(down[D * g:D * g + D]) for g in range(3)])
    t["w_pool"] = i["w_pool"][0].reshape(4, 2, P, BC).transpose(0, 2, 1, 3)
    r = np.zeros((ROWS, NH, ROWS, 64), f)
    for q in range(ROWS):
        r[q, :, :, 16:16 + 31] = i["rpb"][0][:, 7 - q:15 - q, :]
    t["rpb"] = r.reshape(ROWS, NH * ROWS, 64)
    con = np.zeros((P, C_END), f)
    con[:, C_ID:C_ID + P] = np.eye(P)
    con[:, C_OND:C_OND + P] = 1 / D
    con[:64, C_ONH:C_ONH + 64] = con[64:, C_ONH + 64:C_ONH + 128] = 1 / DH
    con[:, C_ONE] = 1
    con[:, C_EPS] = EPS
    con[:, C_EPSQ] = EPS * DH
    con[:, C_ONV:C_ONV + P] = 1 / P
    t["consts"] = con
    n = np.arange(S)
    ang = 2 * np.pi * (np.outer(n, n) % S) / S
    t["dftc"] = np.cos(ang).astype(f).reshape(4, P, S).transpose(1, 0, 2)
    t["dfts"] = (-np.sin(ang)).astype(f).reshape(4, P, S).transpose(1, 0, 2)
    n = np.arange(P)
    ang = 2 * np.pi * (np.outer(n, n) % P) / P
    t["cs"] = (np.concatenate([np.cos(ang), np.sin(ang)], axis=1) / 256).astype(f)
    m = np.full((3, QC, WIN), NEG, f)
    for a, w in enumerate((0, 1, 3)):
        for c in range(QC):
            col = QC * w + c
            s = min(max(col - 8, 0), COLS - 16) - W0[w]
            m[a, c, s:s + 16] = 0
    t["mask"] = np.ascontiguousarray(np.broadcast_to(m.transpose(1, 0, 2)[None, :, :, None, :], (ROWS, QC, 3, ROWS, WIN))).reshape(P, 3, 256)
    full = np.zeros((4, S, S))
    for g, win in enumerate((2, 4, 8, 16)):
        for n in range(S):
            lo, hi = max(0, n - win // 2), min(S, n + win - win // 2)
            full[g, lo:hi, n] = 1 / (hi - lo)
            full[g, n, n] -= 1
    band = np.zeros((P, 3, FG, 144), f)
    for kind, tile in enumerate((0, 1, 3)):
        lo, hi = max(0, P * tile - 8), min(S, P * tile + P + 8)
        r = lo - (P * tile - 8)
        band[:, kind, :, r:r + hi - lo] = full[:, P * tile:P * tile + P, lo:hi].transpose(1, 0, 2)
    t["band"] = band
    q, k = np.arange(P)[:, None], np.arange(256)[None, :]
    t["wmask"] = np.stack([np.where(k <= q, 0, 8 * NEG), np.where((k > q) & (k <= q + P), 0, 8 * NEG)], axis=1).astype(f)
    a, b = np.arange(P)[:, None], np.arange(P)[None, :]
    same = a // 64 == b // 64
    upto = same & (a <= b)
    t["cm"] = np.stack([upto.astype(f) - (same & (a % 64 <= 31)), upto, same & (a > b)], axis=1).astype(f)
    t["cmask"] = np.tile(upto, (1, 4)).astype(np.uint32)
    return {k: np.ascontiguousarray(v) for k, v in t.items()}


def kernel(**inputs):
    import concourse.bacc as _bacc
    from concourse.bass_utils import run_bass_kernel_spmd as _run

    nc = _bacc.Bacc("TRN2", target_bir_lowering=False, num_devices=1)
    arrays = layout({k: np.asarray(v) for k, v in inputs.items()})
    t = {k: nc.dram_tensor(f"in_{k}", a.shape, mybir.dt.from_np(a.dtype), kind="ExternalInput").ap() for k, a in arrays.items()}
    t["out"] = nc.dram_tensor("out_0_dram", (P, KC, S), F32, kind="ExternalOutput").ap()
    build_program(nc, t)
    r = _run(nc, [{f"in_{k}": a for k, a in arrays.items()}], core_ids=[0])
    got = r.results[0]["out_0_dram"]
    return got.transpose(1, 0, 2).reshape(D, S).T.reshape(1, S, D)
```

```python
from contextlib import ExitStack

import numpy as np

import concourse.bass as bass
from concourse import mybir

F32 = mybir.dt.float32
F32R = mybir.dt.float32r
ALU = mybir.AluOpType
ACT = mybir.ActivationFunctionType
AX_X = mybir.AxisListType.X

P = 128
D = 1024
KC = D // P
S = 512
L = 256
BC = 256
EPS = 1e-6
NEG = -1e30
SQ0 = 2
KB = 1024

NH, DH = 8, 64
ROWS, COLS, WIN = 8, 64, 32
QT, QC = 4, 16
W0 = [0, 8, 24, 32]
TOFF = [16, 8, 8, 0]
TMASK = [0, 1, 1, 2]
FG = 4
RAW = 4

PLAN = [("v", 2), ("k", 2), ("q", 2), ("f", 2), ("wout", 4), ("mlp0", 32), ("pool", 4), ("mlp1", 32),
        ("aq", 4), ("akv", 1), ("ga", 8), ("hgrn", 16), ("gb", 8), ("wout2", 4), ("ffn", 34)]
FIRST, _at = {}, 0
for _name, _n in PLAN:
    FIRST[_name] = _at
    _at += _n
BLOCKS = _at
NORM = {"x": 0, "ctx": 1, "mlp0": 2, "pool": 3, "mlp1": 4, "mix2": 5, "ffn": 6, "final": 7}
H_FROM = {"mlp0": FIRST["wout"], "pool": FIRST["mlp0"] + 28, "mix2": FIRST["mlp1"] + 28,
          "ffn": FIRST["wout2"], "final": FIRST["ffn"] + 30}
MOD0, MOD1 = 16, 24

C_ID, C_OND, C_ONH, C_ONE, C_EPS, C_EPSQ, C_ONV, C_END = 0, 128, 256, 384, 385, 386, 387, 515
V_G1, V_G2, V_QG, V_KG, V_MIX, V_FFN, V_FIN, V_PS, V_HG, V_BQ, V_BK, V_BGA, V_BGB, V_BHQ, V_BHF, V_BHG, V_LB, V_SINK, V_END = (
    0, 16, 32, 33, 34, 42, 50, 58, 66, 74, 82, 83, 91, 99, 107, 115, 123, 139, 155)
HG_HEADS = 8


def build_program(nc, t):
    es = ExitStack()
    with es:
        def sem(name):
            return es.enter_context(nc.semaphore(name))

        base = 16512

        def at(name, shape, dt, offset):
            return nc.alloc_sbuf_tensor_at(name, shape, dt, offset=base + offset)

        o = 0
        h = at("h", [P, KC, S], F32, o); o += 16 * KB
        uh = at("uh", [P, KC, S], F32R, o); o += 16 * KB
        ul = at("ul", [P, KC, S], F32R, o); o += 16 * KB
        raw = at("raw", [P, RAW, KC, BC], F32, o); o += 32 * KB
        wh = at("wh", [P, 2, KC, BC], F32R, o); o += 16 * KB
        wl = at("wl", [P, 2, KC, BC], F32R, o); o += 16 * KB
        con = at("con", [P, C_END + 5], F32, o); o += 2080
        vec = at("vec", [P, V_END + 5], F32, o); o += 640
        bmod = at("bmod", [P, 96], F32, o); o += 384
        modc = at("modc", [P, 96], F32, o); o += 384
        modx = at("modx", [P, 16], F32, o); o += 64
        gm = at("gm", [P, 6, KC], F32, o); o += 192
        lbs = at("lbs", [P, 3, KC], F32, o); o += 96
        csil = at("csil", [P, KC, 2], F32, o); o += 64
        craw = at("craw", [P, KC, 2], F32, o); o += 64
        stat = at("stat", [P, 20, 2], F32, o); o += 160
        rc = at("rc", [P, 2, 4], F32, o); o += 32
        A = (o + 31) // 32 * 32
        modf = at("modf", [P, 8, KC, BC], F32, A)
        ctxT = at("ctxT", [P, KC, L], F32, A + 64 * KB)
        modrow = at("modrow", [2, 2048], F32, A + 72 * KB)
        qT = at("qT", [P, 4, S], F32, A)
        kT = at("kT", [P, 4, S], F32, A + 8 * KB)
        kcT = at("kcT", [P, 4, L], F32, A + 16 * KB)
        vc = at("vc", [P, 2, S], F32, A + 20 * KB)
        fT = at("fT", [P, 4, S], F32, A + 24 * KB)
        vnat = at("vnat", [P, 4, S], F32, A + 24 * KB)
        vwin = at("vwin", [P, 2 * QT, S], F32, A + 32 * KB)
        mraw = at("mraw", [P, 2, KC, BC], F32, A + 48 * KB)
        tab = at("tab", [P, NH * ROWS, 48], F32, A + 48 * KB)
        tm = at("tm", [P, 2, S], F32, A + 60 * KB)
        cs = at("cs", [P, 2 * P], F32, A + 60 * KB)
        w4 = at("w4", [P, FG, P], F32, A + 61 * KB)
        uch = at("uch", [P, KC, L], F32R, A + 72 * KB)
        ucl = at("ucl", [P, KC, L], F32R, A + 64 * KB)
        dftc = at("dftc", [P, 4, S], F32, A + 64 * KB)
        dfts = at("dfts", [P, 4, S], F32, A + 72 * KB)
        sc = at("sc", [P, 2, S], F32, A + 64 * KB)
        pn = at("pn", [P, 2, S], F32, A + 68 * KB)
        pT = at("pT", [P, 2, S], F32, A + 72 * KB)
        sq = at("sq", [P, 2, S], F32, A + 80 * KB)
        tt = at("tt", [P, 2, S], F32, A + 84 * KB)
        ysb = at("ysb", [P, 4, 2 * P], F32, A + 80 * KB)
        cw = at("cw", [P, FG, 2 * P], F32, A + 84 * KB)
        sqs0 = at("sqs0", [P, S], F32, A + 88 * KB)
        sqs1 = at("sqs1", [P, S], F32, A + 72 * KB)
        diag = at("diag", [P, 4, P], F32, A + 76 * KB)
        mask = at("mask", [P, 3, 256], F32, A + 88 * KB)
        acc = at("acc", [P, 2, BC], F32, A + 88 * KB)
        ah = at("ah", [P, KC, S], F32R, A)
        al = at("al", [P, KC, S], F32R, A + 16 * KB)
        r1 = at("r1", [P, 2, S], F32, A + 64 * KB)
        v1 = at("v1", [P, 2, S], F32, A + 68 * KB)

        band = at("band", [P, 3, FG, 144], F32, A)
        zt = at("zt", [P, FG, 4, BC], F32, A + 16 * KB)
        aqT = at("aqT", [P, KC, S], F32, A + 32 * KB)
        akT = at("akT", [P, S], F32, A + 48 * KB)
        av = at("av", [P, 4, P], F32, A + 50 * KB)
        wmask = at("wmask", [P, 2, 256], F32, A + 52 * KB)
        bvrow = at("bvrow", [P, P], F32, A + 54 * KB)
        sc2 = at("sc2", [P, 2, S], F32, A + 55 * KB)
        pn2 = at("pn2", [P, 2, S], F32, A + 59 * KB)
        pT2 = at("pT2", [P, 2, S], F32, A + 64 * KB)
        merged = at("merged", [P, KC, S], F32, A + 64 * KB)
        sg = at("sg", [P, 2, S], F32, A + 80 * KB)
        mt = at("mt", [P, 2, S], F32, A + 84 * KB)
        yh = at("yh", [P, KC, S], F32, A + 32 * KB)
        hq = at("hq", [P, 2, S], F32, A)
        hk = at("hk", [P, 2, S], F32, A + 4 * KB)
        hv = at("hv", [P, 2, 4, 2 * P], F32, A + 8 * KB)
        hg = at("hg", [P, 2, S], F32, A + 86 * KB)
        ex = at("ex", [P, 4, S], F32, A + 16 * KB)
        lf = at("lf", [P, S], F32, A + 24 * KB)
        lft = at("lft", [P, 4, P], F32, A + 26 * KB)
        krt = at("krt", [P, 4, P], F32, A + 28 * KB)
        qb = at("qb", [P, S], F32, A + 30 * KB)
        att = at("att", [P, S], F32, A + 48 * KB)
        st = at("st", [P, 8, P], F32, A + 50 * KB)
        cm = at("cm", [P, 3, P], F32, A + 54 * KB)
        cmask = at("cmask", [P, S], mybir.dt.uint32, A + 56 * KB)
        bhrow = at("bhrow", [P, HG_HEADS, P], F32, A + 58 * KB)
        osq = at("osq", [P, S], F32, A + 62 * KB)
        ort = at("ort", [P, S], F32, A + 80 * KB)
        sgm = at("sgm", [P, S], F32, A + 82 * KB)
        onum = at("onum", [P, S], F32, A + 84 * KB)
        gs = at("gs", [P, 2, S], F32, A + 32 * KB)
        gz = at("gz", [P, 2, S], F32, A + 36 * KB)
        fin = at("fin", [P, KC, S], F32, A + 40 * KB)

        bank = [nc.alloc_psum_tensor(f"bank{i}", [P, S], F32) for i in range(8)]

        raw_full = [sem(f"raw_full{i}") for i in range(RAW)]
        split_hi, split_lo = sem("split_hi"), sem("split_lo")
        bank_full = [sem(f"bank_full{i}") for i in range(4)]
        bank_free = [sem(f"bank_free{i}") for i in range(4)]
        c_in, const_in, x_in, ctx_in = sem("c_in"), sem("const_in"), sem("x_in"), sem("ctx_in")
        modf_in = [sem(f"modf_in{i}") for i in range(8)]
        mraw_full = [sem(f"mraw_full{i}") for i in range(2)]
        macc, mcol_full, mcol_used = sem("macc"), sem("mcol_full"), sem("mcol_used")
        csil_ready, modrow_full, modrow_copied, mod0_full, mod0_ready = (
            sem("csil_ready"), sem("modrow_full"), sem("modrow_copied"), sem("mod0_full"), sem("mod0_ready"))
        sq_ready, sq_added, sum_full, root_ready, rstd_ready, diag_ready, rms_full = (
            sem("sq_ready"), sem("sq_added"), sem("sum_full"), sem("root_ready"), sem("rstd_ready"), sem("diag_ready"), sem("rms_full"))
        t_ready, uhi_ready, ulo_ready = sem("t_ready"), sem("uhi_ready"), sem("ulo_ready")
        gain_ready = sem("gain_ready")
        ctx_full, ctx_free = sem("ctx_full"), sem("ctx_free")
        v_copied, vwin_in, tab_in, dft_in, w4_in = (
            sem("v_copied"), sem("vwin_in"), sem("tab_in"), sem("dft_in"), sem("w4_in"))
        hsq_ready, hsum_full, hroot_ready, hrstd_ready = (
            sem("hsq_ready"), sem("hsum_full"), sem("hroot_ready"), sem("hrstd_ready"))
        f_copied, cw_full, cw_ready, y_full, y_ready, four_full, four_hi, four_lo = (
            sem("f_copied"), sem("cw_full"), sem("cw_ready"), sem("y_full"), sem("y_ready"),
            sem("four_full"), sem("four_hi"), sem("four_lo"))
        tm_zero, tm_half, tm_ready, s_full, smax, nmax, p_exp, p_recip, p_norm = (
            sem("tm_zero"), sem("tm_half"), sem("tm_ready"), sem("s_full"), sem("smax"), sem("nmax"),
            sem("p_exp"), sem("p_recip"), sem("p_norm"))
        pt_full, pt_copied, o_full, o_hi, o_lo = sem("pt_full"), sem("pt_copied"), sem("o_full"), sem("o_hi"), sem("o_lo")
        square_ready, a_hi, a_lo = sem("square_ready"), sem("a_hi"), sem("a_lo")
        band_in, yp_full, yp_free = sem("band_in"), sem("yp_full"), sem("yp_free")
        b2_in, lb_ready, akv_ready = sem("b2_in"), sem("lb_ready"), sem("akv_ready")
        s2_full, smax2, nmax2, sink_ready, p2_exp, tot2, p2_recip, p2_norm = (
            sem("s2_full"), sem("smax2"), sem("nmax2"), sem("sink_ready"), sem("p2_exp"), sem("tot2"), sem("p2_recip"), sem("p2_norm"))
        pt2_full, pt2_copied, o2_full, o2_hi, o2_lo = sem("pt2_full"), sem("pt2_copied"), sem("o2_full"), sem("o2_hi"), sem("o2_lo")
        merged_ready = sem("merged_ready")
        hg_in, att_zero = sem("hg_in"), sem("att_zero")
        q_sig, f_sig, k_done, f_lin, f_log = sem("q_sig"), sem("f_sig"), sem("k_done"), sem("f_lin"), sem("f_log")
        lft_full, lft_copied, cum_full, ex_done, qd_done, kd_done, qb_done, kr_done = (
            sem("lft_full"), sem("lft_copied"), sem("cum_full"), sem("ex_done"), sem("qd_done"), sem("kd_done"), sem("qb_done"), sem("kr_done"))
        krt_full, krt_copied, att_full, att_done, upd_full, st_done, oh_full = (
            sem("krt_full"), sem("krt_copied"), sem("att_full"), sem("att_done"), sem("upd_full"), sem("st_done"), sem("oh_full"))
        osq_ready, osum_full, oroot_ready, orstd_ready, on_ready, on_gated, yh_ready = (
            sem("osq_ready"), sem("osum_full"), sem("oroot_ready"), sem("orstd_ready"), sem("on_ready"), sem("on_gated"), sem("yh_ready"))
        y_hi, y_lo, m_hi, m_lo = sem("y_hi"), sem("y_lo"), sem("m_hi"), sem("m_lo")
        gs_ready, gz_ready, zv_ready, z_hi, z_lo, out_ready = (
            sem("gs_ready"), sem("gz_ready"), sem("zv_ready"), sem("z_hi"), sem("z_lo"), sem("out_ready"))
        out_done = sem("out_done")
        S2_BANKS = [(4, 5), (0, 1)]
        ITEMS2 = [(c, n) for c in range(KC) for n in range(4)]

        ident = con[:, C_ID:C_ID + P]
        ones_d = con[:, C_OND:C_OND + P]
        ones_h = con[:, C_ONH:C_ONH + P]
        ones_v = con[:, C_ONV:C_ONV + P]
        one_col = con[:, C_ONE:C_ONE + 1]
        eps_col = con[:, C_EPS:C_EPS + 1]
        epsq_col = con[:, C_EPSQ:C_EPSQ + 1]
        PROJ = 8

        def f32(x):
            return x.bitcast(F32)

        def mod(layer, j, k):
            return modc[:, 48 * layer + 8 * j + k:48 * layer + 8 * j + k + 1]

        def bank_of(b, half):
            return 2 * (b % 2) + half

        def used(b, q=0, per=0):
            return b // 2 + (per // 2) * q if per else b // 2

        def count(b, q=0, per=0):
            return b + per * q if per else b

        def chunks_of(b, per=0):
            return 2 if not per and FIRST["pool"] <= b < FIRST["pool"] + 4 else KC

        def wait_block(eng, b, q=0, per=0):
            eng.wait_ge(bank_full[bank_of(b, 1)], used(b, q, per) + 1)

        HN = [("k", 0), ("k", 1), ("kc", 0), ("k", 2), ("k", 3), ("q", 0), ("q", 1), ("q", 2), ("q", 3), ("kc", 1)]
        HN_AFTER = {(3, -1): 0, (3, 0): 1, (3, 1): 2, (4, 0): 3, (4, 1): 4, (5, 0): 5, (5, 1): 6, (6, 0): 7, (6, 1): 8, (7, 0): 9}

        def hn_place(i):
            kind, m = HN[i]
            if kind == "kc":
                return bank[4 + m][:, :], ctx_free, kcT[:, 2 * m:2 * m + 2, :].rearrange("p a n -> p (a n)")
            b = {"k": 2, "q": 4}[kind] + m // 2
            return bank[bank_of(b, m % 2)][:, :], bank_free[bank_of(b, m % 2)], (kT if kind == "k" else qT)[:, m, :]

        def hn_wait(eng, i):
            kind, m = HN[i]
            if kind == "kc":
                eng.wait_ge(ctx_full, 3 + m)
            else:
                b = {"k": 2, "q": 4}[kind] + m // 2
                eng.wait_ge(bank_full[bank_of(b, m % 2)], used(b) + 1)

        def hn_wait_done(eng, i):
            kind, m = HN[i]
            if kind == "kc":
                eng.wait_ge(ctx_free, 3 + m)
            else:
                b = {"k": 2, "q": 4}[kind] + m // 2
                eng.wait_ge(bank_free[bank_of(b, m % 2)], used(b) + 1)

        def norm_sqs(name):
            return sqs0 if name in ("x", "ctx") else sqs1

        def norm_banks(name):
            return (bank[2], bank[3]) if name == "x" else (bank[6], bank[7])

        def mod_summed(eng, m, q=0, per=0):
            eng.wait_ge(macc, 8 * (m + 1) + 8 * per * q if per else 8 * (m + 1))

        def h_wait(eng, name, k):
            if name in ("x", "ctx"):
                if k == 0:
                    eng.wait_ge(x_in if name == "x" else ctx_in, 16)
                return
            if name == "mlp1":
                eng.wait_ge(yp_free, k + 1)
                return
            b = H_FROM[name] + k // 2
            eng.wait_ge(bank_free[bank_of(b, k % 2)], used(b) + 1)

        def qf_block(n):
            return FIRST["hgrn"] + 2 * n

        def v_block(n):
            return FIRST["hgrn"] + 4 * (n // 2) + 1

        def g_block(n):
            return FIRST["hgrn"] + 4 * (n // 2) + 3

        def periods(heads_after):
            return range(HG_HEADS + heads_after)

        def is_head(n):
            return 0 <= n < HG_HEADS

        ITEMS = [(hp, q, e) for hp in range(4) for q in range(QT) for e in range(2)]

        def by_column(x, lo, n):
            return x.rearrange("p (r c) -> p r c", c=COLS)[:, :, lo:lo + n]

        block = es.enter_context(nc.Block())

        @block.sync
        def _(sp):
            def load(b, src, q=0, per=0, nk=KC):
                if per or b >= RAW:
                    sp.wait_ge(split_hi, count(b - RAW + 1, q, per))
                    sp.wait_ge(split_lo, count(b - RAW + 1, q, per))
                sp.dma_start(raw[:, b % RAW, 0:nk, :], src).then_inc(raw_full[b % RAW], 16)

            def load_mod(m, q=0, per=0):
                if m < 2 and not per:
                    sp.wait_ge(modrow_full, 8)
                else:
                    mod_summed(sp, m - 2, q, per)
                sp.dma_start(mraw[:, m % 2], t["w_modr"][count(m, q, per)]).then_inc(mraw_full[m % 2], 16)

            sp.dma_start(craw[:], t["c_cols"]).then_inc(c_in, 16)
            sp.dma_start(con[:, 0:C_END], t["consts"]).then_inc(const_in, 16)
            sp.dma_start(vec[:, 0:V_END], t["vecs"]).then_inc(const_in, 16)
            sp.dma_start(bmod[:], t["b_mod"]).then_inc(const_in, 16)
            sp.dma_start(modf[:, 0], t["w_modf"][0]).then_inc(modf_in[0], 16)
            sp.dma_start(h[:], t["xT"]).then_inc(x_in, 16)
            for i in range(1, 8):
                if i == 6:
                    load(0, t["w_in"][0])
                sp.dma_start(modf[:, i], t["w_modf"][i]).then_inc(modf_in[i], 16)
            sp.dma_start(ctxT[:], t["ctxT"]).then_inc(ctx_in, 16)
            for b in range(1, 4):
                load(b, t["w_in"][b])
            for b in range(8):
                if 4 <= b + 2 <= 8:
                    load(b + 2, t["w_in"][b + 2] if b < 6 else t["w_out"][0])
                load_mod(b)
                if b == 2:
                    for bi in range(4):
                        sp.wait_ge(bank_free[bi], 1)
                    for w in range(QT):
                        for j in range(ROWS):
                            sp.dma_start(vwin[32 * (j % 4):32 * (j % 4) + 32, 2 * w + j // 4, :],
                                         vnat[64 * (j % 2) + W0[w]:64 * (j % 2) + W0[w] + WIN, j // 2, :])\
                              .then_inc(vwin_in, 16)
                if b == 5:
                    sp.wait_ge(ctx_full, 4)
                    sp.dma_start(dftc[:], t["dftc"]).then_inc(dft_in, 16)
                    sp.dma_start(dfts[:], t["dfts"]).then_inc(dft_in, 16)
            for b in range(8, 12):
                if b == 10:
                    mod_summed(sp, PROJ - 1)
                    sp.dma_start(cs[:], t["cs"]).then_inc(w4_in, 16)
                    sp.dma_start(w4[:], t["w4"]).then_inc(w4_in, 16)
                    for c in range(QC):
                        sp.dma_start(tab[c::QC], t["rpb"][:, :, QC - 1 - c:QC - 1 - c + 48]).then_inc(tab_in, 16)
                    sp.wait_ge(mcol_full, PROJ)
                    sp.dma_start(mask[:], t["mask"]).then_inc(tab_in, 16)
                if b > 8:
                    load(b, t["w_out"][b - 8])
            sp.wait_ge(smax, len(ITEMS))
            for m in range(PROJ, MOD0):
                load_mod(m)
            m0 = FIRST["mlp0"]
            with sp.Fori(0, 4) as q:
                for j in range(8):
                    load(m0 + j, (t["w1_0"] if j < 4 else t["w2_0"])[4 * q + j % 4], q, 8)
                    if j < 6:
                        load_mod(MOD0 + j, q, 6)
            b0 = FIRST["pool"]
            for g in range(FG):
                load(b0 + g, t["w_pool"][g], nk=2)
                if g == 0:
                    wait_block(sp, FIRST["pool"] - 1)
                    sp.dma_start(band[:], t["band"]).then_inc(band_in, 16)
            b0 = FIRST["mlp1"]
            with sp.Fori(0, 4) as q:
                for j in range(8):
                    load(b0 + j, (t["w1_1"] if j < 4 else t["w2_1"])[4 * q + j % 4], q, 8)
            b0 = FIRST["aq"]
            for j in range(5):
                load(b0 + j, t["w_att2"][j])
                if j == 2:
                    wait_block(sp, b0 - 1)
                    sp.dma_start(wmask[:], t["wmask"]).then_inc(b2_in, 16)
                    sp.dma_start(bvrow[:], t["bvrow"]).then_inc(b2_in, 16)
            for j in range(8):
                load(FIRST["ga"] + j, (t["w_ga"] if j % 2 == 0 else t["w_ba"])[j // 2])
            sp.wait_ge(o2_lo, KC)
            for dst, src in ((cm, "cm"), (cmask, "cmask"), (bhrow, "bhrow")):
                sp.dma_start(dst[:], t[src]).then_inc(hg_in, 16)
            b0 = FIRST["hgrn"]
            with sp.Fori(0, 4) as q:
                for j in range(4):
                    load(b0 + j, t["w_hg"][4 * q + j], q, 4)
            for j in range(8):
                load(FIRST["gb"] + j, (t["w_gb"] if j % 2 == 0 else t["w_bb"])[j // 2])
            for j in range(4):
                load(FIRST["wout2"] + j, t["w_out2"][j])
            b0 = FIRST["ffn"]
            with sp.Fori(0, 2) as q:
                for j in range(12):
                    src = t["w_gu"][8 * q + j] if j < 8 else t["w_dn"][4 * q + j - 8]
                    load(b0 + j, src, q, 12)
            for j in range(10):
                load(b0 + 24 + j, t["w_gu"][16 + j] if j < 6 else t["w_dn"][8 + j - 6, :, 0:6, :], nk=KC if j < 6 else 6)
            for k in range(KC):
                sp.wait_ge(out_ready, k + 1)
                sp.dma_start(t["out"][:, k, :], fin[:, k, :]).then_inc(out_done, 16)
            sp.wait_ge(out_done, 16 * KC)

        @block.scalar
        def _(act):
            def split(b, q=0, per=0):
                s = b % RAW
                act.wait_ge(raw_full[s], 16 * (b // RAW + 1) + 16 * (per // RAW) * q if per else 16 * (b // RAW + 1))
                if per or b >= 2:
                    act.wait_ge(bank_full[bank_of(b, 1)], used(b, q, per))
                if 2 <= b < 4:
                    act.wait_ge(ctx_full, b - 1)
                nk = chunks_of(b, per)
                act.activation(wh[:, b % 2, 0:nk], raw[:, s, 0:nk], ACT.Copy).then_inc(split_hi, 1)

            def squares(name, src, ks, n=S):
                i = NORM[name]
                for k in ks:
                    h_wait(act, name, k)
                    if k >= 2:
                        act.wait_ge(sq_added, 6 * i + max(k - 2, 1))
                    elif i:
                        act.wait_ge(sum_full, i)
                    act.activation(sq[:, k % 2, 0:n], src[:, k, :], ACT.Square).then_inc(sq_ready, 1)

            def root(name, n=S):
                i = NORM[name]
                act.wait_ge(sum_full, i + 1)
                act.activation(rc[:, 0, 0:n // P], norm_banks(name)[0][:, 0:n // P], ACT.Sqrt, bias=eps_col).then_inc(root_ready, 1)

            def highs(name, shift, hi, n=S):
                i = NORM[name]
                for k in range(KC):
                    act.wait_ge(t_ready, 8 * i + k + 1)
                    if shift is None:
                        ins = act.activation(hi[:, k, :], tt[:, k % 2, 0:n], ACT.Copy)
                    else:
                        ins = act.activation(hi[:, k, :], tt[:, k % 2, 0:n], ACT.Identity, bias=shift(k))
                    ins.then_inc(uhi_ready, 1)

            act.wait_ge(c_in, 16)
            act.activation(csil[:], craw[:], ACT.Silu).then_inc(csil_ready, 1)
            act.wait_ge(const_in, 48)
            squares("x", h, range(KC))
            root("x")
            split(0)
            highs("x", lambda k: mod(0, 0, k), uh)
            squares("ctx", ctxT, range(KC), L)
            split(1)
            root("ctx", L)
            highs("ctx", lambda k: modx[:, k:k + 1], uch, L)

            def hn_square(i):
                hn_wait(act, i)
                if i >= 2:
                    act.wait_ge(hsum_full, i - 1)
                act.activation(sq[:, i % 2], hn_place(i)[0], ACT.Square).then_inc(hsq_ready, 1)

            def hn_root(i):
                act.wait_ge(hsum_full, i + 1)
                if i >= 2:
                    hn_wait_done(act, i - 2)
                if HN[i][0] == "q":
                    act.activation(tt[:, i % 2], bank[6][:], ACT.Sqrt, bias=epsq_col, scale=float(DH)).then_inc(hroot_ready, 1)
                else:
                    act.activation(tt[:, i % 2], bank[6][:], ACT.Sqrt, bias=eps_col).then_inc(hroot_ready, 1)

            for b in range(8):
                if b:
                    split(b + 1)
                if b in (1, 2):
                    act.wait_ge(ctx_full, b)
                    act.activation(vc[:, :, BC * (b - 1):BC * b], bank[3 + b][:].rearrange("p (a n) -> p a n", a=2), ACT.Copy).then_inc(ctx_free, 1)
                if b == 2:
                    hn_square(0)
                    hn_square(1)
                for half in range(2):
                    for at_ in ((b, -1), (b - 1, 1)) if half == 0 else ((b, 0),):
                        if at_ in HN_AFTER:
                            i = HN_AFTER[at_]
                            hn_root(i)
                            if i + 2 < len(HN):
                                hn_square(i + 2)
                    bi = bank_of(b, half)
                    if b < 2:
                        act.wait_ge(bank_full[bi], used(b) + 1)
                        act.activation(vnat[:, 2 * half:2 * half + 2, BC * b:BC * b + BC],
                                       bank[bi][:].rearrange("p (a n) -> p a n", a=2), ACT.Copy).then_inc(bank_free[bi], 1)
                    if b >= 6:
                        act.wait_ge(bank_full[bi], used(b) + 1)
                        if b == 6 and half == 0:
                            act.wait_ge(vwin_in, 16 * 32)
                        act.activation(fT[:, 2 * (b - 6) + half, :], bank[bi][:], ACT.Copy).then_inc(bank_free[bi], 1)
            for g in range(FG):
                act.wait_ge(y_full, 2 * g + 1)
                if g:
                    act.wait_ge(four_full, g)
                act.activation(ysb[:, 0:2, :], bank[6][:].rearrange("p (a n) -> p a n", a=2), ACT.Copy).then_inc(y_ready, 1)
                act.wait_ge(y_full, 2 * g + 2)
                act.activation(ysb[:, 2:4, :], bank[7][:].rearrange("p (a n) -> p a n", a=2), ACT.Copy).then_inc(y_ready, 1)
                act.wait_ge(four_full, g + 1)
                act.activation(uh[:, g, :], bank[4 + g % 2][:], ACT.Copy).then_inc(four_hi, 1)

            def exp(i):
                act.wait_ge(nmax, i + 1)
                act.activation(sc[:, i % 2], sc[:, i % 2], ACT.Exp, bias=stat[:, 1, i % 2:i % 2 + 1],
                               accum_out=stat[:, 2, i % 2:i % 2 + 1]).then_inc(p_exp, 1)

            def copy_pt(i):
                act.wait_ge(pt_full, i + 1)
                if i >= 2:
                    act.wait_ge(o_full, i - 1)
                act.activation(pT[:, i % 2], bank[6 + i % 2][:], ACT.Copy).then_inc(pt_copied, 1)

            def o_high(hp):
                act.wait_ge(o_full, 8 * hp + 8)
                act.activation(uh[:, 4 + hp, :].rearrange("p (r w c) -> p w r c", r=ROWS, c=QC),
                               bank[2 + hp % 2][:].rearrange("p (w r c) -> p w r c", r=ROWS, c=QC), ACT.Copy).then_inc(o_hi, 1)

            for i in range(len(ITEMS) + 3):
                if i >= 3:
                    copy_pt(i - 3)
                if i < len(ITEMS):
                    exp(i)
                if i >= 8 and i % 8 == 4:
                    o_high(i // 8 - 1)
            o_high(3)
            for b in range(8, 12):
                split(b + 1)
                if b > 8:
                    squares("mlp0", h, (2 * (b - 9), 2 * (b - 9) + 1))
            squares("mlp0", h, (6, 7))
            root("mlp0")

            def mlp(layer, after):
                b0 = FIRST[f"mlp{layer}"]

                def group(q, last=False):
                    for j in range(8):
                        split(b0 + j + 1, q, 8)
                        if last and j > 4:
                            squares(after, h, (2 * (j - 5), 2 * (j - 5) + 1))
                        if j >= 4:
                            continue
                        for half in range(2):
                            bi, m = bank_of(b0 + j, half), 2 * j + half
                            act.wait_ge(bank_full[bi], used(b0 + j, q, 8) + 1)
                            act.wait_ge(square_ready, SQ0 + 32 * layer + m - 1 + 8 * q)
                            act.activation(r1[:, m % 2], bank[bi][:], ACT.Relu).then_inc(bank_free[bi], 1)

                with act.Fori(0, 3) as q:
                    group(q)
                group(3, True)
                squares(after, h, (6, 7))
                root(after)

            highs("mlp0", lambda k: mod(0, 3, k), uh)
            mlp(0, "pool")

            highs("pool", lambda k: mod(1, 0, k), uh)
            b0 = FIRST["pool"]
            for g in range(FG):
                split(b0 + g + 1)
                for half in range(2):
                    bi = bank_of(b0 + g, half)
                    act.wait_ge(bank_full[bi], used(b0 + g) + 1)
                    act.activation(zt[:, g, 2 * half:2 * half + 2, :], bank[bi][:].rearrange("p (a n) -> p a n", a=2), ACT.Copy).then_inc(bank_free[bi], 1)
            squares("mlp1", h, range(KC))
            root("mlp1")
            highs("mlp1", lambda k: mod(1, 3, k), uh)
            mlp(1, "mix2")

            highs("mix2", None, uh)
            act.wait_ge(lb_ready, 1)
            act.activation(lbs[:, 0, :], lbs[:, 0, :], ACT.Sigmoid).then_inc(lb_ready, 1)
            b0 = FIRST["aq"]
            for j in range(5):
                split(b0 + j + 1)
                for half in range(2 if j < 4 else 1):
                    bi = bank_of(b0 + j, half)
                    act.wait_ge(bank_full[bi], used(b0 + j) + 1)
                    out, col = (aqT[:, 2 * j + half, :], V_BQ + 2 * j + half) if j < 4 else (akT[:], V_BK)
                    act.activation(out, bank[bi][:], ACT.Identity, bias=vec[:, col:col + 1]).then_inc(bank_free[bi], 1)

            def exp2(i):
                act.wait_ge(sink_ready, i + 1)
                act.activation(stat[:, 6 + 10 * (i % 2), :], stat[:, 5 + 10 * (i % 2), :], ACT.Exp).then_inc(p2_exp, 1)
                for e in range(2):
                    x = sc2[:, i % 2, 256 * e:256 * e + 256]
                    act.activation(x, x, ACT.Exp, bias=stat[:, 4 + 10 * (i % 2), e:e + 1], accum_out=stat[:, 7 + 10 * (i % 2), e:e + 1]).then_inc(p2_exp, 1)

            def copy_pt2(i):
                act.wait_ge(pt2_full, i + 1)
                if i >= 2:
                    act.wait_ge(o2_full, i - 1)
                act.activation(pT2[:, i % 2], bank[6 + i % 2][:], ACT.Copy).then_inc(pt2_copied, 1)

            def o2_high(c):
                act.wait_ge(o2_full, 4 * c + 4)
                act.activation(ah[:, c, :], bank[2 + c % 2][:], ACT.Copy).then_inc(o2_hi, 1)

            for i in range(len(ITEMS2) + 3):
                if i >= 3:
                    copy_pt2(i - 3)
                if i < len(ITEMS2):
                    exp2(i)
                if i >= 8 and i % 4 == 0:
                    o2_high(i // 4 - 2)
            o2_high(KC - 1)

            def gates(first, col, done=0):
                for j in range(8):
                    if j >= done:
                        split(first + j + 1)
                    if j % 2:
                        continue
                    for half in range(2):
                        bi, m = bank_of(first + j, half), j + half
                        act.wait_ge(bank_full[bi], used(first + j) + 1)
                        if j:
                            act.wait_ge(bank_free[bank_of(first + j - 1, half)], used(first + j - 1) + 1)
                        act.activation(sg[:, half], bank[bi][:], ACT.Sigmoid, bias=vec[:, col + m:col + m + 1]).then_inc(bank_free[bi], 1)

            gates(FIRST["ga"], V_BGA)

            def head_exps(n):
                act.wait_ge(cum_full, n + 1)
                if n:
                    act.wait_ge(st_done, 7 * n)
                for e, (src, sgn) in enumerate(((5, 1.0), (5, -1.0), (6, 1.0), (7, 1.0))):
                    act.activation(ex[:, e], bank[src][:], ACT.Exp, scale=sgn).then_inc(ex_done, 1)

            def head_gate(n):
                b, half = g_block(n), n % 2
                act.wait_ge(bank_full[bank_of(b, half)], used(b) + 1)
                if n >= 2:
                    act.wait_ge(yh_ready, n - 1)
                act.activation(hg[:, n % 2], bank[bank_of(b, half)][:], ACT.Sigmoid, bias=vec[:, V_BHG + n:V_BHG + n + 1]).then_inc(bank_free[bank_of(b, half)], 1)

            def head_q(n):
                b = qf_block(n)
                act.wait_ge(bank_full[bank_of(b, 0)], used(b) + 1)
                if n:
                    act.wait_ge(bank_free[bank_of(b - 2, 0)], used(b - 2) + 1)
                act.activation(sgm[:], bank[bank_of(b, 0)][:], ACT.Sigmoid, bias=vec[:, V_BHQ + n:V_BHQ + n + 1]).then_inc(q_sig, 1)

            def head_turned(n):
                act.wait_ge(krt_full, n + 1)
                if n:
                    act.wait_ge(upd_full, n)
                act.activation(krt[:].rearrange("p a n -> p (a n)"), bank[4][:], ACT.Copy).then_inc(krt_copied, 1)

            def head_f(n):
                b = qf_block(n)
                bi = bank_of(b, 1)
                act.wait_ge(bank_full[bi], used(b) + 1)
                if n:
                    act.wait_ge(lft_full, n)
                act.activation(lf[:], bank[bi][:], ACT.Sigmoid, bias=vec[:, V_BHF + n:V_BHF + n + 1]).then_inc(f_sig, 1)
                if n >= 2:
                    act.wait_ge(kr_done, n - 1)
                act.activation(hk[:, n % 2], bank[bi][:], ACT.Sigmoid, bias=lbs[:, 2, n:n + 1], scale=-1.0).then_inc(bank_free[bi], 1)

            def head_lft(n):
                act.wait_ge(lft_full, n + 1)
                act.activation(lft[:].rearrange("p a n -> p (a n)"), bank[4][:], ACT.Copy).then_inc(lft_copied, 1)

            def head_log(n):
                act.wait_ge(f_lin, n + 1)
                act.activation(lf[:], lf[:], ACT.Ln).then_inc(f_log, 1)

            def head_norm(n):
                act.wait_ge(oh_full, n + 1)
                act.activation(osq[:], bank[5][:], ACT.Square).then_inc(osq_ready, 1)
                act.wait_ge(osum_full, n + 1)
                if n:
                    act.wait_ge(yh_ready, n)
                act.activation(ort[:], bank[4][:], ACT.Sqrt, bias=eps_col).then_inc(oroot_ready, 1)

            act.wait_ge(o2_lo, KC)
            for half in range(2):
                act.wait_ge(bank_free[bank_of(FIRST["ga"] + 7, half)], used(FIRST["ga"] + 7) + 1)
            for p in periods(2):
                if is_head(p - 2):
                    head_exps(p - 2)
                if p <= HG_HEADS:
                    split(qf_block(p) + 1)
                if p % 2 == 0 and p >= 2:
                    head_gate(p - 2)
                    head_gate(p - 1)
                if is_head(p):
                    head_q(p)
                if is_head(p - 2):
                    head_turned(p - 2)
                if is_head(p):
                    head_f(p)
                    split(qf_block(p) + 2)
                if is_head(p - 1):
                    head_lft(p - 1)
                if is_head(p):
                    head_log(p)
                if is_head(p - 2):
                    head_norm(p - 2)

            for k in range(KC):
                act.wait_ge(yh_ready, max(k + 1, HG_HEADS))
                act.activation(ah[:, k, :], yh[:, k, :], ACT.Copy).then_inc(y_hi, 1)
            gates(FIRST["gb"], V_BGB, done=1)
            wait_block(act, FIRST["wout2"] - 1)
            for k in range(KC):
                act.wait_ge(merged_ready, k + 1)
                act.activation(uh[:, k, :], merged[:, k, :], ACT.Copy).then_inc(m_hi, 1)
            for j in range(4):
                split(FIRST["wout2"] + j + 1)
                if j:
                    squares("ffn", h, (2 * j - 2, 2 * j - 1))
            squares("ffn", h, (6, 7))
            root("ffn")
            highs("ffn", None, uh)

            b0 = FIRST["ffn"]

            def gate_units(j, n, q=0, per=0, n_per=0):
                for half in range(2):
                    b = b0 + j
                    bi = bank_of(b, half)
                    act.wait_ge(bank_full[bi], used(b, q, per) + 1)
                    act.wait_ge(gz_ready, SQ0 + (n + half - 1 + n_per * q if per else n + half - 1))
                    act.activation(gs[:, half], bank[bi][:], ACT.Sigmoid).then_inc(gs_ready, 1)

            with act.Fori(0, 2) as q:
                for j in range(12):
                    split(b0 + j + 1, q, 12)
                    if j < 8 and j % 2 == 0:
                        gate_units(j, j, q, 12, 8)
            for j in range(10):
                if j < 9:
                    split(b0 + 24 + j + 1)
                if j < 6 and j % 2 == 0:
                    gate_units(24 + j, 16 + j)
                if j > 6:
                    squares("final", h, (2 * (j - 7), 2 * (j - 7) + 1))
            squares("final", h, (6, 7))
            root("final")

        @block.gpsimd
        def _(pool):
            def split(b, q=0, per=0):
                pool.wait_ge(split_hi, count(b, q, per) + 1)
                nk = chunks_of(b, per)
                pool.tensor_tensor(wl[:, b % 2, 0:nk], raw[:, b % RAW, 0:nk], f32(wh[:, b % 2, 0:nk]), ALU.subtract).then_inc(split_lo, 1)

            def add_squares(name, ks, n=S):
                i, sqs = NORM[name], norm_sqs(name)
                for k in ks:
                    if k == 0:
                        continue
                    pool.wait_ge(sq_ready, 8 * i + k + 1)
                    if k == 1:
                        if i:
                            pool.wait_ge(sum_full, i)
                        pool.tensor_tensor(sqs[:, 0:n], sq[:, 0, 0:n], sq[:, 1, 0:n], ALU.add).then_inc(sq_added, 1)
                    else:
                        pool.wait_ge(sq_added, 6 * i + k - 1)
                        pool.tensor_tensor(sqs[:, 0:n], sqs[:, 0:n], sq[:, k % 2, 0:n], ALU.add).then_inc(sq_added, 1)

            add_squares("x", range(7))
            split(0)
            add_squares("ctx", range(7), L)
            for b in range(1, 9):
                split(b)
            pool.wait_ge(cw_ready, 2)
            pool.memset(tm[:], 0.0).then_inc(tm_zero, 1)
            pool.wait_ge(tm_zero, 1)
            pool.wait_ge(tab_in, 16 * 17)
            for i, (hp, q, e) in enumerate(ITEMS):
                if i >= 2:
                    pool.wait_ge(smax, i - 1)
                pool.tensor_tensor(tm[:, i % 2, 0:256].rearrange("p (j c) -> p j c", c=WIN),
                                   tab[:, ROWS * (2 * hp + e):ROWS * (2 * hp + e) + ROWS, TOFF[q]:TOFF[q] + WIN],
                                   mask[:, TMASK[q], :].rearrange("p (j c) -> p j c", c=WIN), ALU.add).then_inc(tm_ready, 1)
            for b in range(8, 12):
                split(b + 1)
                if b > 8:
                    add_squares("mlp0", (2 * (b - 9), 2 * (b - 9) + 1))
            add_squares("mlp0", (6,))

            def mlp(layer, after):
                def group(q, last=False):
                    for j in range(8):
                        split(FIRST[f"mlp{layer}"] + j + 1, q, 8)
                        if last and j > 4:
                            add_squares(after, (2 * (j - 5), 2 * (j - 5) + 1))

                with pool.Fori(0, 3) as q:
                    group(q)
                group(3, True)
                add_squares(after, (6,))

            mlp(0, "pool")
            for b in range(FIRST["pool"], FIRST["pool"] + 4):
                split(b + 1)
            add_squares("mlp1", range(7))
            mlp(1, "mix2")
            for b in range(FIRST["aq"], FIRST["hgrn"]):
                split(b + 1)
            with pool.Fori(0, 4) as q:
                for j in range(4):
                    split(FIRST["hgrn"] + j + 1, q, 4)
            for b in range(FIRST["gb"], FIRST["ffn"]):
                split(b + 1)
                if b > FIRST["wout2"]:
                    k = 2 * (b - FIRST["wout2"] - 1)
                    add_squares("ffn", (k, k + 1))
            add_squares("ffn", (6,))
            with pool.Fori(0, 2) as q:
                for j in range(12):
                    split(FIRST["ffn"] + j + 1, q, 12)
            for j in range(10):
                if j < 9:
                    split(FIRST["ffn"] + 24 + j + 1)
                if j > 6:
                    add_squares("final", (2 * (j - 7), 2 * (j - 7) + 1))
            add_squares("final", (6,))

        @block.tensor
        def _(pe):
            def passes(out, ah_, al_, bh, bl, first, last):
                pe.matmul(out, ah_, bh, start=first, stop=False)
                pe.matmul(out, ah_, bl, start=False, stop=False)
                return pe.matmul(out, al_, bh, start=False, stop=last)

            def product(b, xh, xl, q=0, per=0, nk=KC, ready=None, after=None):
                pe.wait_ge(split_lo, count(b, q, per) + 1)
                order = [(k, half) for k in range(nk) for half in range(2)] if ready else [(k, half) for half in range(2) for k in range(nk)]
                for k, half in order:
                    bi = bank_of(b, half)
                    if k == 0 and (per or b >= 2):
                        pe.wait_ge(bank_free[bi], used(b, q, per))
                    if ready and not half:
                        ready(k)
                    w = slice(P * half, P * half + P)
                    last = passes(bank[bi][:], wh[:, b % 2, k, w], wl[:, b % 2, k, w], xh[:, k, :], xl[:, k, :], k == 0, k == nk - 1)
                    if k == nk - 1:
                        last.then_inc(bank_full[bi], 1)
                        if after:
                            after(half)

            def normed(name):
                return lambda k: pe.wait_ge(ulo_ready, 8 * NORM[name] + k + 1)

            def product_by_token(b, first=0, nk=KC, ready=None):
                pe.wait_ge(split_lo, b + 1)
                for half in range(2):
                    bi = bank_of(b, half)
                    if b >= 2:
                        pe.wait_ge(bank_free[bi], used(b))
                    for a in range(2):
                        tok = slice(P * (2 * half + a), P * (2 * half + a) + P)
                        for k in range(nk):
                            if ready and half == 0 and a == 0:
                                ready(first + k)
                            last = passes(bank[bi][:, BC * a:BC * a + BC], uh[:, first + k, tok], ul[:, first + k, tok], wh[:, b % 2, k, :], wl[:, b % 2, k, :], k == 0, k == nk - 1)
                    last.then_inc(bank_full[bi], 1)

            def norm_sum(name, n=S):
                i, (sums_, rms) = NORM[name], norm_banks(name)
                pe.wait_ge(sq_added, 6 * i + 6)
                for a in range(n // P):
                    pe.matmul(sums_[:, a:a + 1], norm_sqs(name)[:, P * a:P * a + P], ones_d[:, 0:1], start=(a == 0), stop=False, skip_group_check=True)
                pe.wait_ge(sq_ready, 8 * i + 8)
                for a in range(n // P):
                    last = pe.matmul(sums_[:, a:a + 1], sq[:, 1, P * a:P * a + P], ones_d[:, 0:1], start=False, stop=(a == n // P - 1), skip_group_check=True)
                last.then_inc(sum_full, 1)
                pe.wait_ge(diag_ready, i + 1)
                pe.matmul(rms[:, 0:n], ones_d, diag[:, 0:n // P, :].rearrange("p a n -> p (a n)"), start=True, stop=True).then_inc(rms_full, 1)

            def mod_columns(m, q=0, per=0):
                if per or m:
                    pe.wait_ge(mcol_used, count(m, q, per))
                mod_summed(pe, m, q, per)
                for a in range(2):
                    last = pe.matmul(bank[7][:, a:a + 1], acc[:, m % 2, P * a:P * a + P], one_col, start=True, stop=True)
                last.then_inc(mcol_full, 1)

            pe.wait_ge(const_in, 48)
            pe.wait_ge(csil_ready, 1)
            for i in range(8):
                if i == 4:
                    norm_sum("x")
                pe.wait_ge(modf_in[i], 16)
                for k in range(KC):
                    last = pe.matmul(bank[4 + i // 2][0:2, BC * (i % 2):BC * (i % 2) + BC], csil[:, k, :], modf[:, i, k, :], start=(k == 0), stop=(k == KC - 1))
                last.then_inc(modrow_full, 1)
            for j in range(16):
                if j % 4 == 0:
                    pe.wait_ge(modrow_copied, j // 4 + 1)
                last = pe.matmul(bank[0][:, 2 * j:2 * j + 2], modrow[0:2, P * j:P * j + P], ident[0:2, 0:2], start=True, stop=True)
            last.then_inc(mod0_full, 1)

            def head_sum(i):
                pe.wait_ge(hsq_ready, i + 1)
                if i:
                    pe.wait_ge(hroot_ready, i)
                pe.matmul(bank[6][:], ones_h, sq[:, i % 2], start=True, stop=True).then_inc(hsum_full, 1)

            product_by_token(0, ready=normed("x"))
            norm_sum("ctx", L)
            product_by_token(1)
            pe.wait_ge(ulo_ready, 16)
            def beside(b):
                def after(half):
                    if (b, half) in HN_AFTER:
                        head_sum(HN_AFTER[b, half])
                    if half == 0:
                        mod_columns(b - 1)
                return after

            for b in range(2):
                for a in range(2):
                    tok = slice(P * a, P * a + P)
                    for k in range(KC):
                        last = passes(bank[4 + b][:, BC * a:BC * a + BC], uch[:, k, tok], ucl[:, k, tok], wh[:, b % 2, k, :], wl[:, b % 2, k, :], k == 0, k == KC - 1)
                last.then_inc(ctx_full, 1)
            mod_columns(0)
            for b in range(2, 8):
                pe.wait_ge(split_lo, b + 1)
                if b < 4:
                    pe.wait_ge(ctx_free, b - 1)
                    for half in range(2):
                        w = slice(P * half, P * half + P)
                        for k in range(KC):
                            last = passes(bank[2 + b][:, L * half:L * half + L], wh[:, b % 2, k, w], wl[:, b % 2, k, w], uch[:, k, :], ucl[:, k, :], k == 0, k == KC - 1)
                    last.then_inc(ctx_full, 1)
                    beside(b)(-1)
                product(b, uh, ul, after=beside(b))
            mod_columns(PROJ - 1)

            pe.wait_ge(w4_in, 32)
            pe.wait_ge(ctx_free, 4)
            for g in range(FG):
                for a in range(2):
                    last = pe.matmul(bank[4 + g // 2][:, 2 * P * (g % 2) + P * a:2 * P * (g % 2) + P * a + P], cs[:, P * a:P * a + P], w4[:, g, :], start=True, stop=True)
                if g % 2:
                    last.then_inc(cw_full, 1)

            def fourier_y(g):
                if g == 0:
                    pe.wait_ge(bank_free[bank_of(7, 0)], used(7) + 1)
                    pe.wait_ge(bank_free[bank_of(7, 1)], used(7) + 1)
                    pe.wait_ge(cw_ready, 2)
                    pe.wait_ge(hroot_ready, 10)
                    pe.wait_ge(mcol_used, PROJ)
                for i in range(4):
                    if i % 2 == 0 and g:
                        pe.wait_ge(y_ready, 2 * g - 1 + i // 2)
                    last = pe.matmul(bank[6 + i // 2][:, 2 * P * (i % 2):2 * P * (i % 2) + 2 * P], fT[:, g, P * i:P * i + P], cw[:, g, :], start=True, stop=True)
                    if i % 2:
                        last.then_inc(y_full, 1)

            def fourier_out(g):
                if g == 0:
                    pe.wait_ge(dft_in, 32)
                if g >= 2:
                    pe.wait_ge(four_lo, g - 1)
                pe.wait_ge(y_ready, 2 * g + 2)
                for i in range(4):
                    pe.matmul(bank[4 + g % 2][:], ysb[:, i, 0:P], dftc[:, i, :], start=(i == 0), stop=False)
                    last = pe.matmul(bank[4 + g % 2][:], ysb[:, i, P:2 * P], dfts[:, i, :], start=False, stop=(i == 3))
                last.then_inc(four_full, 1)

            for g in range(FG):
                fourier_y(g)
                fourier_out(g)

            def scores(i):
                hp, w, e = ITEMS[i]
                r = slice(64 * e, 64 * e + 64)
                if i < 2:
                    pe.wait_ge(four_lo, 3 + i)
                    for n in range(len(HN)):
                        hn_wait_done(pe, n)
                else:
                    pe.wait_ge(smax, i - 1)
                qv = qT[r, hp, P * w:P * w + P]
                pe.matmul(bank[4 + i % 2][:, 0:256], qv, by_column(kT[r, hp, :], W0[w], WIN), start=True, stop=True)
                pe.matmul(bank[4 + i % 2][:, 256:512], qv, kcT[r, hp, :], start=True, stop=True).then_inc(s_full, 1)

            def turn(i):
                pe.wait_ge(p_norm, i + 1)
                if i < 2:
                    pe.wait_ge(y_ready, 8)
                else:
                    pe.wait_ge(pt_copied, i - 1)
                for c in range(4):
                    last = pe.transpose(bank[6 + i % 2][:, P * c:P * c + P], pn[:, i % 2, P * c:P * c + P], ident)
                last.then_inc(pt_full, 1)

            def values(i):
                hp, w, e = ITEMS[i]
                hd = slice(64 * (2 * hp + e), 64 * (2 * hp + e) + 64)
                if i == 0:
                    pe.wait_ge(vwin_in, 16 * 32)
                if i % 8 == 0 and hp >= 2:
                    pe.wait_ge(o_lo, hp - 1)
                pe.wait_ge(pt_copied, i + 1)
                for c in range(4):
                    v = vwin[:, 2 * w + c, hd] if c < 2 else vc[:, c - 2, hd]
                    last = pe.matmul(bank[2 + hp % 2][64 * e:64 * e + 64, P * w:P * w + P], v, pT[:, i % 2, P * c:P * c + P], start=(c == 0), stop=(c == 3))
                last.then_inc(o_full, 1)

            for i in range(len(ITEMS) + 4):
                if i < len(ITEMS):
                    scores(i)
                if i >= 4:
                    values(i - 4)
                if 2 <= i <= len(ITEMS) + 1:
                    turn(i - 2)
            pe.wait_ge(o_lo, 4)
            for b in range(8, 12):
                product(b, uh, ul, after=lambda half: mod_columns(PROJ + 2 * (b - 8) + half))

            def mlp(layer):
                b0, i = FIRST[f"mlp{layer}"], NORM[f"mlp{layer}"]
                with pe.Fori(0, 4) as q:
                    for j in range(8):
                        if j < 4:
                            product(b0 + j, uh, ul, q, 8, ready=normed(f"mlp{layer}") if j == 0 else None)
                        else:
                            product(b0 + j, ah, al, q, 8,
                                    ready=(lambda k: pe.wait_ge(a_lo, SQ0 + 32 * layer + k + 1 + 8 * q)) if j == 4 else None)
                        if layer == 0 and j < 6:
                            mod_columns(MOD0 + j, q, 6)

            norm_sum("mlp0")
            mlp(0)

            norm_sum("pool")
            b0 = FIRST["pool"]
            for g in range(FG):
                product_by_token(b0 + g, first=2 * g, nk=2, ready=normed("pool"))
            pe.wait_ge(band_in, 16)
            for m in range(KC):
                g = m // 2
                if m % 2 == 0:
                    for half in range(2):
                        bi = bank_of(b0 + g, half)
                        pe.wait_ge(bank_free[bi], used(b0 + g) + 1)
                if m >= 2:
                    pe.wait_ge(yp_free, m - 1)
                w = slice(P * (m % 2), P * (m % 2) + P)
                for i in range(4):
                    lo, hi = max(0, P * i - 8), min(S, P * i + P + 8)
                    kind = 0 if i == 0 else 2 if i == 3 else 1
                    r = lo - (P * i - 8)
                    last = pe.matmul(bank[4 + m % 2][:, lo:hi], zt[:, g, i, w], band[:, kind, g, r:r + hi - lo],
                                     start=(i == 0), stop=(i == 3), skip_group_check=True)
                last.then_inc(yp_full, 1)
            norm_sum("mlp1")
            mlp(1)

            norm_sum("mix2")
            b0 = FIRST["aq"]
            for j in range(4):
                product(b0 + j, uh, ul, ready=normed("mix2") if j == 0 else None)

            def half_and_half(b, first_by_token, q=0, per=0):
                pe.wait_ge(split_lo, count(b, q, per) + 1)
                for half in range(2):
                    bi = bank_of(b, half)
                    w = slice(P * half, P * half + P)
                    pe.wait_ge(bank_free[bi], used(b, q, per))
                    if half == (0 if first_by_token else 1):
                        for a in range(4):
                            tok = slice(P * a, P * a + P)
                            for k in range(KC):
                                last = passes(bank[bi][:, P * a:P * a + P], uh[:, k, tok], ul[:, k, tok], wh[:, b % 2, k, w], wl[:, b % 2, k, w], k == 0, k == KC - 1)
                    else:
                        for k in range(KC):
                            last = passes(bank[bi][:], wh[:, b % 2, k, w], wl[:, b % 2, k, w], uh[:, k, :], ul[:, k, :], k == 0, k == KC - 1)
                    last.then_inc(bank_full[bi], 1)

            half_and_half(b0 + 4, False)

            def scores2(i):
                c, n = ITEMS2[i]
                if i == 0:
                    for b in range(b0, b0 + 5):
                        for half in range(2):
                            pe.wait_ge(bank_free[bank_of(b, half)], used(b) + 1)
                if i >= 2:
                    pe.wait_ge(smax2, 2 * (i - 1))
                ks = P * max(0, n - 1)
                for e in range(2):
                    r = slice(64 * e, 64 * e + 64)
                    last = pe.matmul(bank[S2_BANKS[i % 2][e]][:, 0:256], aqT[r, c, P * n:P * n + P], akT[r, ks:ks + 256], start=True, stop=True)
                last.then_inc(s2_full, 1)

            def turn2(i):
                pe.wait_ge(p2_norm, 2 * (i + 1))
                if i >= 2:
                    pe.wait_ge(pt2_copied, i - 1)
                for c in range(4):
                    last = pe.transpose(bank[6 + i % 2][:, P * c:P * c + P], pn2[:, i % 2, P * c:P * c + P], ident)
                last.then_inc(pt2_full, 1)

            def values2(i):
                c, n = ITEMS2[i]
                if n == 0 and c >= 2:
                    pe.wait_ge(o2_lo, c - 1)
                pe.wait_ge(pt2_copied, i + 1)
                for e in range(2):
                    for a in range(2):
                        last = pe.matmul(bank[2 + c % 2][64 * e:64 * e + 64, P * n:P * n + P], av[:, max(0, n - 1) + a, 64 * e:64 * e + 64],
                                         pT2[:, i % 2, P * (2 * e + a):P * (2 * e + a) + P], start=(a == 0), stop=(a == 1))
                last.then_inc(o2_full, 1)

            for i in range(len(ITEMS2) + 4):
                if i < len(ITEMS2):
                    scores2(i)
                if i >= 4:
                    values2(i - 4)
                if 2 <= i <= len(ITEMS2) + 1:
                    turn2(i - 2)
            pe.wait_ge(o2_lo, KC)
            for j in range(8):
                if j % 2 == 0:
                    product(FIRST["ga"] + j, uh, ul)
                else:
                    product(FIRST["ga"] + j, ah, al)

            def turn_log(n):
                pe.wait_ge(f_log, n + 1)
                if n:
                    pe.wait_ge(krt_copied, n)
                for a in range(4):
                    last = pe.transpose(bank[4][:, P * a:P * a + P], lf[:, P * a:P * a + P], ident)
                last.then_inc(lft_full, 1)

            def sums(n):
                pe.wait_ge(lft_copied, n + 1)
                if n:
                    pe.wait_ge(on_ready, n)
                    pe.wait_ge(osq_ready, n)
                for e in range(3):
                    for a in range(4):
                        last = pe.matmul(bank[5 + e][:, P * a:P * a + P], lft[:, a, :], cm[:, e, :], start=True, stop=True)
                last.then_inc(cum_full, 1)

            def attend(n):
                pe.wait_ge(qd_done, n + 1)
                pe.wait_ge(kd_done, n + 1)
                pe.wait_ge(ex_done, 4 * n + 4)
                for a in range(4):
                    w = slice(P * a, P * a + P)
                    last = pe.matmul(bank[5][:, w], ex[:, 1, w], ex[:, 0, w], start=True, stop=True)
                last.then_inc(att_full, 1)
                pe.wait_ge(kr_done, n + 1)
                if n:
                    pe.wait_ge(oroot_ready, n)
                for a in range(4):
                    last = pe.transpose(bank[4][:, P * a:P * a + P], ex[:, 3, P * a:P * a + P], ident)
                last.then_inc(krt_full, 1)

            def updates(n):
                pe.wait_ge(krt_copied, n + 1)
                for half in range(2):
                    pe.wait_ge(bank_free[bank_of(v_block(n), half)], used(v_block(n)) + 1)
                for j in range(8):
                    r = slice(64 * (j % 2), 64 * (j % 2) + 64)
                    last = pe.matmul(bank[6 + j % 2][:, P * (j // 2):P * (j // 2) + P], krt[r, j // 2, :],
                                     hv[r, n // 2 % 2, j // 2, P * (n % 2):P * (n % 2) + P], start=True, stop=True)
                last.then_inc(upd_full, 1)

            def outputs(n):
                pe.wait_ge(att_done, n + 1)
                pe.wait_ge(qb_done, n + 1)
                pe.wait_ge(st_done, 7 * n + 7)
                for a in range(4):
                    w = slice(P * a, P * a + P)
                    pe.matmul(bank[5][:, w], hv[:, n // 2 % 2, a, P * (n % 2):P * (n % 2) + P], att[:, w], start=True, stop=False)
                    for j in (2 * a, 2 * a + 1):
                        c = slice(64 * j, 64 * j + 64)
                        last = pe.matmul(bank[5][:, c], st[:, j, :], qb[:, c], start=False, stop=(j % 2 == 1))
                last.then_inc(oh_full, 1)

            def out_sum(n):
                pe.wait_ge(osq_ready, n + 1)
                if is_head(n + 1):
                    pe.wait_ge(lft_copied, n + 2)
                pe.matmul(bank[4][:], ones_v, osq[:], start=True, stop=True).then_inc(osum_full, 1)

            def unit(b, half):
                pe.wait_ge(split_lo, b + 1)
                bi = bank_of(b, half)
                pe.wait_ge(bank_free[bi], used(b))
                if (b - FIRST["hgrn"]) % 4 == 1:
                    for a in range(2):
                        tok = slice(P * (2 * half + a), P * (2 * half + a) + P)
                        for k in range(KC):
                            last = passes(bank[bi][:, BC * a:BC * a + BC], uh[:, k, tok], ul[:, k, tok], wh[:, b % 2, k, :], wl[:, b % 2, k, :], k == 0, k == KC - 1)
                else:
                    w = slice(P * half, P * half + P)
                    for k in range(KC):
                        last = passes(bank[bi][:], wh[:, b % 2, k, w], wl[:, b % 2, k, w], uh[:, k, :], ul[:, k, :], k == 0, k == KC - 1)
                last.then_inc(bank_full[bi], 1)

            pe.wait_ge(hg_in, 48)
            for p in periods(2):
                b = qf_block(p)
                if p <= HG_HEADS:
                    unit(b, 0)
                if is_head(p - 2):
                    attend(p - 2)
                if p <= HG_HEADS:
                    unit(b, 1)
                if is_head(p - 2):
                    updates(p - 2)
                if is_head(p - 1):
                    turn_log(p - 1)
                if is_head(p):
                    unit(b + 1, 0)
                if is_head(p - 2):
                    outputs(p - 2)
                if is_head(p):
                    unit(b + 1, 1)
                if is_head(p - 2):
                    out_sum(p - 2)
                if is_head(p - 1):
                    sums(p - 1)
            for j in range(1, 8):
                if j % 2 == 0:
                    product(FIRST["gb"] + j, uh, ul)
                else:
                    product(FIRST["gb"] + j, ah, al, ready=(lambda k: pe.wait_ge(y_lo, k + 1)) if j == 1 else None)
            for j in range(4):
                product(FIRST["wout2"] + j, uh, ul, ready=(lambda k: pe.wait_ge(m_lo, k + 1)) if j == 0 else None)
            norm_sum("ffn")
            b0 = FIRST["ffn"]
            with pe.Fori(0, 2) as q:
                for j in range(12):
                    if j < 8:
                        product(b0 + j, uh, ul, q, 12, ready=normed("ffn") if j == 0 else None)
                    else:
                        product(b0 + j, ah, al, q, 12, ready=(lambda k: pe.wait_ge(z_lo, k + 1 + 8 * q)) if j == 8 else None)
            for j in range(10):
                if j < 6:
                    product(b0 + 24 + j, uh, ul)
                else:
                    product(b0 + 24 + j, ah, al, nk=6, ready=(lambda k: pe.wait_ge(z_lo, 16 + k + 1)) if j == 6 else None)
            norm_sum("final")

        @block.vector
        def _(dve):
            def norm_factor(name, n=S):
                i, c = NORM[name], n // P
                dve.wait_ge(root_ready, i + 1)
                dve.reciprocal(rc[:, 1, 0:c], rc[:, 0, 0:c]).then_inc(rstd_ready, 1)
                dve.wait_ge(rstd_ready, i + 1)
                dve.scalar_tensor_tensor(diag[:, 0:c, :], ident.rearrange("p (a n) -> p a n", a=1).to_broadcast([P, c, P]), float(D),
                                         rc[:, 1, 0:c].rearrange("p (a n) -> p a n", n=1).to_broadcast([P, c, P]), ALU.mult, ALU.mult).then_inc(diag_ready, 1)

            def norm(name, src, gain, shift, hi, lo, n=S):
                i, rms = NORM[name], norm_banks(name)[1]
                dve.wait_ge(rms_full, i + 1)

                def scaled(k):
                    if k >= 2:
                        dve.wait_ge(ulo_ready, 8 * i + k - 1)
                    dve.scalar_tensor_tensor(tt[:, k % 2, 0:n], src[:, k, :], gain(k), rms[:, 0:n], ALU.mult, ALU.mult).then_inc(t_ready, 1)

                def low(k):
                    dve.wait_ge(uhi_ready, 8 * i + k + 1)
                    if shift is None:
                        ins = dve.tensor_tensor(lo[:, k, :], tt[:, k % 2, 0:n], f32(hi[:, k, :]), ALU.subtract)
                    else:
                        ins = dve.scalar_tensor_tensor(lo[:, k, :], tt[:, k % 2, 0:n], shift(k), f32(hi[:, k, :]), ALU.add, ALU.subtract)
                    ins.then_inc(ulo_ready, 1)

                for k in range(KC + 1):
                    if k < KC:
                        scaled(k)
                    if k:
                        low(k - 1)

            def gain_of(n, scale, g):
                dve.scalar_tensor_tensor(gm[:, n, :], scale, 1.0, g, ALU.add, ALU.mult).then_inc(gain_ready, 1)
                dve.wait_ge(gain_ready, n + 1)

            def mod_sum(m, q=0, per=0):
                n = 8 * m + 8 * per * q if per else 8 * m
                dve.wait_ge(mraw_full[m % 2], 16 * (m // 2 + 1) + 8 * per * q if per else 16 * (m // 2 + 1))
                if per or m >= 2:
                    dve.wait_ge(mcol_full, count(m - 1, q, per))
                dve.tensor_scalar(acc[:, m % 2], mraw[:, m % 2, 0], csil[:, 0, 0:1], None, ALU.mult).then_inc(macc, 1)
                for k in range(1, KC):
                    dve.wait_ge(macc, n + k)
                    dve.scalar_tensor_tensor(acc[:, m % 2], mraw[:, m % 2, k], csil[:, k, 0:1], acc[:, m % 2], ALU.mult, ALU.add).then_inc(macc, 1)

            def mod_store(m, q=0, per=0):
                dve.wait_ge(mcol_full, count(m + 1, q, per))
                c = 16 + 2 * m
                if per:
                    c = c + 2 * per * q
                    out, b = modc[:, bass.ds(c, 2)], bmod[:, bass.ds(c, 2)]
                else:
                    out, b = modc[:, c:c + 2], bmod[:, c:c + 2]
                dve.tensor_tensor(out, bank[7][:, 0:2], b, ALU.add).then_inc(mcol_used, 1)

            dve.wait_ge(const_in, 48)
            norm_factor("x")
            for i in range(4):
                dve.wait_ge(modrow_full, 2 * i + 2)
                dve.tensor_copy(modrow[0:2, S * i:S * i + S], bank[4 + i][0:2, :]).then_inc(modrow_copied, 1)
            dve.wait_ge(mod0_full, 1)
            both = bank[0][:, 0:32].rearrange("p (j a) -> p j a", a=2)
            dve.tensor_tensor(modc[:, 0:16], both[:, :, 0], bmod[:, 0:16], ALU.add).then_inc(mod0_ready, 1)
            dve.tensor_tensor(modx[:, :], both[:, :, 1], bmod[:, 0:16], ALU.add).then_inc(mod0_ready, 1)
            dve.wait_ge(mod0_ready, 2)
            gain_of(0, modc[:, 8:16], vec[:, V_G1:V_G1 + 8])
            gain_of(1, modx[:, 8:16], vec[:, V_G1:V_G1 + 8])
            norm("x", h, lambda k: gm[:, 0, k:k + 1], lambda k: mod(0, 0, k), uh, ul)
            norm_factor("ctx", L)
            norm("ctx", ctxT, lambda k: gm[:, 1, k:k + 1], lambda k: modx[:, k:k + 1], uch, ucl, L)

            def hn_scale(i):
                src, free, out = hn_place(i)
                dve.wait_ge(hroot_ready, i + 1)
                dve.reciprocal(tt[:, i % 2], tt[:, i % 2]).then_inc(hrstd_ready, 1)
                dve.wait_ge(hrstd_ready, i + 1)
                if HN[i][0] != "q":
                    dve.scalar_tensor_tensor(out, src, vec[:, V_KG:V_KG + 1], tt[:, i % 2], ALU.mult, ALU.mult).then_inc(free, 1)
                    return
                for w in range(QT):
                    last = dve.scalar_tensor_tensor(out[:, P * w:P * w + P].rearrange("p (r c) -> p r c", c=QC), by_column(src, QC * w, QC),
                                                    vec[:, V_QG:V_QG + 1], by_column(tt[:, i % 2], QC * w, QC), ALU.mult, ALU.mult)
                last.then_inc(free, 1)

            mod_sum(0)
            mod_sum(1)
            mod_store(0)
            mod_sum(2)
            for b in range(2, 8):
                for half in (-1, 0, 1):
                    if half == 0:
                        mod_store(b - 1)
                    if (b, half) in HN_AFTER:
                        hn_scale(HN_AFTER[b, half])
                    if half == 0 and b + 1 < PROJ:
                        mod_sum(b + 1)
            mod_store(PROJ - 1)
            for a in range(2):
                dve.wait_ge(cw_full, a + 1)
                dve.tensor_copy(cw[:, 2 * a:2 * a + 2, :].rearrange("p a n -> p (a n)"), bank[4 + a][:]).then_inc(cw_ready, 1)
            for g in range(FG):
                dve.wait_ge(four_hi, g + 1)
                dve.tensor_tensor(ul[:, g, :], bank[4 + g % 2][:], f32(uh[:, g, :]), ALU.subtract).then_inc(four_lo, 1)

            def row_max(i):
                dve.wait_ge(s_full, i + 1)
                dve.wait_ge(tm_ready, i + 1)
                if i < 2:
                    dve.wait_ge(four_full, 4)
                else:
                    dve.wait_ge(p_norm, i - 1)
                dve.tensor_tensor_reduce(sc[:, i % 2], bank[4 + i % 2][:], tm[:, i % 2], 1.0, -3e38, ALU.add, ALU.max, stat[:, 0, i % 2:i % 2 + 1]).then_inc(smax, 1)
                dve.wait_ge(smax, i + 1)
                dve.tensor_scalar(stat[:, 1, i % 2:i % 2 + 1], stat[:, 0, i % 2:i % 2 + 1], -1.0, None, ALU.mult).then_inc(nmax, 1)

            def normalise(i):
                dve.wait_ge(p_exp, i + 1)
                dve.reciprocal(stat[:, 3, i % 2:i % 2 + 1], stat[:, 2, i % 2:i % 2 + 1]).then_inc(p_recip, 1)
                dve.wait_ge(p_recip, i + 1)
                if i >= 2:
                    dve.wait_ge(pt_full, i - 1)
                dve.tensor_scalar(pn[:, i % 2], sc[:, i % 2], stat[:, 3, i % 2:i % 2 + 1], None, ALU.mult).then_inc(p_norm, 1)

            def o_low(hp):
                dve.wait_ge(o_hi, hp + 1)
                for w in range(QT):
                    out = by_column(ul[:, 4 + hp, :], QC * w, QC)
                    src = bank[2 + hp % 2][:, P * w:P * w + P].rearrange("p (r c) -> p r c", c=QC)
                    last = dve.tensor_tensor(out, src, by_column(f32(uh[:, 4 + hp, :]), QC * w, QC), ALU.subtract)
                last.then_inc(o_lo, 1)

            for i in range(len(ITEMS) + 1):
                if i < len(ITEMS):
                    row_max(i)
                if i >= 1:
                    normalise(i - 1)
                if i >= 8 and i % 8 == 5:
                    o_low(i // 8 - 1)
            o_low(3)

            def add_to_h(b, m, gate, q=0, per=0):
                bi = bank_of(b, m % 2)
                dve.wait_ge(bank_full[bi], used(b, q, per) + 1)
                if gate is None:
                    ins = dve.tensor_tensor(h[:, m, :], bank[bi][:], h[:, m, :], ALU.add)
                else:
                    ins = dve.scalar_tensor_tensor(h[:, m, :], bank[bi][:], gate, h[:, m, :], ALU.mult, ALU.add)
                ins.then_inc(bank_free[bi], 1)

            mod_sum(PROJ)
            mod_sum(PROJ + 1)
            for b in range(8, 12):
                for half in range(2):
                    m = PROJ + 2 * (b - 8) + half
                    add_to_h(b, 2 * (b - 8) + half, mod(0, 2, 2 * (b - 8) + half), 0)
                    mod_store(m)
                    if m + 2 < MOD0:
                        mod_sum(m + 2)
            dve.wait_ge(mcol_used, MOD0)
            gain_of(2, modc[:, 32:40], vec[:, V_G2:V_G2 + 8])

            def mlp(layer):
                b0, n0 = FIRST[f"mlp{layer}"], 32 * layer
                with dve.Fori(0, 4) as q:
                    for j in range(8):
                        if layer == 0 and j < 6:
                            mod_sum(MOD0 + j, q, 6)
                        for half in range(2):
                            m = 2 * (j % 4) + half
                            if j >= 4:
                                add_to_h(b0 + j, m, mod(layer, 5, m), q, 8)
                                continue
                            bi = bank_of(b0 + j, half)
                            dve.wait_ge(bank_free[bi], used(b0 + j, q, 8) + 1)
                            dve.wait_ge(a_lo, SQ0 + n0 + m - 1 + 8 * q)
                            dve.tensor_tensor(v1[:, m % 2], r1[:, m % 2], r1[:, m % 2], ALU.mult).then_inc(square_ready, 1)
                            dve.wait_ge(square_ready, SQ0 + n0 + m + 1 + 8 * q)
                            dve.tensor_copy(ah[:, m], v1[:, m % 2]).then_inc(a_hi, 1)
                            dve.wait_ge(a_hi, n0 + m + 1 + 8 * q)
                            dve.tensor_tensor(al[:, m], v1[:, m % 2], f32(ah[:, m]), ALU.subtract).then_inc(a_lo, 1)
                        if layer == 0 and j < 6:
                            mod_store(MOD0 + j, q, 6)

            norm_factor("mlp0")
            norm("mlp0", h, lambda k: gm[:, 2, k:k + 1], lambda k: mod(0, 3, k), uh, ul)
            dve.memset(stat[:, 4, 0:1], 0.0).then_inc(square_ready, SQ0)
            dve.memset(stat[:, 4, 1:2], 0.0).then_inc(a_lo, SQ0)
            mlp(0)

            gain_of(3, modc[:, 56:64], vec[:, V_G1 + 8:V_G1 + 16])
            gain_of(4, modc[:, 80:88], vec[:, V_G2 + 8:V_G2 + 16])
            dve.tensor_tensor(gm[:, 5, :], modc[:, 64:72], vec[:, V_PS:V_PS + 8], ALU.mult).then_inc(gain_ready, 1)
            norm_factor("pool")
            norm("pool", h, lambda k: gm[:, 3, k:k + 1], lambda k: mod(1, 0, k), uh, ul)
            dve.wait_ge(gain_ready, 6)
            for m in range(KC):
                dve.wait_ge(yp_full, m + 1)
                dve.scalar_tensor_tensor(h[:, m, :], bank[4 + m % 2][:], gm[:, 5, m:m + 1], h[:, m, :], ALU.mult, ALU.add).then_inc(yp_free, 1)
            norm_factor("mlp1")
            norm("mlp1", h, lambda k: gm[:, 4, k:k + 1], lambda k: mod(1, 3, k), uh, ul)
            mlp(1)

            dve.tensor_tensor(lbs[:, 0, :], vec[:, V_LB:V_LB + 8], vec[:, V_LB + 8:V_LB + 16], ALU.subtract).then_inc(lb_ready, 1)
            dve.tensor_scalar(lbs[:, 2, :], vec[:, V_BHF:V_BHF + 8], -1.0, None, ALU.mult).then_inc(lb_ready, 1)
            norm_factor("mix2")
            norm("mix2", h, lambda k: vec[:, V_MIX + k:V_MIX + k + 1], None, uh, ul)
            dve.wait_ge(lb_ready, 3)
            dve.tensor_scalar(lbs[:, 1, :], lbs[:, 0, :], -1.0, 1.0, ALU.mult, ALU.add).then_inc(lb_ready, 1)
            b = FIRST["aq"] + 4
            dve.wait_ge(b2_in, 32)
            dve.wait_ge(bank_full[bank_of(b, 1)], used(b) + 1)
            dve.tensor_tensor(av[:], bank[bank_of(b, 1)][:].rearrange("p (a n) -> p a n", a=4),
                              bvrow[:].rearrange("p (a n) -> p a n", a=1).to_broadcast([P, 4, P]), ALU.add).then_inc(bank_free[bank_of(b, 1)], 1)
            sinks = vec[:, V_SINK:V_SINK + 16].rearrange("p (e c) -> p c e", e=2)

            def row_max2(i):
                c, n = ITEMS2[i]
                dve.wait_ge(s2_full, i + 1)
                if i >= 2:
                    dve.wait_ge(p2_norm, 2 * (i - 1))
                    dve.wait_ge(p2_exp, 3 * (i - 1))
                for e in range(2):
                    w = slice(256 * e, 256 * e + 256)
                    dve.tensor_tensor_reduce(sc2[:, i % 2, w], bank[S2_BANKS[i % 2][e]][:, 0:256], wmask[:, min(n, 1), :], DH ** -0.5, sinks[:, c, e:e + 1],
                                             ALU.add, ALU.max, stat[:, 3 + 10 * (i % 2), e:e + 1]).then_inc(smax2, 1)
                dve.wait_ge(smax2, 2 * i + 2)
                dve.tensor_scalar(stat[:, 4 + 10 * (i % 2), :], stat[:, 3 + 10 * (i % 2), :], -1.0, None, ALU.mult).then_inc(nmax2, 1)
                dve.wait_ge(nmax2, i + 1)
                dve.tensor_tensor(stat[:, 5 + 10 * (i % 2), :], stat[:, 4 + 10 * (i % 2), :], sinks[:, c, :], ALU.add).then_inc(sink_ready, 1)

            def total2(i):
                dve.wait_ge(p2_exp, 3 * i + 3)
                dve.tensor_tensor(stat[:, 8 + 10 * (i % 2), :], stat[:, 7 + 10 * (i % 2), :], stat[:, 6 + 10 * (i % 2), :], ALU.add).then_inc(tot2, 1)
                dve.wait_ge(tot2, i + 1)
                dve.reciprocal(stat[:, 9 + 10 * (i % 2), :], stat[:, 8 + 10 * (i % 2), :]).then_inc(p2_recip, 1)
                dve.wait_ge(p2_recip, i + 1)
                if i >= 2:
                    dve.wait_ge(pt2_full, i - 1)
                for e in range(2):
                    w = slice(256 * e, 256 * e + 256)
                    dve.tensor_scalar(pn2[:, i % 2, w], sc2[:, i % 2, w], stat[:, 9 + 10 * (i % 2), e:e + 1], None, ALU.mult).then_inc(p2_norm, 1)

            def o2_low(c):
                dve.wait_ge(o2_hi, c + 1)
                dve.tensor_tensor(al[:, c, :], bank[2 + c % 2][:], f32(ah[:, c, :]), ALU.subtract).then_inc(o2_lo, 1)

            for i in range(len(ITEMS2) + 1):
                if i < len(ITEMS2):
                    row_max2(i)
                if i >= 1:
                    total2(i - 1)
                if i >= 8 and i % 4 == 1:
                    o2_low(i // 4 - 2)
            o2_low(KC - 2)
            o2_low(KC - 1)

            def branches(first, second):
                for j in range(1, 8, 2):
                    for half in range(2):
                        b, m = first + j, j - 1 + half
                        bi = bank_of(b, half)
                        dve.wait_ge(bank_full[bi], used(b) + 1)
                        dve.wait_ge(bank_free[bank_of(b - 1, half)], used(b - 1) + 1)
                        out = mt[:, half] if second else merged[:, m, :]
                        if second and m >= 2:
                            dve.wait_ge(merged_ready, m - 1)
                        dve.tensor_tensor(out, bank[bi][:], sg[:, half], ALU.mult).then_inc(bank_free[bi], 1)
                        if second:
                            dve.wait_ge(bank_free[bi], used(b) + 1)
                            dve.tensor_tensor(merged[:, m, :], merged[:, m, :], mt[:, half], ALU.add).then_inc(merged_ready, 1)

            branches(FIRST["ga"], False)

            def head_out(n):
                b = g_block(n)
                dve.wait_ge(on_ready, n + 1)
                dve.wait_ge(bank_free[bank_of(b, n % 2)], used(b) + 1)
                dve.tensor_tensor(onum[:], onum[:], hg[:, n % 2], ALU.mult).then_inc(on_gated, 1)
                dve.wait_ge(oroot_ready, n + 1)
                dve.reciprocal(ort[:], ort[:]).then_inc(orstd_ready, 1)
                dve.wait_ge(orstd_ready, n + 1)
                dve.wait_ge(on_gated, n + 1)
                dve.tensor_tensor(yh[:, n, :], onum[:], ort[:], ALU.mult).then_inc(yh_ready, 1)

            def head_decay(n):
                s = n % 2
                dve.wait_ge(k_done, n + 1)
                dve.wait_ge(ex_done, 4 * n + 2)
                dve.tensor_tensor(ex[:, 0], hq[:, s], ex[:, 0], ALU.mult).then_inc(qd_done, 1)
                dve.tensor_tensor(ex[:, 1], hk[:, s], ex[:, 1], ALU.mult).then_inc(kd_done, 1)
                dve.wait_ge(ex_done, 4 * n + 4)
                dve.tensor_tensor(ex[:, 3], hk[:, s], ex[:, 3], ALU.mult).then_inc(kr_done, 1)
                if n:
                    dve.wait_ge(oh_full, n)
                dve.tensor_tensor(qb[:], hq[:, s], ex[:, 2], ALU.mult).then_inc(qb_done, 1)

            def head_q(n):
                b = qf_block(n)
                dve.wait_ge(q_sig, n + 1)
                if n >= 2:
                    dve.wait_ge(qb_done, n - 1)
                dve.scalar_tensor_tensor(hq[:, n % 2], bank[bank_of(b, 0)][:], vec[:, V_BHQ + n:V_BHQ + n + 1], sgm[:], ALU.add, ALU.mult).then_inc(bank_free[bank_of(b, 0)], 1)

            def head_mask(n):
                dve.wait_ge(att_full, n + 1)
                dve.copy_predicated(att[:], cmask[:], bank[5][:]).then_inc(att_done, 1)

            def head_f(n):
                b = qf_block(n)
                dve.wait_ge(f_sig, n + 1)
                dve.tensor_scalar(lf[:], lf[:], lbs[:, 1, n:n + 1], lbs[:, 0, n:n + 1], ALU.mult, ALU.add).then_inc(f_lin, 1)
                dve.wait_ge(bank_free[bank_of(b, 1)], used(b) + 1)
                dve.tensor_scalar(hk[:, n % 2], hk[:, n % 2], lbs[:, 1, n:n + 1], None, ALU.mult).then_inc(k_done, 1)

            def head_states(n):
                dve.wait_ge(upd_full, n + 1)
                dve.tensor_copy(st[:, 1, :], bank[6][:, 0:P]).then_inc(st_done, 1)
                for j in range(1, 7):
                    dve.wait_ge(st_done, 7 * n + j)
                    dve.scalar_tensor_tensor(st[:, j + 1, :], st[:, j, :], ex[:, 2, 64 * j + 63:64 * j + 64], bank[6 + j % 2][:, P * (j // 2):P * (j // 2) + P],
                                             ALU.mult, ALU.add).then_inc(st_done, 1)

            def pair_values(n, half):
                b, i = v_block(n), n // 2
                bi = bank_of(b, half)
                dve.wait_ge(bank_full[bi], used(b) + 1)
                if i >= 2:
                    dve.wait_ge(oh_full, n - 2)
                row = bhrow[:, n:n + 2, :].rearrange("p a n -> p (a n)").rearrange("p (a n) -> p a n", a=1)
                dve.tensor_tensor(hv[:, i % 2, 2 * half:2 * half + 2, :], bank[bi][:].rearrange("p (a n) -> p a n", a=2), row.to_broadcast([P, 2, BC]), ALU.add)\
                   .then_inc(bank_free[bi], 1)

            def head_copy(n):
                dve.wait_ge(osq_ready, n + 1)
                dve.tensor_scalar(onum[:], bank[5][:], vec[:, V_HG + n:V_HG + n + 1], None, ALU.mult).then_inc(on_ready, 1)

            dve.wait_ge(lb_ready, 4)
            dve.wait_ge(hg_in, 48)
            dve.memset(att[:], 0.0).then_inc(att_zero, 1)
            dve.memset(st[:, 0, :], 0.0).then_inc(att_zero, 1)
            dve.wait_ge(att_zero, 2)
            for p in periods(3):
                if is_head(p - 3):
                    head_out(p - 3)
                if is_head(p - 2):
                    head_decay(p - 2)
                if is_head(p):
                    head_q(p)
                if is_head(p - 2):
                    head_mask(p - 2)
                if is_head(p):
                    head_f(p)
                if is_head(p - 2):
                    head_states(p - 2)
                if is_head(p) and p % 2 == 0:
                    pair_values(p, 0)
                if is_head(p - 2):
                    head_copy(p - 2)
                if is_head(p) and p % 2 == 0:
                    pair_values(p, 1)

            for k in range(KC):
                dve.wait_ge(y_hi, k + 1)
                dve.tensor_tensor(al[:, k, :], yh[:, k, :], f32(ah[:, k, :]), ALU.subtract).then_inc(y_lo, 1)
            branches(FIRST["gb"], True)
            for k in range(KC):
                dve.wait_ge(m_hi, k + 1)
                dve.tensor_tensor(ul[:, k, :], merged[:, k, :], f32(uh[:, k, :]), ALU.subtract).then_inc(m_lo, 1)
            for j in range(4):
                for half in range(2):
                    add_to_h(FIRST["wout2"] + j, 2 * j + half, None)
            norm_factor("ffn")
            norm("ffn", h, lambda k: vec[:, V_FFN + k:V_FFN + k + 1], None, uh, ul)

            b0 = FIRST["ffn"]
            dve.memset(stat[:, 4, 0:1], 0.0).then_inc(gz_ready, SQ0)

            def hidden(j, n, m0, q=0, per=0):
                for half in range(2):
                    bi, c = bank_of(b0 + j, half), (n + half + 8 * q if per else n + half)
                    dve.wait_ge(gs_ready, c + 1)
                    dve.wait_ge(zv_ready, SQ0 + c - 1)
                    dve.tensor_tensor(gz[:, half], bank[bi][:], gs[:, half], ALU.mult).then_inc(gz_ready, 1)
                    dve.wait_ge(gz_ready, SQ0 + c + 1)
                    dve.tensor_copy(stat[:, 0, 0:1], gz[:, half, 0:1]).then_inc(bank_free[bi], 1)
                for half in range(2):
                    bi, c, m = bank_of(b0 + j + 1, half), (n + half + 8 * q if per else n + half), m0 + half
                    dve.wait_ge(bank_full[bi], used(b0 + j + 1, q, per) + 1)
                    dve.tensor_tensor(gz[:, half], bank[bi][:], gz[:, half], ALU.mult).then_inc(bank_free[bi], 1)
                    dve.wait_ge(bank_free[bi], used(b0 + j + 1, q, per) + 1)
                    dve.tensor_copy(ah[:, m], gz[:, half]).then_inc(z_hi, 1)
                    dve.wait_ge(z_hi, c + 1)
                    dve.tensor_tensor(al[:, m], gz[:, half], f32(ah[:, m]), ALU.subtract).then_inc(z_lo, 1)
                    dve.memset(stat[:, 0, 1:2], 0.0).then_inc(zv_ready, 1)

            dve.memset(stat[:, 4, 1:2], 0.0).then_inc(zv_ready, SQ0)
            with dve.Fori(0, 2) as q:
                for j in range(0, 8, 2):
                    hidden(j, j, j, q, 12)
                for j in range(8, 12):
                    for half in range(2):
                        add_to_h(b0 + j, 2 * (j - 8) + half, None, q, 12)
            for j in range(0, 6, 2):
                hidden(24 + j, 16 + j, j)
            for j in range(6, 10):
                for half in range(2):
                    add_to_h(b0 + 24 + j, 2 * (j - 6) + half, None)
            norm_factor("final")
            dve.wait_ge(rms_full, NORM["final"] + 1)
            for k in range(KC):
                dve.scalar_tensor_tensor(fin[:, k, :], h[:, k, :], vec[:, V_FIN + k:V_FIN + k + 1], norm_banks("final")[1][:], ALU.mult, ALU.mult).then_inc(out_ready, 1)


def blocks(w, kc=KC):
    rows, cols = w.shape
    return np.ascontiguousarray(w.reshape(rows // P, P, cols // BC, BC).transpose(2, 1, 0, 3))


def by_feature(v):
    v = np.asarray(v).reshape(-1, P)
    return np.ascontiguousarray(v.T)


def layout(i):
    f = np.float32
    t = {}
    t["xT"] = i["x"][0].T.reshape(KC, P, S).transpose(1, 0, 2)
    t["ctxT"] = i["ctx"][0].T.reshape(KC, P, L).transpose(1, 0, 2)
    t["c_cols"] = np.stack([i["c"][0].reshape(KC, P).T, i["c_ctx"].reshape(KC, P).T], axis=2)
    t["w_modf"] = blocks(i["w_mod"][0][:, :2048])
    t["w_modr"] = np.concatenate([blocks(i["w_mod"][0][:, 2048:]), blocks(i["w_mod"][1])])
    t["b_mod"] = by_feature(i["b_mod"])
    w = i["w_in_even"][0]
    t["w_in"] = np.concatenate([blocks(w[:, n:n + 512]) for n in (1536, 1024, 512, 0)])
    t["w_out"] = blocks(i["w_out_even"][0])
    t["w4"] = i["w_four"][0].transpose(1, 0, 2)
    for l in range(2):
        t[f"w1_{l}"] = blocks(i["w_mlp1"][l])
        t[f"w2_{l}"] = np.concatenate([blocks(i["w_mlp2"][l][D * q:D * q + D]) for q in range(4)])
    pairs = (np.arange(8)[:, None, None] + 8 * np.arange(2)[None, :, None]) * DH + np.arange(DH)
    pairs = pairs.reshape(-1)
    w, b = i["w_in_2"][0], i["b_in_2"][0]
    aq, akv, hq, hf, hi, hg, ga, gb = (slice(x, y) for x, y in zip((0, 1024, 1280, 2304, 3328, 4352, 5376, 6400), (1024, 1280, 2304, 3328, 4352, 5376, 6400, 7424)))
    t["vecs"] = np.concatenate([by_feature(x) for x in (
        i["norm1_g"], i["norm2_g"], np.tile(i["q_norm_g"][0], 2), np.tile(i["k_norm_g"][0], 2), i["norm_mix_g_2"], i["norm_ffn_g_2"],
        i["norm_final_g_2"], i["pool_scale"], i["hgrn_norm_g_2"], b[aq][pairs], b[1024:1152], b[ga], b[gb], b[hq], b[hf], b[hg],
        i["hgrn_lb_logits_2"])] + [np.broadcast_to(i["attn_sinks_2"][0], (P, 16))], axis=1)
    t["bvrow"] = np.broadcast_to(b[1152:1280], (P, P))
    t["bhrow"] = np.broadcast_to(b[hi].reshape(8, P), (P, 8, P))
    t["w_att2"] = np.concatenate([blocks(w[:, aq][:, pairs]), blocks(w[:, akv])])
    t["w_ga"], t["w_gb"] = blocks(w[:, ga]), blocks(w[:, gb])
    t["w_ba"], t["w_bb"] = blocks(i["w_branch_attn_2"][0][pairs]), blocks(i["w_branch_hgrn_2"][0])
    q_, f_, v_, g_ = (w[:, x].reshape(D, 4, 2, P) for x in (hq, hf, hi, hg))
    t["w_hg"] = blocks(np.stack([q_[:, :, 0], f_[:, :, 0], v_[:, :, 0], v_[:, :, 1], q_[:, :, 1], f_[:, :, 1], g_[:, :, 0], g_[:, :, 1]], axis=2).reshape(D, 4 * D))
    t["w_out2"] = blocks(i["w_out_2"][0])
    gate, up = (i[n][0].reshape(D, 11, 1, BC) for n in ("w_ffn_gate_2", "w_ffn_up_2"))
    t["w_gu"] = blocks(np.concatenate([gate, up], axis=2).reshape(D, 22 * BC))
    down = np.zeros((3 * D, D), f)
    down[:2816] = i["w_ffn_down_2"][0]
    t["w_dn"] = np.concatenate([blocks(down[D * g:D * g + D]) for g in range(3)])
    t["w_pool"] = i["w_pool"][0].reshape(4, 2, P, BC).transpose(0, 2, 1, 3)
    r = np.zeros((ROWS, NH, ROWS, 64), f)
    for q in range(ROWS):
        r[q, :, :, 16:16 + 31] = i["rpb"][0][:, 7 - q:15 - q, :]
    t["rpb"] = r.reshape(ROWS, NH * ROWS, 64)
    con = np.zeros((P, C_END), f)
    con[:, C_ID:C_ID + P] = np.eye(P)
    con[:, C_OND:C_OND + P] = 1 / D
    con[:64, C_ONH:C_ONH + 64] = con[64:, C_ONH + 64:C_ONH + 128] = 1 / DH
    con[:, C_ONE] = 1
    con[:, C_EPS] = EPS
    con[:, C_EPSQ] = EPS * DH
    con[:, C_ONV:C_ONV + P] = 1 / P
    t["consts"] = con
    n = np.arange(S)
    ang = 2 * np.pi * (np.outer(n, n) % S) / S
    t["dftc"] = np.cos(ang).astype(f).reshape(4, P, S).transpose(1, 0, 2)
    t["dfts"] = (-np.sin(ang)).astype(f).reshape(4, P, S).transpose(1, 0, 2)
    n = np.arange(P)
    ang = 2 * np.pi * (np.outer(n, n) % P) / P
    t["cs"] = (np.concatenate([np.cos(ang), np.sin(ang)], axis=1) / 256).astype(f)
    m = np.full((3, QC, WIN), NEG, f)
    for a, w in enumerate((0, 1, 3)):
        for c in range(QC):
            col = QC * w + c
            s = min(max(col - 8, 0), COLS - 16) - W0[w]
            m[a, c, s:s + 16] = 0
    t["mask"] = np.ascontiguousarray(np.broadcast_to(m.transpose(1, 0, 2)[None, :, :, None, :], (ROWS, QC, 3, ROWS, WIN))).reshape(P, 3, 256)
    full = np.zeros((4, S, S))
    for g, win in enumerate((2, 4, 8, 16)):
        for n in range(S):
            lo, hi = max(0, n - win // 2), min(S, n + win - win // 2)
            full[g, lo:hi, n] = 1 / (hi - lo)
            full[g, n, n] -= 1
    band = np.zeros((P, 3, FG, 144), f)
    for kind, tile in enumerate((0, 1, 3)):
        lo, hi = max(0, P * tile - 8), min(S, P * tile + P + 8)
        r = lo - (P * tile - 8)
        band[:, kind, :, r:r + hi - lo] = full[:, P * tile:P * tile + P, lo:hi].transpose(1, 0, 2)
    t["band"] = band
    q, k = np.arange(P)[:, None], np.arange(256)[None, :]
    t["wmask"] = np.stack([np.where(k <= q, 0, 8 * NEG), np.where((k > q) & (k <= q + P), 0, 8 * NEG)], axis=1).astype(f)
    a, b = np.arange(P)[:, None], np.arange(P)[None, :]
    same = a // 64 == b // 64
    upto = same & (a <= b)
    t["cm"] = np.stack([upto.astype(f) - (same & (a % 64 <= 31)), upto, same & (a > b)], axis=1).astype(f)
    t["cmask"] = np.tile(upto, (1, 4)).astype(np.uint32)
    return {k: np.ascontiguousarray(v) for k, v in t.items()}


def kernel(**inputs):
    import concourse.bacc as _bacc
    from concourse.bass_utils import run_bass_kernel_spmd as _run

    nc = _bacc.Bacc("TRN2", target_bir_lowering=False, num_devices=1)
    arrays = layout({k: np.asarray(v) for k, v in inputs.items()})
    t = {k: nc.dram_tensor(f"in_{k}", a.shape, mybir.dt.from_np(a.dtype), kind="ExternalInput").ap() for k, a in arrays.items()}
    t["out"] = nc.dram_tensor("out_0_dram", (P, KC, S), F32, kind="ExternalOutput").ap()
    build_program(nc, t)
    r = _run(nc, [{f"in_{k}": a for k, a in arrays.items()}], core_ids=[0])
    got = r.results[0]["out_0_dram"]
    return got.transpose(1, 0, 2).reshape(D, S).T.reshape(1, S, D)
```
